# Optimizing a Trainium2 kernel written in Bass

```python
import math
import jax, jax.numpy as jnp
from jax import lax
import numpy as np

D_MODEL = 1024
BATCH = 1
SEQ = 256
DEPTH = 1

RMS_EPS = 1e-6
NEG_INF = -1e30

S5_WIDTH = D_MODEL // 2
S5_GROUP = 16
S5_GROUPS = S5_WIDTH // S5_GROUP
S5_STATE = 64

N_Q_HEADS = 16
N_KV_HEADS = 4
HEAD_DIM = 64
Q_PER_KV = N_Q_HEADS // N_KV_HEADS
WINDOW = 128
ATTN_BLOCK = 128
N_BUCKETS = 32
MAX_DISTANCE = 128

PEER_HEADS = 8
PEER_KEY_DIM = 128
N_SUB_KEYS = 128
N_EXPERTS = N_SUB_KEYS * N_SUB_KEYS
PEER_TOPK = 16
PEER_TOKEN_BLOCK = 128

Q_WIDTH = N_Q_HEADS * HEAD_DIM
KV_WIDTH = N_KV_HEADS * HEAD_DIM
GATE_WIDTH = 2 * D_MODEL
IN_WIDTH = S5_WIDTH + Q_WIDTH + 2 * KV_WIDTH + GATE_WIDTH


def rms_norm(x, g):
    xf = x.astype(jnp.float32)
    r = lax.rsqrt(jnp.mean(xf * xf, axis=-1, keepdims=True) + RMS_EPS)
    return (xf * r).astype(x.dtype) * g

def _complex_scan_combine(c1, c2):
    a1r, a1i, b1r, b1i = c1
    a2r, a2i, b2r, b2i = c2
    ar = a2r * a1r - a2i * a1i
    ai = a2r * a1i + a2i * a1r
    br = a2r * b1r - a2i * b1i + b2r
    bi = a2r * b1i + a2i * b1r + b2i
    return (ar, ai, br, bi)

def s5_mixer(u, lam_re, lam_im, log_step, b_re, b_im, c_re, c_im, d_skip, w_glu):
    bsz, seq, _ = u.shape
    f32 = jnp.float32
    uf = u.astype(f32).reshape(bsz, seq, S5_GROUPS, S5_GROUP)
    lr, li = lam_re.astype(f32), lam_im.astype(f32)
    step = jnp.exp(log_step.astype(f32))[:, None]
    mag = jnp.exp(lr * step)
    abar_re = mag * jnp.cos(li * step)
    abar_im = mag * jnp.sin(li * step)
    den = lr * lr + li * li
    nr, ni = abar_re - 1.0, abar_im
    coef_re = ((nr * lr + ni * li) / den)[..., None]
    coef_im = ((ni * lr - nr * li) / den)[..., None]
    br, bi = b_re.astype(f32), b_im.astype(f32)
    bbar_re = coef_re * br - coef_im * bi
    bbar_im = coef_re * bi + coef_im * br
    bu_re = jnp.einsum('blgc,gpc->blgp', uf, bbar_re)
    bu_im = jnp.einsum('blgc,gpc->blgp', uf, bbar_im)
    a_re = jnp.broadcast_to(abar_re, bu_re.shape)
    a_im = jnp.broadcast_to(abar_im, bu_im.shape)
    _, _, h_re, h_im = lax.associative_scan(
        _complex_scan_combine, (a_re, a_im, bu_re, bu_im), axis=1)
    y = (jnp.einsum('blgp,gcp->blgc', h_re, c_re.astype(f32))
         - jnp.einsum('blgp,gcp->blgc', h_im, c_im.astype(f32))
         + d_skip.astype(f32) * uf)
    y = jax.nn.gelu(y.reshape(bsz, seq, S5_WIDTH), approximate=False).astype(u.dtype)
    ab = y @ w_glu
    a, b = jnp.split(ab, 2, axis=-1)
    return a * jax.nn.sigmoid(b)

def t5_bucket(dist):
    max_exact = N_BUCKETS // 2
    d_f = jnp.maximum(dist, 1).astype(jnp.float32)
    large = max_exact + (jnp.log(d_f / max_exact) / math.log(MAX_DISTANCE / max_exact)
                         * (N_BUCKETS - max_exact)).astype(jnp.int32)
    large = jnp.minimum(large, N_BUCKETS - 1)
    return jnp.where(dist < max_exact, dist, large)

def sliding_window_attention(q, k, v, q_norm_g, k_norm_g, rel_bias_table, sinks):
    bsz, seq, _ = q.shape
    nb = seq // ATTN_BLOCK
    q = rms_norm(q.reshape(bsz, seq, N_KV_HEADS, Q_PER_KV, HEAD_DIM), q_norm_g)
    k = rms_norm(k.reshape(bsz, seq, N_KV_HEADS, HEAD_DIM), k_norm_g)
    v = v.reshape(bsz, seq, N_KV_HEADS, HEAD_DIM)
    qb = q.reshape(bsz, nb, ATTN_BLOCK, N_KV_HEADS, Q_PER_KV, HEAD_DIM)

    def band(t):
        pad = jnp.pad(t, ((0, 0), (ATTN_BLOCK, 0), (0, 0), (0, 0)))
        prev = pad[:, :seq].reshape(bsz, nb, ATTN_BLOCK, N_KV_HEADS, HEAD_DIM)
        cur = t.reshape(bsz, nb, ATTN_BLOCK, N_KV_HEADS, HEAD_DIM)
        return jnp.concatenate([prev, cur], axis=2)

    kb, vb = band(k), band(v)
    scale = HEAD_DIM ** -0.5
    scores = jnp.einsum('bnqkgd,bnskd->bnkgqs', qb, kb).astype(jnp.float32) * scale

    qi = jnp.arange(ATTN_BLOCK)[:, None]
    si = jnp.arange(2 * ATTN_BLOCK)[None, :]
    dist = ATTN_BLOCK + qi - si
    band_ok = (dist >= 0) & (dist < WINDOW)
    bias = rel_bias_table.astype(jnp.float32)[t5_bucket(jnp.maximum(dist, 0))]
    bias = bias.transpose(2, 0, 1).reshape(N_KV_HEADS, Q_PER_KV, ATTN_BLOCK, 2 * ATTN_BLOCK)
    blk = jnp.arange(nb)[:, None, None]
    key_ok = (blk - 1) * ATTN_BLOCK + si[None] >= 0
    valid = (band_ok[None] & key_ok)[None, :, None, None]

    scores = jnp.where(valid, scores + bias, NEG_INF)
    sink = sinks.astype(jnp.float32).reshape(1, 1, N_KV_HEADS, Q_PER_KV, 1, 1)
    m = jnp.maximum(jnp.max(scores, axis=-1, keepdims=True), sink)
    p = jnp.exp(scores - m)
    p = p / (jnp.sum(p, axis=-1, keepdims=True) + jnp.exp(sink - m))
    out = jnp.einsum('bnkgqs,bnskd->bnqkgd', p.astype(vb.dtype), vb)
    return out.reshape(bsz, seq, Q_WIDTH)

def peer_mixer(xn, w_query, sub_keys, u_tab, v_tab):
    bsz, seq, d = xn.shape
    t = bsz * seq
    xt = xn.reshape(t, d)
    q = (xt @ w_query).reshape(t, PEER_HEADS, 2, PEER_KEY_DIM // 2)
    s = jnp.einsum('thkd,hknd->thkn', q, sub_keys).astype(jnp.float32)
    vals, idx = lax.top_k(s, PEER_TOPK)
    cand = (vals[:, :, 0, :, None] + vals[:, :, 1, None, :]).reshape(t, PEER_HEADS, PEER_TOPK * PEER_TOPK)
    best, pos = lax.top_k(cand, PEER_TOPK)
    i1 = jnp.take_along_axis(idx[:, :, 0], pos // PEER_TOPK, axis=-1)
    i2 = jnp.take_along_axis(idx[:, :, 1], pos % PEER_TOPK, axis=-1)
    expert = (i1 * N_SUB_KEYS + i2).reshape(t, PEER_HEADS * PEER_TOPK)
    gate = jax.nn.softmax(best, axis=-1).reshape(t, PEER_HEADS * PEER_TOPK)

    def block_fn(args):
        xb, eb, gb = args
        a = jnp.einsum('cd,ced->ce', xb, u_tab[eb]).astype(jnp.float32)
        w = (gb * jax.nn.gelu(a, approximate=False)).astype(xb.dtype)
        return jnp.einsum('ce,ced->cd', w, v_tab[eb])

    nblk = t // PEER_TOKEN_BLOCK
    out = lax.map(block_fn, (xt.reshape(nblk, PEER_TOKEN_BLOCK, d),
                             expert.reshape(nblk, PEER_TOKEN_BLOCK, -1),
                             gate.reshape(nblk, PEER_TOKEN_BLOCK, -1)))
    return out.reshape(bsz, seq, d)

def first_inputs(seed: int = 0) -> dict:
    key = jax.random.key(seed)
    ks = jax.random.split(key, 26)
    f32 = jnp.float32
    L, D, G, P, C = DEPTH, D_MODEL, S5_GROUPS, S5_STATE, S5_GROUP
    nrm = lambda k, shape, s: jax.random.normal(k, shape, f32) * s
    inp = {}
    inp['x'] = nrm(ks[0], (BATCH, SEQ, D), 1.0)
    inp['ln1_g'] = 1.0 + nrm(ks[1], (L, D), 0.02)
    inp['w_in'] = nrm(ks[2], (L, D, IN_WIDTH), D ** -0.5)
    inp['b_gate'] = nrm(ks[3], (L, GATE_WIDTH), 0.02)
    inp['s5_lambda_re'] = -0.5 + nrm(ks[4], (L, G, P), 0.01)
    inp['s5_lambda_im'] = jnp.pi * jnp.arange(P, dtype=f32) + nrm(ks[5], (L, G, P), 0.01)
    inp['s5_log_step'] = jax.random.uniform(ks[6], (L, G), f32, math.log(1e-3), math.log(1e-1))
    inp['s5_b_re'] = nrm(ks[7], (L, G, P, C), (2 * C) ** -0.5)
    inp['s5_b_im'] = nrm(ks[8], (L, G, P, C), (2 * C) ** -0.5)
    inp['s5_c_re'] = nrm(ks[9], (L, G, C, P), P ** -0.5)
    inp['s5_c_im'] = nrm(ks[10], (L, G, C, P), P ** -0.5)
    inp['s5_d'] = nrm(ks[11], (L, G, C), 1.0)
    inp['s5_w_glu'] = nrm(ks[12], (L, S5_WIDTH, 2 * S5_WIDTH), S5_WIDTH ** -0.5)
    inp['w_s5_branch'] = nrm(ks[13], (L, S5_WIDTH, D), S5_WIDTH ** -0.5)
    inp['q_norm_g'] = 1.0 + nrm(ks[14], (L, HEAD_DIM), 0.02)
    inp['k_norm_g'] = 1.0 + nrm(ks[15], (L, HEAD_DIM), 0.02)
    inp['rel_bias_table'] = nrm(ks[16], (N_BUCKETS, N_Q_HEADS), 0.1)
    inp['attn_sinks'] = nrm(ks[17], (L, N_Q_HEADS), 0.5)
    inp['w_attn_branch'] = nrm(ks[18], (L, Q_WIDTH, D), Q_WIDTH ** -0.5)
    inp['w_out'] = nrm(ks[19], (L, D, D), D ** -0.5)
    inp['ln2_g'] = 1.0 + nrm(ks[20], (L, D), 0.02)
    inp['peer_w_query'] = nrm(ks[21], (L, D, PEER_HEADS * PEER_KEY_DIM), D ** -0.5)
    inp['peer_sub_keys'] = nrm(ks[22], (L, PEER_HEADS, 2, N_SUB_KEYS, PEER_KEY_DIM // 2), (PEER_KEY_DIM // 2) ** -0.5)
    inp['peer_u'] = nrm(ks[23], (L, N_EXPERTS, D), D ** -0.5)
    inp['peer_v'] = nrm(ks[24], (L, N_EXPERTS, D), D ** -0.5)
    return inp

def first_block(x, ln1_g, w_in, b_gate, s5_lambda_re, s5_lambda_im, s5_log_step,
              s5_b_re, s5_b_im, s5_c_re, s5_c_im, s5_d, s5_w_glu, w_s5_branch,
              q_norm_g, k_norm_g, rel_bias_table, attn_sinks, w_attn_branch, w_out,
              ln2_g, peer_w_query, peer_sub_keys, peer_u, peer_v):
    splits = [S5_WIDTH, S5_WIDTH + Q_WIDTH, S5_WIDTH + Q_WIDTH + KV_WIDTH,
              S5_WIDTH + Q_WIDTH + 2 * KV_WIDTH]
    h = x
    for layer in range(DEPTH):
        xn = rms_norm(h, ln1_g[layer])
        proj = xn @ w_in[layer]
        u_s5, q, k, v, gate_logits = jnp.split(proj, splits, axis=-1)
        gates = jax.nn.sigmoid(gate_logits + b_gate[layer])
        g_s5, g_attn = jnp.split(gates, 2, axis=-1)
        y_s5 = s5_mixer(u_s5, s5_lambda_re[layer], s5_lambda_im[layer], s5_log_step[layer],
                        s5_b_re[layer], s5_b_im[layer], s5_c_re[layer], s5_c_im[layer],
                        s5_d[layer], s5_w_glu[layer]) @ w_s5_branch[layer]
        y_attn = sliding_window_attention(q, k, v, q_norm_g[layer], k_norm_g[layer],
                                          rel_bias_table, attn_sinks[layer]) @ w_attn_branch[layer]
        h = h + (g_s5 * y_s5 + g_attn * y_attn) @ w_out[layer]
        xn2 = rms_norm(h, ln2_g[layer])
        h = h + peer_mixer(xn2, peer_w_query[layer], peer_sub_keys[layer],
                           peer_u[layer], peer_v[layer])
    return h


DEPTH_2 = 2

NSA_HEADS = 8
NSA_KV_GROUPS = 2
NSA_HEAD_DIM = 64
NSA_BRANCHES = 3
CMP_BLOCK = 32
CMP_STRIDE = 16
CMP_HIDDEN = 256
SEL_BLOCK = 64
N_SELECT = 16
N_LOCAL = 2
WINDOW_2 = 512
NSA_Q_CHUNK = 64

MLA_HEADS = 8
MLA_NOPE_DIM = 64
MLA_ROPE_DIM = 32
MLA_V_DIM = 64
Q_LORA_RANK = 256
KV_LORA_RANK = 128

D_FF = 4 * D_MODEL
ROPE_THETA = 10000.0
NORM_EPS = 1e-6
NEG_INF_2 = -1e30
FORCE_BONUS = 1e4

NSA_WIDTH = NSA_HEADS * NSA_HEAD_DIM
NSA_KV_WIDTH = NSA_KV_GROUPS * NSA_HEAD_DIM
MLA_WIDTH = MLA_HEADS * MLA_V_DIM
MIX_WIDTH = NSA_WIDTH + MLA_WIDTH
IN_SIZES = (NSA_WIDTH, NSA_KV_WIDTH, NSA_KV_WIDTH, NSA_KV_WIDTH, NSA_KV_WIDTH,
            NSA_KV_WIDTH, NSA_KV_WIDTH, NSA_BRANCHES * NSA_HEADS,
            Q_LORA_RANK, KV_LORA_RANK, MLA_ROPE_DIM)
IN_WIDTH_2 = sum(IN_SIZES)


def _rms_norm(x, gain):
    xf = x.astype(jnp.float32)
    y = xf * lax.rsqrt(jnp.mean(xf * xf, axis=-1, keepdims=True) + NORM_EPS)
    return (y * gain.astype(jnp.float32)).astype(x.dtype)

def _rope_tables(seq, dim, dtype):
    inv_freq = 1.0 / (ROPE_THETA ** (jnp.arange(0, dim, 2, dtype=jnp.float32) / dim))
    ang = jnp.arange(seq, dtype=jnp.float32)[:, None] * inv_freq[None, :]
    ang = jnp.concatenate([ang, ang], axis=-1)
    return jnp.cos(ang).astype(dtype), jnp.sin(ang).astype(dtype)

def _rope(x, cos, sin):
    half = x.shape[-1] // 2
    rot = jnp.concatenate([-x[..., half:], x[..., :half]], axis=-1)
    return x * cos[:, None, :] + rot * sin[:, None, :]

def _masked_softmax(s, mask):
    s = jnp.where(mask, s, NEG_INF_2)
    m = jnp.max(s, axis=-1, keepdims=True)
    e = jnp.where(mask, jnp.exp(s - m), 0.0)
    return e / jnp.maximum(jnp.sum(e, axis=-1, keepdims=True), 1e-30)

def _heads(t, n):
    b, s, w = t.shape
    return t.reshape(b, s, n, w // n)

def _compress(kv, pos_emb, w1, w2):
    B, S, G, dk = kv.shape
    ratio = CMP_BLOCK // CMP_STRIDE
    n_cmp = S // CMP_STRIDE - ratio + 1
    chunks = kv.reshape(B, S // CMP_STRIDE, CMP_STRIDE, G, dk)
    blocks = jnp.concatenate([chunks[:, i:i + n_cmp] for i in range(ratio)], axis=2)
    blocks = blocks + pos_emb[None, None, :, None, :]
    flat = jnp.swapaxes(blocks, 2, 3).reshape(B, n_cmp, G, CMP_BLOCK * dk)
    return jax.nn.silu(flat @ w1) @ w2

def _nsa(q, k_cmp, v_cmp, k_sel, v_sel, k_win, v_win, gates):
    B, S, H, dk = q.shape
    G = k_sel.shape[2]
    R = H // G
    n_cmp = k_cmp.shape[1]
    n_blk = S // SEL_BLOCK
    n_sel = min(N_SELECT, n_blk)
    QC = NSA_Q_CHUNK
    scale = dk ** -0.5
    qg = q.reshape(B, S, G, R, dk)
    gg = gates.reshape(B, S, G, R, NSA_BRANCHES)
    k_blocks = k_sel.reshape(B, n_blk, SEL_BLOCK, G, dk).transpose(0, 3, 1, 2, 4)
    v_blocks = v_sel.reshape(B, n_blk, SEL_BLOCK, G, dk).transpose(0, 3, 1, 2, 4)
    pad = ((0, 0), (WINDOW_2, 0), (0, 0), (0, 0))
    k_win_pad = jnp.pad(k_win, pad)
    v_win_pad = jnp.pad(v_win, pad)
    cmp_end = jnp.arange(n_cmp) * CMP_STRIDE + CMP_BLOCK - 1
    blk_ids = jnp.arange(n_blk)
    a = SEL_BLOCK // CMP_STRIDE
    b = CMP_BLOCK // CMP_STRIDE
    overlap = np.convolve(np.ones(a), np.ones(b))
    bi = jnp.arange(B)[:, None, None, None]
    gi = jnp.arange(G)[None, :, None, None]

    def chunk(c):
        s0 = c * QC
        t = s0 + jnp.arange(QC)
        qc = lax.dynamic_slice_in_dim(qg, s0, QC, axis=1)
        gc = lax.dynamic_slice_in_dim(gg, s0, QC, axis=1)
        s_cmp = jnp.einsum('bqgrd,bngd->bgrqn', qc, k_cmp, preferred_element_type=jnp.float32) * scale
        p_cmp = _masked_softmax(s_cmp, cmp_end[None, :] <= t[:, None])
        o_cmp = jnp.einsum('bgrqn,bngd->bqgrd', p_cmp.astype(v_cmp.dtype), v_cmp)
        imp = jnp.pad(p_cmp.sum(axis=2), ((0, 0), (0, 0), (0, 0), (b - 1, b - 1)))
        imp_blk = sum(float(overlap[j]) * imp[..., j:j + a * (n_blk - 1) + 1:a] for j in range(a + b - 1))
        cur = t // SEL_BLOCK
        valid = blk_ids[None, :] <= cur[:, None]
        forced = valid & ((blk_ids[None, :] == 0) | (blk_ids[None, :] > cur[:, None] - N_LOCAL))
        score = jnp.where(forced, FORCE_BONUS, jnp.where(valid, imp_blk, -1.0))
        _, idx = lax.top_k(score, n_sel)
        k_g = k_blocks[bi, gi, idx]
        v_g = v_blocks[bi, gi, idx]
        key_pos = idx[..., None] * SEL_BLOCK + jnp.arange(SEL_BLOCK)
        m_sel = (key_pos <= t[:, None, None]).reshape(B, G, 1, QC, n_sel * SEL_BLOCK)
        s_sel = jnp.einsum('bqgrd,bgqnkd->bgrqnk', qc, k_g, preferred_element_type=jnp.float32) * scale
        p_sel = _masked_softmax(s_sel.reshape(B, G, R, QC, n_sel * SEL_BLOCK), m_sel)
        o_sel = jnp.einsum('bgrqj,bgqjd->bqgrd', p_sel.astype(v_g.dtype),
                           v_g.reshape(B, G, QC, n_sel * SEL_BLOCK, dk))
        kw = lax.dynamic_slice_in_dim(k_win_pad, s0, WINDOW_2 + QC, axis=1)
        vw = lax.dynamic_slice_in_dim(v_win_pad, s0, WINDOW_2 + QC, axis=1)
        win_pos = s0 - WINDOW_2 + jnp.arange(WINDOW_2 + QC)
        m_win = ((win_pos[None, :] <= t[:, None]) & (win_pos[None, :] > t[:, None] - WINDOW_2)
                 & (win_pos[None, :] >= 0))
        s_win = jnp.einsum('bqgrd,bkgd->bgrqk', qc, kw, preferred_element_type=jnp.float32) * scale
        p_win = _masked_softmax(s_win, m_win)
        o_win = jnp.einsum('bgrqk,bkgd->bqgrd', p_win.astype(vw.dtype), vw)
        return gc[..., 0:1] * o_cmp + gc[..., 1:2] * o_sel + gc[..., 2:3] * o_win

    out = lax.map(chunk, jnp.arange(S // QC))
    return jnp.swapaxes(out, 0, 1).reshape(B, S, H * dk)

def _causal_attention(q, k, v):
    B, S, H, dk = q.shape
    dv = v.shape[-1]
    scale = dk ** -0.5
    kpos = jnp.arange(S)

    def block(c):
        s0 = c * ATTN_BLOCK
        qb = lax.dynamic_slice_in_dim(q, s0, ATTN_BLOCK, axis=1)
        s = jnp.einsum('bqhd,bkhd->bhqk', qb, k, preferred_element_type=jnp.float32) * scale
        mask = kpos[None, :] <= (s0 + jnp.arange(ATTN_BLOCK))[:, None]
        p = _masked_softmax(s, mask)
        return jnp.einsum('bhqk,bkhd->bqhd', p.astype(v.dtype), v)

    out = lax.map(block, jnp.arange(S // ATTN_BLOCK))
    return jnp.swapaxes(out, 0, 1).reshape(B, S, H, dv)

def _mla(c_q, c_kv, k_rope, q_norm, w_q_up, kv_norm, w_kv_up, cos, sin):
    B, S, _ = c_q.shape
    q = (_rms_norm(c_q, q_norm) @ w_q_up).reshape(B, S, MLA_HEADS, MLA_NOPE_DIM + MLA_ROPE_DIM)
    q = jnp.concatenate([q[..., :MLA_NOPE_DIM], _rope(q[..., MLA_NOPE_DIM:], cos, sin)], axis=-1)
    kv = (_rms_norm(c_kv, kv_norm) @ w_kv_up).reshape(B, S, MLA_HEADS, MLA_NOPE_DIM + MLA_V_DIM)
    k_nope, v = kv[..., :MLA_NOPE_DIM], kv[..., MLA_NOPE_DIM:]
    k_pe = _rope(k_rope[:, :, None, :], cos, sin)
    k = jnp.concatenate([k_nope, jnp.broadcast_to(k_pe, (B, S, MLA_HEADS, MLA_ROPE_DIM))], axis=-1)
    return _causal_attention(q, k, v).reshape(B, S, MLA_WIDTH)

def second_inputs(seed: int = 0) -> dict:
    key = jax.random.key(seed)
    ks = jax.random.split(key, 20)
    L = DEPTH_2
    dk = NSA_HEAD_DIM

    def dense(k, shape, fan_in):
        return jax.random.normal(k, shape, jnp.float32) * fan_in ** -0.5

    def gain(k, shape):
        return 1.0 + 0.02 * jax.random.normal(k, shape, jnp.float32)

    return {
        "x": jax.random.normal(ks[0], (BATCH, SEQ, D_MODEL), jnp.float32),
        "attn_norm": gain(ks[1], (L, D_MODEL)),
        "w_in": dense(ks[2], (L, D_MODEL, IN_WIDTH_2), D_MODEL),
        "cmp_pos_k": 0.1 * jax.random.normal(ks[3], (L, CMP_BLOCK, dk), jnp.float32),
        "cmp_w1_k": dense(ks[4], (L, CMP_BLOCK * dk, CMP_HIDDEN), CMP_BLOCK * dk),
        "cmp_w2_k": dense(ks[5], (L, CMP_HIDDEN, dk), CMP_HIDDEN),
        "cmp_pos_v": 0.1 * jax.random.normal(ks[6], (L, CMP_BLOCK, dk), jnp.float32),
        "cmp_w1_v": dense(ks[7], (L, CMP_BLOCK * dk, CMP_HIDDEN), CMP_BLOCK * dk),
        "cmp_w2_v": dense(ks[8], (L, CMP_HIDDEN, dk), CMP_HIDDEN),
        "mla_q_norm": gain(ks[9], (L, Q_LORA_RANK)),
        "w_q_up": dense(ks[10], (L, Q_LORA_RANK, MLA_HEADS * (MLA_NOPE_DIM + MLA_ROPE_DIM)), Q_LORA_RANK),
        "mla_kv_norm": gain(ks[11], (L, KV_LORA_RANK)),
        "w_kv_up": dense(ks[12], (L, KV_LORA_RANK, MLA_HEADS * (MLA_NOPE_DIM + MLA_V_DIM)), KV_LORA_RANK),
        "nsa_out_norm": gain(ks[13], (L, NSA_WIDTH)),
        "mla_out_norm": gain(ks[14], (L, MLA_WIDTH)),
        "w_out": dense(ks[15], (L, MIX_WIDTH, D_MODEL), MIX_WIDTH),
        "mlp_norm": gain(ks[16], (L, D_MODEL)),
        "w_ff1": dense(ks[17], (L, D_MODEL, D_FF), D_MODEL),
        "w_ff2": dense(ks[18], (L, D_FF, D_MODEL), D_FF),
        "final_norm": gain(ks[19], (D_MODEL,)),
    }

def second_block(x, attn_norm, w_in, cmp_pos_k, cmp_w1_k, cmp_w2_k, cmp_pos_v, cmp_w1_v, cmp_w2_v,
              mla_q_norm, w_q_up, mla_kv_norm, w_kv_up, nsa_out_norm, mla_out_norm, w_out,
              mlp_norm, w_ff1, w_ff2, final_norm):
    B, S, _ = x.shape
    cos_a, sin_a = _rope_tables(S, NSA_HEAD_DIM, x.dtype)
    cos_b, sin_b = _rope_tables(S, MLA_ROPE_DIM, x.dtype)
    offsets = [int(o) for o in np.cumsum(IN_SIZES)[:-1]]
    G = NSA_KV_GROUPS
    for l in range(DEPTH_2):
        h = _rms_norm(x, attn_norm[l])
        proj = h @ w_in[l]
        (q_a, k_c, v_c, k_s, v_s, k_w, v_w, g_a, c_q, c_kv, k_r) = jnp.split(proj, offsets, axis=-1)
        q_a = _rope(_heads(q_a, NSA_HEADS), cos_a, sin_a)
        k_cmp = _compress(_rope(_heads(k_c, G), cos_a, sin_a), cmp_pos_k[l], cmp_w1_k[l], cmp_w2_k[l])
        v_cmp = _compress(_heads(v_c, G), cmp_pos_v[l], cmp_w1_v[l], cmp_w2_v[l])
        gates = jax.nn.sigmoid(g_a).reshape(B, S, NSA_HEADS, NSA_BRANCHES)
        o_a = _nsa(q_a, k_cmp, v_cmp,
                   _rope(_heads(k_s, G), cos_a, sin_a), _heads(v_s, G),
                   _rope(_heads(k_w, G), cos_a, sin_a), _heads(v_w, G), gates)
        o_b = _mla(c_q, c_kv, k_r, mla_q_norm[l], w_q_up[l], mla_kv_norm[l], w_kv_up[l], cos_b, sin_b)
        mixed = jnp.concatenate([_rms_norm(o_a, nsa_out_norm[l]), _rms_norm(o_b, mla_out_norm[l])], axis=-1)
        x = x + mixed @ w_out[l]
        h = _rms_norm(x, mlp_norm[l])
        x = x + jnp.square(jax.nn.relu(h @ w_ff1[l])) @ w_ff2[l]
    return _rms_norm(x, final_norm)


def setup_inputs(seed=0):
    out = dict(first_inputs(seed))
    for name, value in second_inputs(seed + 1).items():
        if name != "x":
            out[name + "_2"] = value
    return out


def reference(
    x, ln1_g, w_in, b_gate, s5_lambda_re, s5_lambda_im, s5_log_step, s5_b_re, s5_b_im, s5_c_re,
    s5_c_im, s5_d, s5_w_glu, w_s5_branch, q_norm_g, k_norm_g, rel_bias_table, attn_sinks,
    w_attn_branch, w_out, ln2_g, peer_w_query, peer_sub_keys, peer_u, peer_v, attn_norm_2,
    w_in_2, cmp_pos_k_2, cmp_w1_k_2, cmp_w2_k_2, cmp_pos_v_2, cmp_w1_v_2, cmp_w2_v_2,
    mla_q_norm_2, w_q_up_2, mla_kv_norm_2, w_kv_up_2, nsa_out_norm_2, mla_out_norm_2, w_out_2,
    mlp_norm_2, w_ff1_2, w_ff2_2, final_norm_2,
):
    x = first_block(
        x, ln1_g, w_in, b_gate, s5_lambda_re, s5_lambda_im, s5_log_step, s5_b_re, s5_b_im,
        s5_c_re, s5_c_im, s5_d, s5_w_glu, w_s5_branch, q_norm_g, k_norm_g, rel_bias_table,
        attn_sinks, w_attn_branch, w_out, ln2_g, peer_w_query, peer_sub_keys, peer_u, peer_v,
    )
    return second_block(
        x, attn_norm_2, w_in_2, cmp_pos_k_2, cmp_w1_k_2, cmp_w2_k_2, cmp_pos_v_2, cmp_w1_v_2,
        cmp_w2_v_2, mla_q_norm_2, w_q_up_2, mla_kv_norm_2, w_kv_up_2, nsa_out_norm_2,
        mla_out_norm_2, w_out_2, mlp_norm_2, w_ff1_2, w_ff2_2, final_norm_2,
    )


_drawn_inputs = setup_inputs


def setup_inputs(seed=0):
    import zlib

    import numpy as np

    out = dict(_drawn_inputs(seed))
    spreads = {}
    factors = {'ln1_g': 5.991,
     'b_gate': 8.0,
     's5_lambda_re': 64.0,
     's5_lambda_im': 3.126,
     's5_log_step': 3.26,
     's5_b_re': 4.4,
     's5_b_im': 4.4,
     's5_c_re': 4.396,
     's5_c_im': 4.386,
     'q_norm_g': 8.0,
     'k_norm_g': 8.0,
     'rel_bias_table': 4.192,
     'attn_sinks': 3.594,
     'ln2_g': 8.0,
     'peer_w_query': 3.226,
     'peer_sub_keys': 3.242,
     'peer_u': 3.562,
     'peer_v': 3.293,
     'cmp_pos_k_2': 7.139,
     'mla_q_norm_2': 7.682,
     'mla_kv_norm_2': 3.202,
     'nsa_out_norm_2': 17.093,
     'mla_out_norm_2': 16.419,
     'mlp_norm_2': 2.875}
    for name, (base, spread) in spreads.items():
        noise = np.random.default_rng([zlib.crc32(name.encode()), seed]).standard_normal(out[name].shape)
        drawn = base * np.exp(spread * noise) if base else spread * noise
        out[name] = __import__('jax').numpy.asarray(drawn.astype(out[name].dtype))
    for name, factor in factors.items():
        out[name] = (out[name] * factor).astype(out[name].dtype)
    return out
```

```python
import numpy as np
import concourse.bass as bass
from concourse import mybir
from contextlib import ExitStack

F32 = mybir.dt.float32
U32 = mybir.dt.uint32
ALU = mybir.AluOpType
ACT = mybir.ActivationFunctionType
AX = mybir.AxisListType

P = 128
T = 256
TT = T // P
D = 1024
DC = D // P
EPS = 1e-6
NEG = -1e30

SLOTS = 4
SLOT = 2048

G1 = 32
SC = 16
UC = 4

NH, NKV, HD = 16, 4, 64

PH, TOPK, NSUB = 8, 16, 128
NE2 = NSUB

LAYERS = 2
NCMP = 15
FF = 4096
FC = FF // P
IN2_UNITS, UP_UNITS, CMP_UNITS, OUT_UNITS, FF1_UNITS, FF2_UNITS = 7, 2, 4, 4, 16, 16
LAYER_UNITS = IN2_UNITS + UP_UNITS + CMP_UNITS + OUT_UNITS + FF1_UNITS + FF2_UNITS

CONST = {}
_at = 0
for _name, _n in [("ones", 128), ("blk64", 128), ("ident", 128), ("rot64", 128), ("rot32", 128),
                  ("cosA", 256), ("sinA", 256), ("cosB", 256), ("sinB", 256),
                  ("mask1", 256), ("cmp_add", 32), ("cmp_mul", 32), ("time", 256), ("lane", 128)]:
    CONST[_name] = (_at, _at + _n)
    _at += _n
NCONST = _at

PAR1 = {}
_at = 0
for _name, _n in [("ln1", 8), ("ln2", 8), ("bgate", 16), ("lre", SC), ("lim", SC), ("lstep", SC),
                  ("dskip", UC), ("gq", 1), ("gk", 1), ("sinks", NH), ("final", 8), ("cs5", SC * 2 * 16)]:
    PAR1[_name] = (_at, _at + _n)
    _at += _n
NPAR1 = _at

PAR2 = {}
_at = 0
for _name, _n in [("attn", 8), ("mlp", 8), ("qn", 2), ("kvn", 1), ("nsa", 4), ("mla", 4), ("posk", 16),
                  ("posv", 16), ("w2k", 128), ("w2v", 128), ("wg", DC * 24)]:
    PAR2[_name] = (_at, _at + _n)
    _at += _n
NPAR2 = _at


class Banks:

    def __init__(self, full, drained, tensors):
        self.full, self.drained, self.tensors = full, drained, tensors
        self.reset()

    def reset(self):
        self.turn, self.done, self.jobs = 0, [0] * 8, {}

    def plan(self, names):
        for n in names:
            b = self.turn % 8
            self.turn += 1
            self.jobs[n] = (b, self.done[b])
            self.done[b] += 1

    def open(self, pe, name):
        b, before = self.jobs[name]
        if before:
            pe.wait_ge(self.drained[b], before)
        return self.tensors[b]

    def close(self, ins, name):
        ins.then_inc(self.full[self.jobs[name][0]], 1)

    def take(self, eng, name):
        b, before = self.jobs[name]
        eng.wait_ge(self.full[b], before + 1)
        return self.tensors[b]

    def give(self, ins, name):
        ins.then_inc(self.drained[self.jobs[name][0]], 1)

    def wait_drained(self, eng, name):
        b, before = self.jobs[name]
        eng.wait_ge(self.drained[b], before + 1)


class Ring:

    def __init__(self, loaded, used, slots):
        self.loaded, self.used, self.slots = loaded, used, slots
        self.reset()

    def reset(self):
        self.issued = self.taken = self.marks = 0
        self.last = []

    def plan(self, banks, jobs):
        for j in jobs:
            if j is None:
                self.marks += 1
                self.last.append((self.used, self.marks))
            elif not isinstance(j, str) and not isinstance(j[0], str):
                self.last.append(j)
            else:
                b, before = banks.jobs[j]
                self.last.append((banks.full[b], before + 1))

    def load(self, sp, source):
        u, s = self.issued, self.issued % SLOTS
        if u >= SLOTS:
            sp.wait_ge(*self.last[u - SLOTS])
        sp.dma_start(self.slots[:, s, :], source).then_inc(self.loaded[s], 16)
        self.issued += 1

    def unit(self, pe):
        u, s = self.taken, self.taken % SLOTS
        pe.wait_ge(self.loaded[s], 16 * (u // SLOTS + 1))
        self.taken += 1
        return self.slots[:, s, :]


class Chain:

    def __init__(self, eng, sem, start=0):
        self.eng, self.sem, self.n = eng, sem, start

    def __call__(self, ins):
        self.n += 1
        ins.then_inc(self.sem, 1)
        self.eng.wait_ge(self.sem, self.n)


def build(nc, stop_after, xT, consts, par1, bias1, w1, keys, wu, wv, par2, w2, out):
    ctx = ExitStack()
    with ctx:
        def sb(name, cols, dt=F32):
            return ctx.enter_context(nc.sbuf_tensor(name, [P, cols], dt))

        def sem(name):
            return ctx.enter_context(nc.semaphore(name))

        h = sb("h", DC * T)
        xn = sb("xn", DC * T)
        slots = sb("slots", SLOTS * SLOT)
        arena = sb("arena", 32768)
        cst = sb("cst", NCONST)
        p1 = sb("p1", NPAR1)
        small = sb("small", 2900)
        idx = sb("idx", 512, U32)

        hT = h[:, :].rearrange("p (c t) -> p c t", t=T)
        xnT = xn[:, :].rearrange("p (c t) -> p c t", t=T)
        slots_v = slots[:, :].rearrange("p (s n) -> p s n", s=SLOTS)

        def const(name):
            a, b = CONST[name]
            return cst[:, a:b]

        def par(name, table=PAR1):
            a, b = table[name]
            return (p1 if table is PAR1 else small)[:, a:b]

        ps = ctx.enter_context(nc.psum_tensor("ps", [P, 8 * 512], F32))
        psum = [ps[:, 512 * b:512 * b + 512] for b in range(8)]
        banks = Banks([sem(f"full{b}") for b in range(8)], [sem(f"drained{b}") for b in range(8)], psum)
        ring = Ring([sem(f"loaded{s}") for s in range(SLOTS)], sem("used"), slots_v)

        def view(at, *dims):
            n = int(np.prod(dims))
            v = arena[:, at:at + n]
            if len(dims) == 2:
                return v.rearrange("p (a b) -> p a b", b=dims[1])
            if len(dims) == 3:
                return v.rearrange("p (a b c) -> p a b c", b=dims[1], c=dims[2])
            return v

        def two(ap, w=T):
            return ap.rearrange("p (a b) -> p a b", b=w)

        def sum_squares(pe, name, squares, chunks, ready=None, matrix="ones"):
            bank = banks.open(pe, name)
            if ready:
                pe.wait_ge(*ready)
            for c in range(chunks):
                ins = pe.matmul(bank[:, 0:T], const(matrix), squares[:, c, :],
                                start=(c == 0), stop=(c == chunks - 1))
            banks.close(ins, name)

        def linear(pe, name, weights, source, kc, cols):
            bank = banks.open(pe, name)
            for j, c0 in enumerate(cols):
                for k in range(kc):
                    ins = pe.matmul(bank[:, j * T:(j + 1) * T], weights[:, k, c0:c0 + P], source[:, k, :],
                                    start=(k == 0), stop=(k == kc - 1))
            return ins

        def root_of_mean(eng, bank, n, std, width=T):
            return eng.activation(std, bank[:, 0:width], ACT.Sqrt, bias=eps[:, 0:1], scale=1.0 / n)

        eps = sb("eps", 4)
        std = sb("std", 512)
        rst = sb("rst", 512)

        gates = view(0, 16, T)
        uT = view(4096, UC, T)
        mix = view(5120, 8, T)
        attnT = view(7168, 8, T)
        V1 = view(9216, TT, T)
        qT = view(9728, 8, T)
        KZ = view(11776, 4, 2 * T)
        qraw = view(13824, 10, T)
        qsq = view(16384, 10, T)
        kn = view(18944, 2, T)
        sq = view(19456, 8, T)
        bias_v = view(22016, NH, T)

        loaded_x, loaded_c, loaded_b = sem("loaded_x"), sem("loaded_c"), sem("loaded_b")
        s_sq, s_std, s_xn, s_zero, s_qsq, s_gates, s_dve, s_kz = (
            sem(n) for n in ("sq1", "std1", "xn1", "zero", "qsq", "gates", "dve1", "kz"))

        banks.plan(["ms"] + [("u", i) for i in range(2)] + [("q", i) for i in range(4)] + ["k", "v"]
                   + [("qn", i) for i in range(5)] + [("g", i) for i in range(8)])

        ring.plan(banks, [("u", 0), ("u", 1), ("q", 0), ("q", 1), ("q", 2), ("q", 3), "k", "v"]
                  + [("g", i) for i in range(8)])

        with nc.Block() as block:
            @block.sync
            def _(sp):
                sp.dma_start(h[:, :], xT).then_inc(loaded_x, 16)
                sp.dma_start(cst[:, :], consts).then_inc(loaded_c, 16)
                sp.dma_start(p1[:, :], par1).then_inc(loaded_c, 16)
                for u in range(16 + SLOTS):
                    ring.load(sp, w1[u, :, :])
                sp.dma_start(bias_v, bias1.rearrange("p (a b) -> p a b", b=T)).then_inc(loaded_b, 16)
                sp.wait_ge(loaded_b, 16)

            @block.gpsimd
            def _(pool):
                pool.memset(eps[:, 0:1], EPS).then_inc(s_zero, 1)
                pool.memset(eps[:, 1:2], 0.0).then_inc(s_zero, 1)
                pool.memset(KZ, 0.0).then_inc(s_zero, 1)

            @block.scalar
            def _(act):
                act.wait_ge(loaded_x, 16)
                act.activation(sq, hT, ACT.Square).then_inc(s_sq, 1)
                act.wait_ge(s_zero, 2)
                b = banks.take(act, "ms")
                act.wait_ge(loaded_c, 32)
                ins = root_of_mean(act, b, D, std[:, 0:T])
                banks.give(ins, "ms")
                for i in range(4):
                    b = banks.take(act, ("q", i))
                    act.activation(qsq[:, 2 * i:2 * i + 2, :], two(b[:, :]), ACT.Square).then_inc(s_qsq, 1)
                    banks.give(act.activation(qraw[:, 2 * i:2 * i + 2, :], two(b[:, :]), ACT.Copy), ("q", i))
                b = banks.take(act, "k")
                act.activation(qsq[:, 8:10, :], two(b[:, :]), ACT.Square).then_inc(s_qsq, 1)
                banks.give(act.activation(qraw[:, 8:10, :], two(b[:, :]), ACT.Copy), "k")
                for i in range(5):
                    b = banks.take(act, ("qn", i))
                    if i:
                        act.wait_ge(s_kz, i)
                    else:
                        act.wait_ge(s_dve, 1)
                    banks.give(root_of_mean(act, b, HD, std[:, :], 512), ("qn", i))
                for i in range(8):
                    b = banks.take(act, ("g", i))
                    for j in range(2):
                        ins = act.activation(gates[:, 2 * i + j, :], b[:, j * T:(j + 1) * T], ACT.Sigmoid,
                                             bias=par("bgate")[:, 2 * i + j:2 * i + j + 1])
                    banks.give(ins, ("g", i))

            @block.vector
            def _(dve):
                link = Chain(dve, s_dve)
                banks.wait_drained(dve, "ms")
                link(dve.reciprocal(rst[:, 0:T], std[:, 0:T]))
                for c in range(DC):
                    dve.scalar_tensor_tensor(xnT[:, c, :], hT[:, c, :], par("ln1")[:, c:c + 1], rst[:, 0:T],
                                             ALU.mult, ALU.mult).then_inc(s_xn, 1)
                for i in range(2):
                    b = banks.take(dve, ("u", i))
                    banks.give(dve.tensor_copy(uT[:, 2 * i:2 * i + 2, :], two(b[:, :])), ("u", i))
                b = banks.take(dve, "v")
                banks.give(dve.tensor_copy(V1, two(b[:, :])), "v")
                for i in range(5):
                    banks.wait_drained(dve, ("qn", i))
                    dve.reciprocal(rst[:, :], std[:, :]).then_inc(s_kz, 1)
                    dve.wait_ge(s_kz, i + 1)
                    dst = qT[:, 2 * i:2 * i + 2, :] if i < 4 else kn
                    link(dve.scalar_tensor_tensor(dst, qraw[:, 2 * i:2 * i + 2, :], par("gq" if i < 4 else "gk"),
                                                  two(rst[:, :]), ALU.mult, ALU.mult))
                dve.wait_ge(s_zero, 3)
                for kv in range(NKV):
                    src = kn[64 * (kv % 2):64 * (kv % 2) + 64, kv // 2, :]
                    for v in range(2):
                        dve.tensor_copy(KZ[64 * v:64 * v + 64, kv, v * T:(v + 1) * T], src)

            @block.tensor
            def _(pe):
                pe.wait_ge(loaded_c, 32)
                sum_squares(pe, "ms", sq, DC, (s_sq, 1))
                pe.wait_ge(s_xn, DC)
                for i in range(16):
                    w = ring.unit(pe).rearrange("p (k n) -> p k n", k=DC)
                    name = (("u", i) if i < 2 else ("q", i - 2) if i < 6 else "k" if i == 6
                            else "v" if i == 7 else ("g", i - 8))
                    if i == 7:
                        bank = banks.open(pe, name)
                        for t in range(TT):
                            for k in range(DC):
                                ins = pe.matmul(bank[:, t * T:(t + 1) * T], xnT[:, k, t * P:(t + 1) * P], w[:, k, :],
                                                start=(k == 0), stop=(k == DC - 1))
                    else:
                        ins = linear(pe, name, w, xnT, DC, (0, P))
                    banks.close(ins, name)
                    if i == 7:
                        for n in range(5):
                            b = banks.open(pe, ("qn", n))
                            pe.wait_ge(s_qsq, n + 1)
                            banks.close(pe.matmul(b[:, :], const("blk64"), qsq[:, 2 * n:2 * n + 2, :],
                                                  start=True, stop=True), ("qn", n))

        def attention_tensor_scores(pe, pairs, name):
            for t in range(TT):
                for c, (queries, keys) in enumerate(pairs):
                    bank = banks.open(pe, (name, t, c))
                    w = P * (t + 1)
                    if len(keys) == 1:
                        ins = pe.matmul(bank[:, 0:2 * w], queries[0][:, t * P:(t + 1) * P], keys[0][:, :, 0:w],
                                        start=True, stop=True)
                    else:
                        for j in range(2):
                            ins = pe.matmul(bank[:, j * w:(j + 1) * w], queries[j][:, t * P:(t + 1) * P],
                                            keys[j][:, 0:w], start=True, stop=True)
                    banks.close(ins, (name, t, c))

        def attention_tensor_transposes(pe, S0, S1, head, name):
            bank = banks.open(pe, (name, head))
            pe.transpose(bank[:, 0:128], S0[:, head, :], const("ident"))
            pe.transpose(bank[:, 128:256], S1[:, head, 0:P], const("ident"))
            banks.close(pe.transpose(bank[:, 256:384], S1[:, head, P:T], const("ident")), (name, head))

        def attention_vector_scores(dve, S0, S1, npairs, scales, biases, name, t):
            S = (S0, S1)[t]
            w = P * (t + 1)
            for c in range(npairs):
                b = banks.take(dve, (name, t, c))
                banks.give(dve.scalar_tensor_tensor(S[:, 2 * c:2 * c + 2, :], two(b[:, 0:2 * w], w), scales(c),
                                                    biases(t, c), ALU.mult, ALU.add), (name, t, c))
            banks.wait_drained(dve, (name, t, npairs - 1))

        def bcast(ap, n):
            return ap.rearrange("p (a o) -> p a o", o=1).broadcast_to([P, ap.shape[1], n])

        S0 = view(13824, NH, P)
        S1 = view(26112, NH, T)
        PT = view(15872, NH, 384)
        st = small[:, 0:6 * TT * NH].rearrange("p (k t n) -> p k t n", k=6, t=TT)
        MX, NM, DEN, ES, RC, _SP = (st[:, i] for i in range(6))
        s_mx, s_den, s_es, s_p, s_dve2, s_pt = (sem(n) for n in ("mx2", "den2", "es2", "p2", "dve2", "pt2"))
        banks.plan([("s", t, c) for t in range(TT) for c in range(8)])
        for c in range(8):
            banks.plan([("t", 2 * c), ("t", 2 * c + 1), ("o", c)])

        with nc.Block() as block:
            @block.vector
            def _(dve):
                link = Chain(dve, s_dve2)
                for t in range(TT):
                    S = (S0, S1)[t]
                    attention_vector_scores(
                        dve, S0, S1, 8, lambda c: HD ** -0.5,
                        lambda t, c: bias_v[:, 2 * c:2 * c + 2, P * (1 - t):T], "s", t)
                    link(dve.tensor_reduce(MX[:, t, :], S, AX.X, ALU.max))
                    link(dve.tensor_tensor(MX[:, t, :], MX[:, t, :], par("sinks"), ALU.max))
                    dve.tensor_scalar(NM[:, t, :], MX[:, t, :], -1.0, None, ALU.mult).then_inc(s_mx, 1)
                    dve.wait_ge(s_mx, 2 * t + 1)
                    dve.tensor_tensor(ES[:, t, :], NM[:, t, :], par("sinks"), ALU.add).then_inc(s_mx, 1)
                for t in range(TT):
                    S = (S0, S1)[t]
                    dve.wait_ge(s_es, t + 1)
                    link(dve.tensor_tensor(DEN[:, t, :], DEN[:, t, :], ES[:, t, :], ALU.add))
                    link(dve.reciprocal(RC[:, t, :], DEN[:, t, :]))
                    dve.tensor_tensor(S, S, bcast(RC[:, t, :], P * (t + 1)), ALU.mult).then_inc(s_p, 1)

            @block.scalar
            def _(act):
                for t in range(TT):
                    S = (S0, S1)[t]
                    act.wait_ge(s_mx, 2 * t + 2)
                    for hd in range(NH):
                        act.activation(S[:, hd, :], S[:, hd, :], ACT.Exp, bias=NM[:, t, hd:hd + 1],
                                       accum_out=DEN[:, t, hd:hd + 1]).then_inc(s_den, 1)
                    act.wait_ge(s_den, NH * (t + 1))
                    act.activation(ES[:, t, :], ES[:, t, :], ACT.Exp).then_inc(s_es, 1)
                for c in range(8):
                    for j in range(2):
                        b = banks.take(act, ("t", 2 * c + j))
                        banks.give(act.activation(PT[:, 2 * c + j, :], b[:, 0:384], ACT.Copy), ("t", 2 * c + j))
                    if c:
                        b = banks.take(act, ("o", c - 1))
                        banks.give(act.activation(attnT[:, c - 1, :], b[:, 0:T], ACT.Copy), ("o", c - 1))
                b = banks.take(act, ("o", 7))
                banks.give(act.activation(attnT[:, 7, :], b[:, 0:T], ACT.Copy), ("o", 7))

            @block.tensor
            def _(pe):
                attention_tensor_scores(
                    pe, [((qT[:, c, :],), (KZ[:, c // 2, :].rearrange("p (v t) -> p v t", v=2),)) for c in range(8)], "s")
                pe.wait_ge(s_p, TT)
                for c in range(8):
                    for j in range(2):
                        attention_tensor_transposes(pe, S0, S1, 2 * c + j, "t")
                    bank = banks.open(pe, ("o", c))
                    for j in range(2):
                        hd = 2 * c + j
                        banks.wait_drained(pe, ("t", hd))
                        v = V1[:, :, 64 * (hd // 4):64 * (hd // 4) + 64]
                        rows = slice(64 * j, 64 * j + 64)
                        pe.matmul(bank[rows, 0:T], v[:, 0, :], PT[:, hd, 0:T], start=True, stop=False)
                        ins = pe.matmul(bank[rows, P:T], v[:, 1, :], PT[:, hd, T:384], start=False, stop=True)
                    banks.close(ins, ("o", c))

        CZ = view(9728, SC * 2, P)
        cosT, sinT, fr, kk, ta, tb, wr, wi, gr, gi = (view(13824 + 1024 * i, 4, T) for i in range(10))
        s5 = small[:, 0:24 * SC].rearrange("p (k n) -> p k n", n=SC)
        s5c = small[:, 24 * SC:24 * SC + 1536].rearrange("p (k n) -> p k n", k=6)
        MAGIC = 12582912.0
        TWO_PI = 2.0 * np.pi
        TURN = float(np.float32(TWO_PI * (1 - 1e-7)))
        (STEP, LS, TH, TAU, MAG, SIN, COS, TAUC, NR, NI, DN, CRE, CIM, TA, TB, KA, RDN) = range(17)
        s_a3, s_v3, s_tab, s_fr, s_g, s_gel, s_zero3, s_rot = (
            sem(n) for n in ("a3", "v3", "tab3", "fr3", "g3", "gel3", "zero3", "rot3"))
        s_b, s_y = sem("b3"), sem("y3")
        ring.plan(banks, [(s_b, 2), (s_b, 4)])

        def psum4(first):
            return ps[:, 512 * first:512 * first + 2048].rearrange("p (b n) -> p b n", n=512)

        with nc.Block() as block:
            @block.gpsimd
            def _(pool):
                pool.memset(CZ, 0.0).then_inc(s_zero3, 1)

            @block.scalar
            def _(act):
                link = Chain(act, s_a3)
                link(act.activation(s5[:, STEP], par("lstep"), ACT.Exp))
                act.wait_ge(s_v3, 2)
                link(act.activation(s5[:, MAG], s5[:, LS], ACT.Exp))
                act.wait_ge(s_v3, 9)
                act.activation(s5[:, SIN], s5[:, TAU], ACT.Sin, scale=TURN).then_inc(s_a3, 1)
                link_n = 3
                act.activation(s5[:, COS], s5[:, TAUC], ACT.Sin, scale=TURN).then_inc(s_a3, 1)
                for uc in range(UC):
                    act.wait_ge(s_fr, 2 * uc + 1)
                    act.activation(sinT, fr, ACT.Sin, scale=TURN).then_inc(s_tab, 1)
                    act.wait_ge(s_fr, 2 * uc + 2)
                    act.activation(cosT, kk, ACT.Sin, scale=TURN).then_inc(s_tab, 1)
                for uc in range(UC):
                    act.wait_ge(s_gel, uc + 1)
                    act.activation(uT[:, uc, :], uT[:, uc, :], ACT.Gelu).then_inc(s_a3, 1)

            @block.vector
            def _(dve):
                link = Chain(dve, s_v3)

                def col(i):
                    return s5[:, i]

                dve.wait_ge(s_a3, 1)
                link(dve.tensor_tensor(col(LS), par("lre"), col(STEP), ALU.mult))
                link(dve.tensor_tensor(col(TH), par("lim"), col(STEP), ALU.mult))
                link(dve.tensor_scalar(col(TAU), col(TH), 1.0 / TWO_PI, None, ALU.mult))
                link(dve.tensor_scalar(col(KA), col(TAU), MAGIC, None, ALU.add))
                link(dve.tensor_scalar(col(KA), col(KA), MAGIC, None, ALU.subtract))
                link(dve.tensor_tensor(col(TAU), col(TAU), col(KA), ALU.subtract))
                link(dve.tensor_scalar(col(KA), col(TAU), 0.25, None, ALU.is_ge))
                link(dve.tensor_scalar(col(TAUC), col(TAU), 0.25, None, ALU.add))
                link(dve.tensor_tensor(col(TAUC), col(TAUC), col(KA), ALU.subtract))
                link(dve.tensor_tensor(col(TA), par("lre"), par("lre"), ALU.mult))
                link(dve.tensor_tensor(col(TB), par("lim"), par("lim"), ALU.mult))
                link(dve.tensor_tensor(col(DN), col(TA), col(TB), ALU.add))
                link(dve.reciprocal(col(RDN), col(DN)))
                dve.wait_ge(s_a3, 4)
                link(dve.tensor_tensor(col(NR), col(MAG), col(COS), ALU.mult))
                link(dve.tensor_scalar(col(NR), col(NR), 1.0, None, ALU.subtract))
                link(dve.tensor_tensor(col(NI), col(MAG), col(SIN), ALU.mult))
                for out_col, x, y, op in ((CRE, NR, NI, ALU.add), (CIM, NI, NR, ALU.subtract)):
                    link(dve.tensor_tensor(col(TA), col(x), par("lre"), ALU.mult))
                    link(dve.tensor_tensor(col(TB), col(y), par("lim"), ALU.mult))
                    link(dve.tensor_tensor(col(TA), col(TA), col(TB), op))
                    link(dve.tensor_tensor(col(out_col), col(TA), col(RDN), ALU.mult))
                cs = par("cs5").rearrange("p (s k c) -> p k s c", k=2, c=16)

                def c5(i):
                    return s5c[:, i].rearrange("p (s c) -> p s c", c=16)

                link(dve.tensor_tensor(c5(0), cs[:, 0], bcast(col(CRE), 16), ALU.mult))
                link(dve.tensor_tensor(c5(1), cs[:, 1], bcast(col(CIM), 16), ALU.mult))
                link(dve.tensor_tensor(c5(2), cs[:, 0], bcast(col(CIM), 16), ALU.mult))
                link(dve.tensor_tensor(c5(3), cs[:, 1], bcast(col(CRE), 16), ALU.mult))
                link(dve.tensor_tensor(c5(4), c5(0), c5(1), ALU.subtract))
                link(dve.scalar_tensor_tensor(s5c[:, 5], s5c[:, 2], -1.0, s5c[:, 3], ALU.mult, ALU.subtract))
                dve.wait_ge(s_zero3, 1)
                for g in range(2):
                    for r in range(2):
                        for q in range(4):
                            dst = CZ[64 * g:64 * g + 64, :, :].rearrange("p (u q k) n -> p k q u n", q=4, k=2)
                            src = s5c[64 * g:64 * g + 64, 4 + r].rearrange("p (u q c) -> p q u c", q=4, c=16)
                            col0 = 32 * q + 16 * g
                            ins = dve.tensor_copy(dst[:, r, q, :, col0:col0 + 16], src[:, q])
                link(ins)

                def tables():
                    for i in range(4):
                        tau = col(TAU)[:, 4 * uc + i:4 * uc + i + 1]
                        ins = dve.tensor_scalar(kk[:, i, :], const("time"), tau, MAGIC, ALU.mult, ALU.add)
                    link(ins)
                    link(dve.tensor_scalar(kk, kk, MAGIC, None, ALU.subtract))
                    for i in range(4):
                        tau = col(TAU)[:, 4 * uc + i:4 * uc + i + 1]
                        ins = dve.scalar_tensor_tensor(fr[:, i, :], const("time"), tau, kk[:, i, :],
                                                       ALU.mult, ALU.subtract)
                    ins.then_inc(s_fr, 1)
                    dve.wait_ge(s_fr, 2 * uc + 1)
                    link(dve.tensor_scalar(kk, fr, 0.25, None, ALU.is_ge))
                    dve.scalar_tensor_tensor(kk, fr, 0.25, kk, ALU.add, ALU.subtract).then_inc(s_fr, 1)

                for uc in range(UC):
                    tables()
                    re, im = psum4(0)[:, :, 0:T], psum4(0)[:, :, T:2 * T]
                    dve.wait_ge(s_b, uc + 1)
                    dve.wait_ge(s_tab, 2 * uc + 2)
                    dve.tensor_tensor(ta, re, cosT, ALU.mult)
                    link(dve.tensor_tensor(tb, im, sinT, ALU.mult))
                    link(dve.tensor_tensor(wr, ta, tb, ALU.add))
                    dve.tensor_tensor(ta, im, cosT, ALU.mult)
                    link(dve.tensor_tensor(tb, re, sinT, ALU.mult))
                    dve.tensor_tensor(wi, ta, tb, ALU.subtract).then_inc(s_rot, 1)
                    dve.wait_ge(s_rot, uc + 1)
                    for i in range(4):
                        mag = col(MAG)[:, 4 * uc + i:4 * uc + i + 1].broadcast_to([P, T])
                        dve.tensor_tensor_scan(gr[:, i, :], mag, wr[:, i, :], 0.0, ALU.mult, ALU.add)
                        ins = dve.tensor_tensor_scan(gi[:, i, :], mag, wi[:, i, :], 0.0, ALU.mult, ALU.add)
                    link(ins)
                    dve.tensor_tensor(ta, gr, cosT, ALU.mult)
                    link(dve.tensor_tensor(tb, gi, sinT, ALU.mult))
                    link(dve.tensor_tensor(wr, ta, tb, ALU.subtract))
                    dve.tensor_tensor(ta, gr, sinT, ALU.mult)
                    link(dve.tensor_tensor(tb, gi, cosT, ALU.mult))
                    dve.tensor_tensor(wi, ta, tb, ALU.add).then_inc(s_g, 1)
                    dve.wait_ge(s_y, uc + 1)
                    dve.scalar_tensor_tensor(uT[:, uc, :], uT[:, uc, :], par("dskip")[:, uc:uc + 1],
                                             psum[4 + uc % 2][:, 0:T],
                                             ALU.mult, ALU.add).then_inc(s_gel, 1)

            @block.tensor
            def _(pe):
                for uc in range(UC):
                    if uc % 2 == 0:
                        w = ring.unit(pe).rearrange("p (u q k n) -> p u q k n", u=2, q=4, k=2)
                    if uc:
                        pe.wait_ge(s_rot, uc)
                    for i in range(4):
                        for k in range(2):
                            ins = pe.matmul(psum[i][:, k * T:(k + 1) * T], w[:, uc % 2, i, k, :], uT[:, uc, :],
                                            start=True, stop=True)
                    ins.then_inc(s_b, 1)
                    bank = psum[4 + uc % 2]
                    if uc >= 2:
                        pe.wait_ge(s_gel, uc - 1)
                    pe.wait_ge(s_g, uc + 1)
                    for i in range(4):
                        for k, src in enumerate((wr, wi)):
                            ins = pe.matmul(bank[:, 0:T], CZ[:, 2 * (4 * uc + i) + k, :], src[:, i, :],
                                            start=(i + k == 0), stop=(i + k == 4))
                    ins.then_inc(s_y, 1)

        gluT = view(9728, 4, T)
        sig = view(10752, 4, T)
        tmp = view(11776, 2, T)
        sq4 = view(12288, 8, T)
        s_mix, s_sq4, s_v4 = (sem(n) for n in ("mix4", "sq4", "v4"))
        banks.plan([("gb", i) for i in range(2)] + [("ga", i) for i in range(2)] + [("ya", i) for i in range(4)]
                   + [("ys", i) for i in range(4)] + [("out", i) for i in range(4)] + ["ms2"])
        ring.plan(banks, [("gb", 1), ("ga", 1)] + [("ya", i) for i in range(4)] + [("ys", 1), ("ys", 3)]
                  + [("out", i) for i in range(4)])

        with nc.Block() as block:
            @block.sync
            def _(sp):
                while ring.issued < 30 + SLOTS:
                    ring.load(sp, w1[ring.issued, :, :])

            @block.scalar
            def _(act):
                for i in range(2):
                    b = banks.take(act, ("gb", i))
                    banks.give(act.activation(sig[:, 2 * i:2 * i + 2, :], two(b[:, :]), ACT.Sigmoid), ("gb", i))
                for i in range(4):
                    banks.wait_drained(act, ("out", i))
                    act.activation(sq4[:, 2 * i:2 * i + 2, :], hT[:, 2 * i:2 * i + 2, :], ACT.Square).then_inc(s_sq4, 1)
                b = banks.take(act, "ms2")
                banks.give(root_of_mean(act, b, D, std[:, 0:T]), "ms2")

            @block.vector
            def _(dve):
                link = Chain(dve, s_v4)
                for i in range(2):
                    b = banks.take(dve, ("ga", i))
                    banks.wait_drained(dve, ("gb", i))
                    banks.give(dve.tensor_tensor(gluT[:, 2 * i:2 * i + 2, :], two(b[:, :]), sig[:, 2 * i:2 * i + 2, :],
                                                 ALU.mult), ("ga", i))
                for i in range(4):
                    b = banks.take(dve, ("ya", i))
                    banks.give(dve.tensor_tensor(mix[:, 2 * i:2 * i + 2, :], two(b[:, :]),
                                                 gates[:, 8 + 2 * i:10 + 2 * i, :], ALU.mult), ("ya", i))
                for i in range(4):
                    b = banks.take(dve, ("ys", i))
                    if i:
                        dve.wait_ge(s_mix, i)
                    banks.give(dve.tensor_tensor(tmp, two(b[:, :]), gates[:, 2 * i:2 * i + 2, :], ALU.mult), ("ys", i))
                    banks.wait_drained(dve, ("ys", i))
                    dve.tensor_tensor(mix[:, 2 * i:2 * i + 2, :], mix[:, 2 * i:2 * i + 2, :], tmp,
                                      ALU.add).then_inc(s_mix, 1)
                for i in range(4):
                    b = banks.take(dve, ("out", i))
                    banks.give(dve.tensor_tensor(hT[:, 2 * i:2 * i + 2, :], hT[:, 2 * i:2 * i + 2, :], two(b[:, :]),
                                                 ALU.add), ("out", i))
                banks.wait_drained(dve, "ms2")
                link(dve.reciprocal(rst[:, 0:T], std[:, 0:T]))
                for c in range(DC):
                    dve.scalar_tensor_tensor(xnT[:, c, :], hT[:, c, :], par("ln2")[:, c:c + 1], rst[:, 0:T],
                                             ALU.mult, ALU.mult)

            @block.tensor
            def _(pe):
                for name in ("gb", "ga"):
                    w = ring.unit(pe).rearrange("p (k n) -> p k n", k=4)
                    for i in range(2):
                        banks.close(linear(pe, (name, i), w, uT, 4, (2 * i * P, 2 * i * P + P)), (name, i))
                for i in range(4):
                    w = ring.unit(pe).rearrange("p (k n) -> p k n", k=DC)
                    banks.close(linear(pe, ("ya", i), w, attnT, DC, (0, P)), ("ya", i))
                for i in range(4):
                    if i % 2 == 0:
                        w = ring.unit(pe).rearrange("p (k n) -> p k n", k=4)
                    if i == 0:
                        banks.wait_drained(pe, ("ga", 1))
                    c = 2 * (i % 2) * P
                    banks.close(linear(pe, ("ys", i), w, gluT, 4, (c, c + P)), ("ys", i))
                pe.wait_ge(s_mix, 4)
                for i in range(4):
                    w = ring.unit(pe).rearrange("p (k n) -> p k n", k=DC)
                    banks.close(linear(pe, ("out", i), w, mix, DC, (0, P)), ("out", i))
                sum_squares(pe, "ms2", sq4, DC, (s_sq4, 4))

        qp = view(0, PH, T)
        keys_v = view(2048, PH, T)
        s_v = view(4096, TT, PH * 2, NSUB)
        cand = view(8192, TT, PH, 256)
        eq = view(12288, PH * TOPK, TOPK)
        sel = view(14336, PH * TOPK, TOPK)
        f5 = arena[:, 16384:16384 + 8 * 512]
        vals = f5[:, 0:512].rearrange("p (t g n) -> p t g n", t=TT, n=TOPK)
        idxf = f5[:, 512:1024].rearrange("p (t g n) -> p t g n", t=TT, n=TOPK)
        best = f5[:, 1024:1280].rearrange("p (g n) -> p g n", n=TOPK)
        gate = f5[:, 1280:1536].rearrange("p (g n) -> p g n", n=TOPK)
        rank = f5[:, 1536:2048].rearrange("p (k t n) -> p k t n", k=2, t=TT)
        chosen = f5[:, 2048:2560].rearrange("p (k t n) -> p k t n", k=2, t=TT)
        gsum = f5[:, 2560:2576]
        iota16 = const("lane")[:, 0:TOPK]
        ranku = f5[:, 2688:3200].bitcast(U32).rearrange("p (k n) -> p k n", k=2)
        per_slot = small[:, 0:768].rearrange("p (k t) -> p k t", k=3)
        I1, I2, GT = per_slot[:, 0], per_slot[:, 1], per_slot[:, 2]
        idx_v = idx[:, :].rearrange("p (t g n) -> p t g n", t=TT, n=TOPK)
        pos = f5[:, 3200:3456].bitcast(U32).rearrange("p (g n) -> p g n", n=TOPK)
        s_keys, s_v5, s_e5, s_x5, s_sel = (sem(n) for n in ("keys5", "v5", "e5", "x5", "sel5"))
        banks.plan([("pq", i) for i in range(4)] + [("ps", i) for i in range(8)] + [("tr", k) for k in range(3)])
        ring.plan(banks, [("pq", i) for i in range(4)])

        with nc.Block() as block:
            @block.sync
            def _(sp):
                sp.dma_start(keys_v, keys.rearrange("p (h n) -> p h n", h=PH)).then_inc(s_keys, 16)
                for u in range(SLOTS):
                    ring.load(sp, wu[u, :, :])
                sp.wait_ge(s_keys, 16)

            @block.scalar
            def _(act):
                for i in range(4):
                    b = banks.take(act, ("pq", i))
                    banks.give(act.activation(qp[:, 2 * i:2 * i + 2, :], two(b[:, :]), ACT.Copy), ("pq", i))
                for i in range(8):
                    b = banks.take(act, ("ps", i))
                    dst = s_v[:, i // 4, 4 * (i % 4):4 * (i % 4) + 4, :]
                    banks.give(act.activation(dst, two(b[:, :], P), ACT.Copy), ("ps", i))
                act.wait_ge(s_x5, 1)
                act.activation(gate, gate, ACT.Exp).then_inc(s_e5, 1)
                for k in range(3):
                    b = banks.take(act, ("tr", k))
                    banks.give(act.activation(per_slot[:, k], b[:, 0:T], ACT.Copy), ("tr", k))

            @block.vector
            def _(dve):
                link = Chain(dve, s_v5)
                low = -3e38

                def top16(rows, values, indices):
                    for a in (0, 8):
                        for r, v, i in zip(rows, values, indices):
                            ins = dve.max(v[:, a:a + 8], r)
                        link(ins)
                        for r, v, i in zip(rows, values, indices):
                            ins = dve.max_index(i[:, a:a + 8], v[:, a:a + 8], r)
                        if a == 0:
                            link(ins)
                            for r, v, i in zip(rows, values, indices):
                                ins = dve.match_replace(r, v[:, 0:8], r, low)
                            link(ins)
                    link(ins)

                for t in range(TT):
                    for i in range(4):
                        banks.wait_drained(dve, ("ps", 4 * t + i))
                    top16([s_v[:, t, g, :] for g in range(16)], [vals[:, t, g, :] for g in range(16)],
                          [idx_v[:, t, g, :] for g in range(16)])
                    pair = vals[:, t].rearrange("p (h k) n -> p h k n", k=2)
                    first = pair[:, :, 0, :].rearrange("p h (n o) -> p h n o", o=1).broadcast_to([P, PH, 16, 16])
                    second = pair[:, :, 1, :].rearrange("p h (o n) -> p h o n", o=1).broadcast_to([P, PH, 16, 16])
                    link(dve.tensor_tensor(cand[:, t].rearrange("p h (i j) -> p h i j", j=16), first, second, ALU.add))
                    top16([cand[:, t, g, :] for g in range(PH)], [best[:, PH * t + g, :] for g in range(PH)],
                          [pos[:, PH * t + g, :] for g in range(PH)])
                dve.tensor_copy(idxf, idx_v)
                dve.tensor_tensor(gate, best, best[:, :, 0:1].broadcast_to([P, TT * PH, TOPK]),
                                  ALU.subtract).then_inc(s_x5, 1)
                posf = pos.rearrange("p g n -> p (g n)")
                dve.tensor_scalar(ranku[:, 0], posf, 4, None, ALU.logical_shift_right)
                link(dve.tensor_scalar(ranku[:, 1], posf, 15, None, ALU.bitwise_and))
                link(dve.tensor_copy(rank, ranku.rearrange("p k (t n) -> p k t n", t=TT)))
                for t in range(TT):
                    pair = idxf[:, t].rearrange("p (h k) n -> p h k n", k=2)
                    for k in range(2):
                        link(dve.tensor_tensor(
                            eq, bcast(rank[:, k, t, :], TOPK),
                            iota16.rearrange("p (o n) -> p o n", o=1).broadcast_to([P, P, TOPK]), ALU.is_equal))
                        place = pair[:, :, k, :].rearrange("p h (o n) -> p h o n", o=1).broadcast_to([P, PH, 16, 16])
                        link(dve.tensor_tensor(sel.rearrange("p (h r) n -> p h r n", h=PH),
                                               eq.rearrange("p (h r) n -> p h r n", h=PH), place, ALU.mult))
                        dve.tensor_reduce(chosen[:, k, t, :], sel, AX.X, ALU.add).then_inc(s_sel, 1)
                dve.wait_ge(s_e5, 1)
                link(dve.tensor_reduce(gsum, gate, AX.X, ALU.add))
                link(dve.reciprocal(gsum, gsum))
                dve.tensor_tensor(gate, gate, bcast(gsum, TOPK), ALU.mult).then_inc(s_sel, 1)

            @block.tensor
            def _(pe):
                for i in range(4):
                    w = ring.unit(pe).rearrange("p (k n) -> p k n", k=DC)
                    banks.close(linear(pe, ("pq", i), w, xnT, DC, (0, P)), ("pq", i))
                pe.wait_ge(s_keys, 16)
                for i in range(8):
                    bank = banks.open(pe, ("ps", i))
                    t = i // 4
                    for j in range(2):
                        hd = 2 * (i % 4) + j
                        if j == 0:
                            banks.wait_drained(pe, ("pq", i % 4))
                        ins = pe.matmul(bank[:, j * T:(j + 1) * T], qp[:, hd, t * P:(t + 1) * P], keys_v[:, hd, :],
                                        start=True, stop=True)
                    banks.close(ins, ("ps", i))
                pe.wait_ge(s_sel, 5)
                gate_t = gate.rearrange("p (t h) n -> p t (h n)", t=TT)
                for k in range(3):
                    bank = banks.open(pe, ("tr", k))
                    for t in range(TT):
                        src = chosen[:, k, t, :] if k < 2 else gate_t[:, t, :]
                        ins = pe.transpose(bank[:, t * P:(t + 1) * P], src, const("ident"))
                    banks.close(ins, ("tr", k))
        if stop_after == "retrieve":
            return

        A = view(0, NE2, T)
        UNITS = NE2 // 2
        base = 34

        def slot_of(n, j):
            return (base + j) % SLOTS, 16 * ((base + j) // SLOTS + 1)

        a_full, a_drained = sem("a_full"), sem("a_drained")

        with nc.Block() as block:
            @block.sync
            def _(sp):
                with sp.Fori(0, (UNITS - SLOTS) // SLOTS) as it:
                    for j in range(SLOTS):
                        s, _ = slot_of(0, j)
                        sp.wait_ge(a_full, it * SLOTS + (j + 1))
                        sp.dma_start(slots_v[:, s, :], wu[it * SLOTS + (SLOTS + j), :, :]).then_inc(ring.loaded[s], 16)
                for j in range(SLOTS):
                    s, _ = slot_of(0, j)
                    sp.wait_ge(a_full, UNITS - SLOTS + j + 1)
                    sp.dma_start(slots_v[:, s, :], wv[j, :, :]).then_inc(ring.loaded[s], 16)

            @block.scalar
            def _(act):
                with act.Fori(0, UNITS // 8) as it:
                    for j in range(8):
                        act.wait_ge(a_full, it * 8 + (j + 1))
                        act.activation(A[:, bass.ds(it * 16 + 2 * j, 2), :], two(psum[j]), ACT.Gelu).then_inc(a_drained, 1)

            @block.tensor
            def _(pe):
                def body(it, first):
                    for j in range(8):
                        s, count = slot_of(0, j)
                        if not first:
                            pe.wait_ge(a_drained, it * 8 + (j - 7))
                        pe.wait_ge(ring.loaded[s], it * 32 + count)
                        w = slots_v[:, s, :].rearrange("p (e k n) -> p e k n", e=2, k=DC)
                        for e in range(2):
                            for k in range(DC):
                                ins = pe.matmul(psum[j][:, e * T:(e + 1) * T], w[:, e, k, :], xnT[:, k, :],
                                                start=(k == 0), stop=(k == DC - 1))
                        ins.then_inc(a_full, 1)
                body(0, True)
                with pe.Fori(1, UNITS // 8) as it:
                    body(it, False)

        oh = small[:, 768:768 + 2048].rearrange("p (b k t n) -> p b k t n", b=2, k=2, t=4)
        OH1, OH2 = oh[:, :, 0], oh[:, :, 1]
        GROUPS = T // 4
        g_one, g_full, g_done = (sem(n) for n in ("onehot", "grid_full", "grid_done"))

        with nc.Block() as block:
            @block.vector
            def _(dve):
                def build(n, b, early):
                    if not early:
                        dve.wait_ge(g_full, n - 1)
                    for t in range(4):
                        at = n * 4 + t
                        ins = dve.tensor_scalar(OH1[:, b, t, :], const("lane"), I1[:, bass.ds(at, 1)],
                                                GT[:, bass.ds(at, 1)], ALU.is_equal, ALU.mult)
                        ins = dve.tensor_scalar(OH2[:, b, t, :], const("lane"), I2[:, bass.ds(at, 1)], None,
                                                ALU.is_equal)
                    ins.then_inc(g_one, 1)

                def spread(n, bank):
                    dve.wait_ge(g_full, n + 1)
                    a = A[:, :, bass.ds(n * 4, 4)]
                    dve.tensor_tensor(a, psum[bank].rearrange("p (t e) -> p e t", t=4), a, ALU.mult).then_inc(g_done, 1)

                build(0, 0, True)
                build(1, 1, True)
                spread(0, 0)
                with dve.Fori(0, (GROUPS - 4) // 4) as it:
                    for j in range(4):
                        build(it * 4 + (j + 2), j % 2, False)
                        spread(it * 4 + (j + 1), (j + 1) % 4)
                for n in range(GROUPS - 4, GROUPS - 1):
                    if n + 2 < GROUPS:
                        build(n + 2, n % 2, False)
                    spread(n + 1, (n + 1) % 4)

            @block.tensor
            def _(pe):
                def body(it, first):
                    for j in range(4):
                        if not first:
                            pe.wait_ge(g_done, it * 4 + (j - 3))
                        pe.wait_ge(g_one, it * 4 + (j + 1))
                        for t in range(4):
                            ins = pe.matmul(psum[j][:, t * P:(t + 1) * P], OH1[:, j % 2, t, :], OH2[:, j % 2, t, :],
                                            start=True, stop=True)
                        ins.then_inc(g_full, 1)
                body(0, True)
                with pe.Fori(1, GROUPS // 4) as it:
                    body(it, False)

        v_used, s_h8 = sem("v_used"), sem("h8")

        with nc.Block() as block:
            @block.sync
            def _(sp):
                with sp.Fori(0, (UNITS - SLOTS) // SLOTS) as it:
                    for j in range(SLOTS):
                        s, _ = slot_of(0, j)
                        sp.wait_ge(v_used, it * SLOTS + (j + 1))
                        sp.dma_start(slots_v[:, s, :], wv[it * SLOTS + (SLOTS + j), :, :]).then_inc(ring.loaded[s], 16)

            @block.vector
            def _(dve):
                dve.wait_ge(v_used, UNITS)
                for b in range(4):
                    dve.tensor_tensor(hT[:, 2 * b:2 * b + 2, :], hT[:, 2 * b:2 * b + 2, :], two(psum[b]),
                                      ALU.add).then_inc(s_h8, 1)

            @block.tensor
            def _(pe):
                def body(it, first):
                    for j in range(SLOTS):
                        s, count = slot_of(0, j)
                        pe.wait_ge(ring.loaded[s], it * 16 + (count + 16 * (UNITS // SLOTS)))
                        w = slots_v[:, s, :].rearrange("p (e n) -> p e n", e=2)
                        for e in range(2):
                            for c in range(DC):
                                ins = pe.matmul(psum[c // 2][:, (c % 2) * T:(c % 2 + 1) * T],
                                                w[:, e, c * P:(c + 1) * P],
                                                A[:, bass.ds(it * 8 + (2 * j + e), 1), :].rearrange("p o t -> p (o t)"),
                                                start=(first and j + e == 0 and c % 2 == 0), stop=False,
                                                skip_group_check=True)
                        ins.then_inc(v_used, 1)
                body(0, True)
                with pe.Fori(1, UNITS // SLOTS) as it:
                    body(it, False)
        if stop_after == "peer":
            return

        banks.reset()
        ring.reset()
        raw = view(0, 8, T)
        qA = view(2048, 4, T)
        KZ2 = arena[:, 3072:5120].rearrange("p (b g v t) -> p b g v t", b=2, g=2, v=2)
        KZC = arena[:, 5120:5184].rearrange("p (g v i) -> p g v i", g=2, v=2)
        kcr = arena[:, 5184:5440]
        X = arena[:, 5440:6464].rearrange("p (k l n) -> p k l n", k=2, l=16)
        Z = arena[:, 6464:7488].rearrange("p (k g t) -> p k g t", k=2, g=2)
        cq, cqn = view(7488, 2, T), view(8000, 2, T)
        ckr = view(8512, 2, T)
        ckvn = arena[:, 9024:9280]
        kpe = arena[:, 9280:9536]
        qMr, qM, KM = view(9536, 8, T), view(11584, 8, T), view(13632, 8, T)
        V2, Vm = view(15680, TT, T), view(16192, TT, 512)
        GA = arena[:, 17216:17264].rearrange("p (t h b) -> p t h b", t=TT, b=3)
        hid = arena[:, 17264:17392].rearrange("p (k c n) -> p k c n", k=2, c=2)
        vcmp = view(17392, 2, 64)
        ra, rb = view(17520, 2, T), view(18032, 2, T)
        sqL = view(18544, 8, T)
        sqc = view(20592, 3, T)
        SA0, SA1 = view(18544, 24, P), view(21616, 24, T)
        PTR = view(27760, 8, 384)
        Sc = arena[:, 30832:31088].rearrange("p (t h i) -> p t h i", t=TT, h=8)
        PTC = view(0, 8, T)
        aT = view(9536, 8, T)
        sqo = view(2048, 8, T)
        mixT = view(11584, 8, T)
        hidden = view(13632, FC, T)
        relu = view(21824, 4, T).rearrange("p (b c) t -> p b c t", b=2)
        st2 = small[:, 512:512 + 192].rearrange("p (k t n) -> p k t n", k=4, t=TT)
        MX2, NM2, DEN2, RC2 = (st2[:, i] for i in range(4))
        stc = small[:, 704:704 + 48].rearrange("p (k t n) -> p k t n", k=3, t=TT)

        def p2(name):
            return par(name, PAR2)

        names = ("lpar", "lsq", "lxn", "lzero", "lstep", "lsqc", "lrope", "lX", "lcx", "lkzc", "lmsq", "lmskv", "lku",
                 "amx", "aden", "ap", "avec", "acv", "acx", "acp", "az", "fsq", "fmix", "frelu", "fhid", "fvec", "fh",
                 "fsq2", "fxn2", "lcopies")
        L = {n: sem(n) for n in names}
        loop_sems = ring.loaded + [ring.used] + banks.full + banks.drained + list(L.values())

        banks.plan(["ms", ("in", 0), ("in", 1), ("in", 2), ("in", 3), ("in", 4), ("in", 5), "V", "G",
                    "rc", "msq", "mskv", ("rp", 0), ("rp", 1), ("rp", 2), "rk"]
                   + [("uq", i) for i in range(4)] + [("uk", i) for i in range(4)] + [("uv", t) for t in range(TT)]
                   + [("ck", 0), ("ck", 1), ("cv", 0), ("cv", 1)] + [("rq", i) for i in range(4)] + ["k2", "v2"])
        ring.plan(banks, [("in", i) for i in range(6)] + ["V", ("uq", 3), ("uv", 1), None, ("ck", 1), None, ("cv", 1)])

        pair_jobs = []
        for c in range(8):
            if c < 4:
                pair_jobs.append(([("tc", c)], [2 * c, 2 * c + 1, 8 + 2 * c, 9 + 2 * c]))
            else:
                pair_jobs.append(([], [8 + 2 * c, 9 + 2 * c]))
        banks.plan(["sc"] + [("s2", t, c) for t in range(TT) for c in range(12)])
        for c, (tc, heads) in enumerate(pair_jobs):
            banks.plan(tc + [("t2", hd) for hd in heads] + [("o2", c)])
        order = [hd for _, heads in pair_jobs for hd in heads]
        slot = {hd: i % 8 for i, hd in enumerate(order)}

        banks.plan(["mo0", "mo1"] + [("wo", i) for i in range(4)] + ["mf"] + [("f1", i) for i in range(16)]
                   + [("f2", b) for b in range(4)])
        ring.plan(banks, [("wo", i) for i in range(4)] + [("f1", i) for i in range(16)]
                  + [None] * 15 + [("f2", 3)])

        with nc.Fori(0, LAYERS) as layer:
            with nc.Block() as block:
                @block.gpsimd
                def _(pool):
                    for x in loop_sems:
                        pool.sem_clear(x)

            with nc.Block() as block:
                @block.sync
                def _(sp):
                    sp.dma_start(small[:, 0:NPAR2], par2[layer, :, :]).then_inc(L["lpar"], 16)
                    for u in range(13 + SLOTS):
                        ring.load(sp, w2[layer, u, :, :])

                @block.gpsimd
                def _(pool):
                    pool.memset(KZ2, 0.0).then_inc(L["lzero"], 1)
                    pool.memset(arena[:, 5120:5184], 0.0).then_inc(L["lzero"], 1)
                    pool.memset(vcmp, 0.0).then_inc(L["lzero"], 1)

                @block.scalar
                def _(act):
                    act.activation(sqL, hT, ACT.Square).then_inc(L["lsq"], 1)
                    b = banks.take(act, "ms")
                    banks.give(root_of_mean(act, b, D, std[:, 0:T]), "ms")
                    for i in range(4):
                        b = banks.take(act, ("in", i))
                        banks.give(act.activation(raw[:, 2 * i:2 * i + 2, :], two(b[:, :]), ACT.Copy), ("in", i))
                    b = banks.take(act, ("in", 4))
                    act.activation(sqc[:, 0:2, :], two(b[:, :]), ACT.Square).then_inc(L["lsqc"], 1)
                    banks.give(act.activation(cq, two(b[:, :]), ACT.Copy), ("in", 4))
                    b = banks.take(act, ("in", 5))
                    act.activation(sqc[:, 2, :], b[:, 0:T], ACT.Square).then_inc(L["lsqc"], 1)
                    banks.give(act.activation(ckr, two(b[:, :]), ACT.Copy), ("in", 5))
                    b = banks.take(act, "V")
                    banks.give(act.activation(V2, two(b[:, :]), ACT.Copy), "V")
                    b = banks.take(act, "G")
                    banks.give(act.activation(arena[:, 17216:17264], b[:, 0:48], ACT.Sigmoid), "G")
                    b = banks.take(act, "msq")
                    act.wait_ge(L["lstep"], 1)
                    banks.give(root_of_mean(act, b, 256, std[:, 0:T]), "msq")
                    b = banks.take(act, "mskv")
                    banks.give(root_of_mean(act, b, 128, std[:, T:2 * T]), "mskv")
                    for i in range(4):
                        b = banks.take(act, ("uq", i))
                        banks.give(act.activation(qMr[:, 2 * i:2 * i + 2, :], two(b[:, :]), ACT.Copy), ("uq", i))
                    for t in range(TT):
                        b = banks.take(act, ("uv", t))
                        banks.give(act.activation(Vm[:, t, :], b[:, :], ACT.Copy), ("uv", t))
                    for k, n in enumerate(("ck", "cv")):
                        for c in range(2):
                            b = banks.take(act, (n, c))
                            banks.give(act.activation(hid[:, k, c, 0:30], b[:, 0:30], ACT.Silu), (n, c))

                @block.vector
                def _(dve):
                    link = Chain(dve, L["lstep"])
                    banks.wait_drained(dve, "ms")
                    link(dve.reciprocal(rst[:, 0:T], std[:, 0:T]))
                    dve.wait_ge(L["lpar"], 16)
                    for c in range(DC):
                        dve.scalar_tensor_tensor(xnT[:, c, :], hT[:, c, :], p2("attn")[:, c:c + 1], rst[:, 0:T],
                                                 ALU.mult, ALU.mult).then_inc(L["lxn"], 1)

                    def rope(job, source, tag, outs):
                        n = source.shape[1]
                        cos, sin = (const(f + tag).rearrange("p (o t) -> p o t", o=1).broadcast_to([P, n, T])
                                    for f in ("cos", "sin"))
                        b = banks.take(dve, job)
                        dve.tensor_tensor(ra[:, 0:n, :], source, cos, ALU.mult).then_inc(L["lcopies"], 1)
                        banks.give(dve.tensor_tensor(rb[:, 0:n, :], two(b[:, 0:n * T]), sin, ALU.mult), job)
                        banks.wait_drained(dve, job)
                        ropes.append(1)
                        dve.wait_ge(L["lcopies"], len(ropes))
                        link(outs(ra[:, 0:n, :], rb[:, 0:n, :]))

                    ropes = []

                    def add_to(dst):
                        return lambda x, y: dve.tensor_tensor(dst, x, y, ALU.add)

                    def windows(k, source):
                        for g in range(2):
                            dve.tensor_copy(Z[0:64, k, g, :], source[64 * g:64 * g + 64, :])
                            ins = dve.tensor_copy(Z[64:128, k, g, 0:T - 1], source[64 * g:64 * g + 64, 1:T])
                        link(ins)
                        z = Z[:, k].rearrange("p g (i l two) -> p l g i two", l=8, two=2)[:, :, :, :, 0]
                        pos = p2("posk" if k == 0 else "posv")
                        for half in range(2):
                            add = pos[:, 8 * half:8 * half + 8].rearrange("p (l a b) -> p l a b", a=1, b=1)\
                                .broadcast_to([P, 8, 2, NCMP])
                            dve.tensor_tensor(X[:, k, 8 * half:8 * half + 8, 0:30].rearrange("p l (g i) -> p l g i", g=2),
                                              z[:, :, :, half:half + NCMP], add, ALU.add).then_inc(L["lX"], 1)

                    rope("rc", raw[:, 4:5, :], "A", add_to(kcr.rearrange("p (o t) -> p o t", o=1)))
                    dve.memset(Z[64:128, :, :, T - 1:T], 0.0)
                    windows(0, kcr)
                    banks.wait_drained(dve, ("in", 2))
                    windows(1, raw[:, 5, :])
                    banks.wait_drained(dve, "msq")
                    banks.wait_drained(dve, "mskv")
                    link(dve.reciprocal(rst[:, :], std[:, :]))
                    for c in range(2):
                        dve.scalar_tensor_tensor(cqn[:, c, :], cq[:, c, :], p2("qn")[:, c:c + 1], rst[:, 0:T],
                                                 ALU.mult, ALU.mult).then_inc(L["lcx"], 1)
                    dve.scalar_tensor_tensor(ckvn, ckr[:, 0, :], p2("kvn"), rst[:, T:2 * T],
                                             ALU.mult, ALU.mult).then_inc(L["lcx"], 1)
                    for i in range(2):
                        rope(("rp", i), raw[:, 2 * i:2 * i + 2, :], "A", add_to(qA[:, 2 * i:2 * i + 2, :]))
                    dve.wait_ge(L["lzero"], 3)

                    def split_keys(x, y):
                        for g in range(2):
                            r = slice(64 * g, 64 * g + 64)
                            for v in range(2):
                                ins = dve.tensor_tensor(KZ2[64 * v:64 * v + 64, :, g, v, :], x[r], y[r], ALU.add)
                        return ins

                    rope(("rp", 2), raw[:, 6:8, :], "A", split_keys)
                    rope("rk", ckr[:, 1:2, :], "B", add_to(kpe.rearrange("p (o t) -> p o t", o=1)))
                    kpe2 = kpe.rearrange("p (o t) -> p o t", o=1).broadcast_to([P, 2, T])
                    for i in range(4):
                        b = banks.take(dve, ("uk", i))
                        banks.give(dve.tensor_tensor(KM[:, 2 * i:2 * i + 2, :], two(b[:, :]), kpe2, ALU.add), ("uk", i))
                    for i in range(4):
                        rope(("rq", i), qMr[:, 2 * i:2 * i + 2, :], "B", add_to(qM[:, 2 * i:2 * i + 2, :]))
                    b = banks.take(dve, "k2")
                    src = b[0:64, 0:30].rearrange("p (g i) -> p g i", g=2)
                    dve.tensor_copy(KZC[0:64, :, 0, 0:NCMP], src)
                    banks.give(dve.tensor_copy(KZC[64:128, :, 1, 0:NCMP], src), "k2")
                    b = banks.take(dve, "v2")
                    banks.give(dve.tensor_copy(vcmp[0:NCMP], two(b[0:NCMP, 0:128], 64)), "v2")

                @block.tensor
                def _(pe):
                    sum_squares(pe, "ms", sqL, DC, (L["lsq"], 1))
                    pe.wait_ge(L["lxn"], DC)
                    for i in range(6):
                        w = ring.unit(pe).rearrange("p (k n) -> p k n", k=DC)
                        banks.close(linear(pe, ("in", i), w, xnT, DC, (0, P)), ("in", i))
                    w = ring.unit(pe).rearrange("p (k n) -> p k n", k=DC)
                    bank = banks.open(pe, "V")
                    for t in range(TT):
                        for k in range(DC):
                            ins = pe.matmul(bank[:, t * T:(t + 1) * T], xnT[:, k, t * P:(t + 1) * P], w[:, k, :],
                                            start=(k == 0), stop=(k == DC - 1))
                    banks.close(ins, "V")
                    bank = banks.open(pe, "G")
                    wg = p2("wg").rearrange("p (k n) -> p k n", k=DC)
                    for t in range(TT):
                        for k in range(DC):
                            ins = pe.matmul(bank[:, t * 24:(t + 1) * 24], xnT[:, k, t * P:(t + 1) * P], wg[:, k, :],
                                            start=(k == 0), stop=(k == DC - 1))
                    banks.close(ins, "G")

                    def rotate(job, matrix, source, after):
                        n = source.shape[1]
                        bank = banks.open(pe, job)
                        banks.wait_drained(pe, after)
                        banks.close(pe.matmul(bank[:, 0:n * T], const(matrix), source, start=True, stop=True), job)

                    rotate("rc", "rot64", raw[:, 4:5, :], ("in", 2))
                    sum_squares(pe, "msq", sqc, 2, (L["lsqc"], 1))
                    sum_squares(pe, "mskv", sqc[:, 2:3, :], 1, (L["lsqc"], 2))
                    for i in range(2):
                        rotate(("rp", i), "rot64", raw[:, 2 * i:2 * i + 2, :], ("in", i))
                    rotate(("rp", 2), "rot64", raw[:, 6:8, :], ("in", 3))
                    rotate("rk", "rot32", ckr[:, 1:2, :], ("in", 5))
                    w = ring.unit(pe).rearrange("p (k n) -> p k n", k=2)
                    pe.wait_ge(L["lcx"], 3)
                    for i in range(4):
                        banks.close(linear(pe, ("uq", i), w, cqn, 2, (2 * i * P, 2 * i * P + P)), ("uq", i))
                    w = ring.unit(pe)
                    for i in range(4):
                        bank = banks.open(pe, ("uk", i))
                        for j in range(2):
                            ins = pe.matmul(bank[:, j * T:(j + 1) * T], w[:, (2 * i + j) * P:(2 * i + j + 1) * P], ckvn,
                                            start=True, stop=True)
                        banks.close(ins, ("uk", i))
                    for t in range(TT):
                        bank = banks.open(pe, ("uv", t))
                        banks.close(pe.matmul(bank[:, :], ckvn[:, t * P:(t + 1) * P], w[:, 1024:1536],
                                              start=True, stop=True), ("uv", t))
                    for k, n in enumerate(("ck", "cv")):
                        two_banks = [banks.open(pe, (n, c)) for c in range(2)]
                        pe.wait_ge(L["lX"], 2 * k + 2)
                        for half in range(2):
                            w = ring.unit(pe).rearrange("p (l n) -> p l n", n=T)
                            for lp in range(8):
                                for c in range(2):
                                    ins = pe.matmul(two_banks[c][:, 0:30], w[:, lp, c * P:(c + 1) * P],
                                                    X[:, k, 8 * half + lp, 0:30], start=(half + lp == 0),
                                                    stop=(half == 1 and lp == 7))
                                    if half == 1 and lp == 7:
                                        banks.close(ins, (n, c))
                            if half == 0:
                                ins.then_inc(ring.used, 1)
                    for i in range(4):
                        rotate(("rq", i), "rot32", qMr[:, 2 * i:2 * i + 2, :], ("uq", i))
                    banks.wait_drained(pe, ("cv", 1))
                    bank = banks.open(pe, "k2")
                    w2k = p2("w2k").rearrange("p (c n) -> p c n", c=2)
                    w2v = p2("w2v").rearrange("p (c n) -> p c n", c=2)
                    for c in range(2):
                        ins = pe.matmul(bank[0:64, 0:30], w2k[:, c, :], hid[:, 0, c, 0:30], start=(c == 0), stop=(c == 1))
                    banks.close(ins, "k2")
                    bank = banks.open(pe, "v2")
                    for g in range(2):
                        for c in range(2):
                            ins = pe.matmul(bank[0:NCMP, 64 * g:64 * g + 64], hid[:, 1, c, NCMP * g:NCMP * g + NCMP],
                                            w2v[:, c, :], start=(c == 0), stop=(c == 1))
                    banks.close(ins, "v2")

            with nc.Block() as block:
                @block.gpsimd
                def _(pool):
                    pool.memset(PTC, 0.0).then_inc(L["az"], 1)

                @block.vector
                def _(dve):
                    link = Chain(dve, L["avec"])
                    b = banks.take(dve, "sc")
                    bc = b[:, 0:TT * 8 * NCMP].rearrange("p (t h i) -> p t h i", t=TT, h=8)
                    S = Sc[:, :, :, 0:NCMP]
                    for t in range(TT):
                        add = const("cmp_add")[:, 16 * t:16 * t + NCMP].rearrange("p (o i) -> p o i", o=1)\
                            .broadcast_to([P, 8, NCMP])
                        ins = dve.scalar_tensor_tensor(S[:, t], bc[:, t], 64 ** -0.5, add, ALU.mult, ALU.add)
                    banks.give(ins, "sc")
                    banks.wait_drained(dve, "sc")
                    link(dve.tensor_reduce(stc[:, 0], S, AX.X, ALU.max))
                    for t in range(TT):
                        ins = dve.tensor_tensor(S[:, t], S[:, t], bcast(stc[:, 0, t], NCMP), ALU.subtract)
                        ins.then_inc(L["acv"], 1)

                    def compressed():
                        dve.wait_ge(L["acx"], TT)
                        for t in range(TT):
                            mul = const("cmp_mul")[:, 16 * t:16 * t + NCMP].rearrange("p (o i) -> p o i", o=1)\
                                .broadcast_to([P, 8, NCMP])
                            ins = dve.tensor_tensor(S[:, t], S[:, t], mul, ALU.mult)
                        link(ins)
                        link(dve.tensor_reduce(stc[:, 1], S, AX.X, ALU.add))
                        link(dve.tensor_scalar(stc[:, 1], stc[:, 1], 1e-30, None, ALU.max))
                        link(dve.reciprocal(stc[:, 2], stc[:, 1]))
                        link(dve.tensor_tensor(stc[:, 2], stc[:, 2], GA[:, :, :, 0], ALU.mult))
                        for t in range(TT):
                            dve.tensor_tensor(S[:, t], S[:, t], bcast(stc[:, 2, t], NCMP), ALU.mult).then_inc(L["acp"], 1)

                    for t in range(TT):
                        w = P * (t + 1)
                        attention_vector_scores(
                            dve, SA0, SA1, 12, lambda c: (64 if c < 8 else 96) ** -0.5,
                            lambda t, c: const("mask1")[:, P * (1 - t):T].rearrange("p (o s) -> p o s", o=1)
                            .broadcast_to([P, 2, P * (t + 1)]), "s2", t)
                        dve.tensor_reduce(NM2[:, t, :], (SA0, SA1)[t], AX.X, ALU.max, negate=True)\
                            .then_inc(L["amx"], 1)
                    compressed()
                    for t in range(TT):
                        S2 = (SA0, SA1)[t]
                        dve.wait_ge(L["aden"], 24 * (t + 1))
                        link(dve.reciprocal(RC2[:, t, :], DEN2[:, t, :]))
                        dve.tensor_tensor(RC2[:, t, 0:8], RC2[:, t, 0:8], GA[:, t, :, 1], ALU.mult)
                        link(dve.tensor_tensor(RC2[:, t, 8:16], RC2[:, t, 8:16], GA[:, t, :, 2], ALU.mult))
                        dve.tensor_tensor(S2, S2, bcast(RC2[:, t, :], P * (t + 1)), ALU.mult).then_inc(L["ap"], 1)

                @block.scalar
                def _(act):
                    act.wait_ge(L["acv"], TT)
                    for t in range(TT):
                        act.activation(Sc[:, t, :, 0:NCMP], Sc[:, t, :, 0:NCMP], ACT.Exp).then_inc(L["acx"], 1)
                    for t in range(TT):
                        S2 = (SA0, SA1)[t]
                        act.wait_ge(L["amx"], t + 1)
                        for hd in range(24):
                            act.activation(S2[:, hd, :], S2[:, hd, :], ACT.Exp, bias=NM2[:, t, hd:hd + 1],
                                           accum_out=DEN2[:, t, hd:hd + 1]).then_inc(L["aden"], 1)
                    act.wait_ge(L["az"], 1)

                    def output(c):
                        b = banks.take(act, ("o2", c))
                        banks.give(act.activation(aT[:, c, :], b[:, 0:T], ACT.Copy), ("o2", c))

                    for c, (tc, heads) in enumerate(pair_jobs):
                        for job in tc:
                            b = banks.take(act, job)
                            banks.give(act.activation(PTC[0:NCMP, 2 * c:2 * c + 2, :], two(b[0:NCMP, :]), ACT.Copy), job)
                        for hd in heads:
                            b = banks.take(act, ("t2", hd))
                            banks.give(act.activation(PTR[:, slot[hd], :], b[:, 0:384], ACT.Copy), ("t2", hd))
                        if c:
                            output(c - 1)
                    output(7)

                @block.tensor
                def _(pe):
                    bank = banks.open(pe, "sc")
                    for t in range(TT):
                        for c in range(4):
                            a = (t * 8 + 2 * c) * NCMP
                            ins = pe.matmul(bank[:, a:a + 2 * NCMP], qA[:, c, t * P:(t + 1) * P],
                                            KZC[:, c // 2, :, 0:NCMP], start=True, stop=True)
                    banks.close(ins, "sc")
                    pairs = [((qA[:, c % 4, :],), (KZ2[:, c // 4, (c % 4) // 2],)) for c in range(8)]
                    pairs += [((qM[:, 2 * c, :], qM[:, 2 * c + 1, :]), (KM[:, 2 * c, :], KM[:, 2 * c + 1, :]))
                              for c in range(4)]
                    attention_tensor_scores(pe, pairs, "s2")
                    pe.wait_ge(L["acp"], TT)
                    pe.wait_ge(L["ap"], TT)
                    for c, (tc, heads) in enumerate(pair_jobs):
                        for job in tc:
                            bank = banks.open(pe, job)
                            for j in range(2):
                                for t in range(TT):
                                    a = (2 * j + t) * P
                                    ins = pe.transpose(bank[0:NCMP, a:a + P], Sc[:, t, 2 * c + j, 0:NCMP], const("ident"))
                            banks.close(ins, job)
                        for hd in heads:
                            attention_tensor_transposes(pe, SA0, SA1, hd, "t2")
                        for hd in heads:
                            banks.wait_drained(pe, ("t2", hd))
                        bank = banks.open(pe, ("o2", c))
                        for j in range(2):
                            rows = slice(64 * j, 64 * j + 64)
                            own = [hd for hd in heads if hd % 2 == j]
                            if c < 4:
                                banks.wait_drained(pe, ("tc", c))
                                pe.matmul(bank[rows, 0:T], vcmp[:, c // 2, :], PTC[:, 2 * c + j, :],
                                          start=True, stop=False)
                            for n, hd in enumerate(own):
                                if c < 4:
                                    col = P * (hd // 8) + 64 * (c // 2)
                                    v = V2[:, :, col:col + 64]
                                else:
                                    v = Vm[:, :, 64 * (hd - 16):64 * (hd - 15)]
                                pe.matmul(bank[rows, 0:T], v[:, 0, :], PTR[:, slot[hd], 0:T],
                                          start=(c >= 4), stop=False)
                                ins = pe.matmul(bank[rows, P:T], v[:, 1, :], PTR[:, slot[hd], T:384],
                                                start=False, stop=(n == len(own) - 1))
                        banks.close(ins, ("o2", c))

            with nc.Block() as block:
                @block.sync
                def _(sp):
                    while ring.issued < LAYER_UNITS:
                        ring.load(sp, w2[layer, ring.issued, :, :])

                @block.scalar
                def _(act):
                    act.activation(sqo, aT, ACT.Square).then_inc(L["fsq"], 1)
                    for k in range(2):
                        b = banks.take(act, f"mo{k}")
                        banks.give(root_of_mean(act, b, 512, std[:, T * k:T * k + T]), f"mo{k}")
                    for i in range(4):
                        banks.wait_drained(act, ("wo", i))
                        act.activation(sqo[:, 2 * i:2 * i + 2, :], hT[:, 2 * i:2 * i + 2, :], ACT.Square)\
                           .then_inc(L["fsq2"], 1)
                    b = banks.take(act, "mf")
                    act.wait_ge(L["fmix"], DC)
                    banks.give(root_of_mean(act, b, D, std[:, 0:T]), "mf")
                    for i in range(16):
                        b = banks.take(act, ("f1", i))
                        if i >= 2:
                            act.wait_ge(L["fhid"], i - 1)
                        banks.give(act.activation(relu[:, i % 2], two(b[:, :]), ACT.Relu), ("f1", i))

                @block.vector
                def _(dve):
                    link = Chain(dve, L["fvec"])
                    for k in range(2):
                        banks.wait_drained(dve, f"mo{k}")
                    link(dve.reciprocal(rst[:, :], std[:, :]))
                    for k, n in enumerate(("nsa", "mla")):
                        for c in range(4):
                            dve.scalar_tensor_tensor(mixT[:, 4 * k + c, :], aT[:, 4 * k + c, :], p2(n)[:, c:c + 1],
                                                     rst[:, T * k:T * k + T], ALU.mult, ALU.mult).then_inc(L["fmix"], 1)
                    for i in range(4):
                        b = banks.take(dve, ("wo", i))
                        banks.give(dve.tensor_tensor(hT[:, 2 * i:2 * i + 2, :], hT[:, 2 * i:2 * i + 2, :], two(b[:, :]),
                                                     ALU.add), ("wo", i))
                    banks.wait_drained(dve, "mf")
                    dve.wait_ge(L["fmix"], DC)
                    link(dve.reciprocal(rst[:, 0:T], std[:, 0:T]))
                    for c in range(DC):
                        dve.scalar_tensor_tensor(xnT[:, c, :], hT[:, c, :], p2("mlp")[:, c:c + 1], rst[:, 0:T],
                                                 ALU.mult, ALU.mult).then_inc(L["fxn2"], 1)
                    for i in range(16):
                        banks.wait_drained(dve, ("f1", i))
                        dve.tensor_tensor(hidden[:, 2 * i:2 * i + 2, :], relu[:, i % 2], relu[:, i % 2],
                                          ALU.mult).then_inc(L["fhid"], 1)
                    for b in range(4):
                        bank = banks.take(dve, ("f2", b))
                        banks.give(dve.tensor_tensor(hT[:, 2 * b:2 * b + 2, :], hT[:, 2 * b:2 * b + 2, :], two(bank[:, :]),
                                                     ALU.add), ("f2", b))

                @block.tensor
                def _(pe):
                    for k in range(2):
                        sum_squares(pe, f"mo{k}", sqo[:, 4 * k:4 * k + 4, :], 4, (L["fsq"], 1))
                    pe.wait_ge(L["fmix"], DC)
                    for i in range(4):
                        w = ring.unit(pe).rearrange("p (k n) -> p k n", k=DC)
                        banks.close(linear(pe, ("wo", i), w, mixT, DC, (0, P)), ("wo", i))
                    sum_squares(pe, "mf", sqo, DC, (L["fsq2"], 4))
                    pe.wait_ge(L["fxn2"], DC)
                    for i in range(16):
                        w = ring.unit(pe).rearrange("p (k n) -> p k n", k=DC)
                        banks.close(linear(pe, ("f1", i), w, xnT, DC, (0, P)), ("f1", i))
                    out_banks = [banks.open(pe, ("f2", b)) for b in range(4)]
                    for u in range(FF2_UNITS):
                        w = ring.unit(pe).rearrange("p (k n) -> p k n", k=2)
                        pe.wait_ge(L["fhid"], u + 1)
                        for k in range(2):
                            for c in range(DC):
                                ins = pe.matmul(out_banks[c // 2][:, (c % 2) * T:(c % 2 + 1) * T],
                                                w[:, k, c * P:(c + 1) * P], hidden[:, 2 * u + k, :],
                                                start=(u + k == 0 and c % 2 == 0), stop=(u == FF2_UNITS - 1 and k == 1),
                                                skip_group_check=True)
                                if u == FF2_UNITS - 1 and k == 1 and c % 2:
                                    banks.close(ins, ("f2", c // 2))
                        if u < FF2_UNITS - 1:
                            ins.then_inc(ring.used, 1)

        e_sq, e_ms, e_std, e_rst, e_y, e_out = (sem(n) for n in ("end_sq", "end_ms", "end_std", "end_rst", "end_y", "end_out"))
        with nc.Block() as block:
            @block.scalar
            def _(act):
                act.activation(sqL, hT, ACT.Square).then_inc(e_sq, 1)
                act.wait_ge(e_ms, 1)
                root_of_mean(act, psum[0], D, std[:, 0:T]).then_inc(e_std, 1)

            @block.tensor
            def _(pe):
                pe.wait_ge(e_sq, 1)
                for c in range(DC):
                    ins = pe.matmul(psum[0][:, 0:T], const("ones"), sqL[:, c, :], start=(c == 0), stop=(c == DC - 1))
                ins.then_inc(e_ms, 1)

            @block.vector
            def _(dve):
                dve.wait_ge(e_std, 1)
                dve.reciprocal(rst[:, 0:T], std[:, 0:T]).then_inc(e_rst, 1)
                dve.wait_ge(e_rst, 1)
                for c in range(DC):
                    dve.scalar_tensor_tensor(xnT[:, c, :], hT[:, c, :], par("final")[:, c:c + 1], rst[:, 0:T],
                                             ALU.mult, ALU.mult).then_inc(e_y, 1)

            @block.sync
            def _(sp):
                for half in range(2):
                    sp.wait_ge(e_y, DC // 2 * (half + 1))
                    cols = slice(half * D, (half + 1) * D)
                    sp.dma_start(out[:, cols], xn[:, cols]).then_inc(e_out, 16)
                sp.wait_ge(e_out, 32)


def _blocks(w, k, n):
    rows, cols = w.shape
    return w.reshape(k, P, cols // n, n).transpose(2, 1, 0, 3).reshape(cols // n, P, k * n)


def _tall(v):
    return v.reshape(-1, P).T


def _constants():
    c = np.zeros((P, NCONST), np.float32)

    def put(name, a):
        lo, hi = CONST[name]
        c[:a.shape[0], lo:lo + a.shape[1]] = a

    i = np.arange(P)
    put("ones", np.ones((P, P)))
    put("blk64", (i[:, None] // 64 == i[None, :] // 64).astype(np.float32))
    put("ident", np.eye(P))
    for name, dim, starts in (("rot64", 64, (0, 64)), ("rot32", 32, (64,))):
        r = np.zeros((P, P), np.float32)
        for s in starts:
            for d in range(dim // 2):
                r[s + d + dim // 2, s + d] = -1.0
                r[s + d, s + d + dim // 2] = 1.0
        put(name, r)
    for tag, dim, starts in (("A", 64, (0, 64)), ("B", 32, (64,))):
        inv = (np.float32(1.0) / (np.float32(10000.0) ** (np.arange(0, dim, 2, dtype=np.float32) / np.float32(dim))))
        ang = np.arange(T, dtype=np.float32)[:, None] * inv.astype(np.float32)[None, :]
        ang = np.concatenate([ang, ang], axis=-1).T
        cos, sin = np.ones((P, T), np.float32), np.zeros((P, T), np.float32)
        for s in starts:
            cos[s:s + dim], sin[s:s + dim] = np.cos(ang), np.sin(ang)
        put("cos" + tag, cos)
        put("sin" + tag, sin)
    put("mask1", np.concatenate([np.zeros((P, P)), np.where(i[None, :] <= i[:, None], 0.0, NEG)], axis=1))
    end = np.arange(NCMP) * 16 + 31
    ok = np.stack([end[None, :] <= (i[:, None] + P * t) for t in range(TT)], axis=1)
    wide = np.zeros((P, TT, 16), np.float32)
    wide[:, :, :NCMP] = np.where(ok, 0.0, NEG)
    put("cmp_add", wide.reshape(P, 32).copy())
    wide[:, :, :NCMP] = ok
    put("cmp_mul", wide.reshape(P, 32))
    put("time", np.tile(np.arange(T, dtype=np.float32), (P, 1)))
    put("lane", np.tile(i.astype(np.float32), (P, 1)))
    return c


def _lay(inputs):
    a = {k: np.asarray(v) for k, v in inputs.items()}
    f = np.float32
    out = {}
    out["xT"] = a["x"][0].T.reshape(DC, P, T).transpose(1, 0, 2).reshape(P, DC * T)
    out["consts"] = _constants()

    par = np.zeros((P, NPAR1), f)

    def put(name, v, table=PAR1, dst=None):
        lo, hi = table[name]
        (par if dst is None else dst)[:, lo:lo + v.shape[1]] = v

    put("ln1", _tall(a["ln1_g"][0]))
    put("ln2", _tall(a["ln2_g"][0]))
    put("bgate", _tall(a["b_gate"][0]))
    for name, key in (("lre", "s5_lambda_re"), ("lim", "s5_lambda_im")):
        put(name, a[key][0].reshape(SC, P).T)
    put("lstep", np.repeat(a["s5_log_step"][0].reshape(SC, 2), 64, axis=1).T)
    put("dskip", _tall(a["s5_d"][0].reshape(-1)))
    put("gq", np.tile(a["q_norm_g"][0], 2)[:, None])
    put("gk", np.tile(a["k_norm_g"][0], 2)[:, None])
    put("sinks", np.tile(a["attn_sinks"][0], (P, 1)))
    put("final", _tall(a["final_norm_2"]))
    cs = np.stack([a["s5_c_re"][0], a["s5_c_im"][0]], axis=1)
    cs = cs.reshape(SC, 2, 2, 16, 64).transpose(1, 4, 0, 2, 3).reshape(P, SC * 32)
    put("cs5", cs)
    out["par1"] = par

    dist = np.arange(P)[:, None] + P - np.arange(2 * P)[None, :]
    d = np.maximum(dist, 0)
    d_f = np.maximum(d, 1).astype(f)
    large = 16 + (np.log(d_f / f(16)) / f(np.log(8.0)) * f(16)).astype(np.int32)
    bucket = np.where(d < 16, d, np.minimum(large, 31))
    table = a["rel_bias_table"][bucket].transpose(0, 2, 1)
    ok = (dist >= 0) & (dist < 128)
    out["bias1"] = np.where(ok[:, None, :], table, f(NEG)).reshape(P, NH * T)

    bs = np.zeros((UC, 4, 2, P, P), f)
    for k, key in enumerate(("s5_b_re", "s5_b_im")):
        b = a[key][0]
        for g in range(G1):
            sc, half = g // 2, g % 2
            uc, q = sc // 4, sc % 4
            r0 = 32 * q + 16 * half
            bs[uc, q, k, r0:r0 + 16, 64 * half:64 * half + 64] = b[g].T
    bs = bs.transpose(3, 0, 1, 2, 4).reshape(P, 2, SLOT).transpose(1, 0, 2)
    glu = _blocks(a["s5_w_glu"][0], 4, 512)
    out["w1"] = np.concatenate([
        _blocks(a["w_in"][0], DC, 256), bs, glu[::-1], _blocks(a["w_attn_branch"][0], DC, 256),
        _blocks(a["w_s5_branch"][0], 4, 512), _blocks(a["w_out"][0], DC, 256),
        _blocks(a["peer_w_query"][0], DC, 256)])
    sk = a["peer_sub_keys"][0]
    keys = np.zeros((2, 64, PH, 2, NSUB), f)
    for k in range(2):
        keys[k, :, :, k, :] = sk[:, k].transpose(2, 0, 1)
    out["keys"] = keys.reshape(P, PH * T)
    u = a["peer_u"][0].reshape(NSUB, NE2 // 2, 2, DC, P)
    out["wu"] = np.ascontiguousarray(u.transpose(1, 4, 2, 3, 0)).reshape(NE2 // 2, P, SLOT)
    v = a["peer_v"][0].reshape(NSUB, NE2 // 2, SLOT)
    out["wv"] = np.ascontiguousarray(v.transpose(1, 0, 2))
    _lay_layers(a, out)
    return {k: np.ascontiguousarray(v, dtype=v.dtype) for k, v in out.items()}


def _lay_layers(a, out):
    f = np.float32
    pars, units = [], []
    for l in range(LAYERS):
        par = np.zeros((P, NPAR2), f)

        def put(name, v):
            lo, hi = PAR2[name]
            par[:, lo:lo + v.shape[1]] = v

        for name, key in (("attn", "attn_norm_2"), ("mlp", "mlp_norm_2"), ("qn", "mla_q_norm_2"),
                          ("kvn", "mla_kv_norm_2"), ("nsa", "nsa_out_norm_2"), ("mla", "mla_out_norm_2")):
            put(name, _tall(a[key][l]))
        for name, key in (("posk", "cmp_pos_k_2"), ("posv", "cmp_pos_v_2")):
            put(name, a[key][l].reshape(16, P).T)
        for name, key in (("w2k", "cmp_w2_k_2"), ("w2v", "cmp_w2_v_2")):
            put(name, a[key][l].reshape(2, P, 64).transpose(1, 0, 2).reshape(P, 128))
        w = a["w_in_2"][l]
        q, kc, vc, ks, vs, kw, vw, g, cq, ckv, kr = np.split(w, np.cumsum([512] + [128] * 6 + [24, 256, 128]), axis=1)
        put("wg", g.reshape(DC, P, 24).transpose(1, 0, 2).reshape(P, DC * 24))
        krp = np.zeros((D, P), f)
        krp[:, 64:96] = kr
        w_in = np.concatenate([q, kc, vc, ks, kw, cq, ckv, krp, vs, vw], axis=1)
        wq = np.zeros((256, 8, P), f)
        wq[:, :, :96] = a["w_q_up_2"][l].reshape(256, 8, 96)
        wkv = a["w_kv_up_2"][l].reshape(P, 8, P)
        up = np.zeros((1, P, SLOT), f)
        up[0, :, 0:1024].reshape(P, 8, P)[:, :, :64] = wkv[:, :, :64]
        up[0, :, 1024:1536] = wkv[:, :, 64:].reshape(P, 512)
        tall = [a[k][l].reshape(-1, SLOT // a[k].shape[2], P, a[k].shape[2]).transpose(0, 2, 1, 3).reshape(-1, P, SLOT)
                for k in ("cmp_w1_k_2", "cmp_w1_v_2", "w_ff2_2")]
        units.append(np.concatenate([
            _blocks(w_in, DC, 256), _blocks(wq.reshape(256, 1024), 2, 1024), up, tall[0], tall[1],
            _blocks(a["w_out_2"][l], DC, 256), _blocks(a["w_ff1_2"][l], DC, 256), tall[2]]))
        pars.append(par)
    out["par2"] = np.stack(pars)
    out["w2"] = np.stack(units)


_INS = ["xT", "consts", "par1", "bias1", "w1", "keys", "wu", "wv", "par2", "w2"]


def kernel(**inputs):
    import concourse.bacc as _bacc
    from concourse.bass_utils import run_bass_kernel_spmd as _run

    arrays = _lay(inputs)
    nc = _bacc.Bacc("TRN2", target_bir_lowering=False, num_devices=1)
    args = [nc.dram_tensor(n, arrays[n].shape, mybir.dt.from_np(arrays[n].dtype), kind="ExternalInput").ap() for n in _INS]
    out = nc.dram_tensor("yT", (P, DC * T), F32, kind="ExternalOutput").ap()
    build(nc, None, *args, out)
    r = _run(nc, [{n: arrays[n] for n in _INS}], core_ids=[0])
    y = np.asarray(r.results[0]["yT"]).reshape(P, DC, T).transpose(2, 1, 0).reshape(1, T, D)
    return y
```

```python
import numpy as np
import concourse.bass as bass
from concourse import mybir
from contextlib import ExitStack

F32 = mybir.dt.float32
U32 = mybir.dt.uint32
F32R = mybir.dt.float32r
ALU = mybir.AluOpType
ACT = mybir.ActivationFunctionType
AX = mybir.AxisListType

P = 128
T = 256
TT = T // P
D = 1024
DC = D // P
EPS = 1e-6
NEG = -1e30

SLOTS = 4
SLOT = 1024

G1 = 32
SC = 16
UC = 4

NH, NKV, HD = 16, 4, 64

PH, TOPK, NSUB = 8, 16, 128
NE2 = NSUB

LAYERS = 2
NCMP = 15
FF = 4096
FC = FF // P
IN2_UNITS, UP_UNITS, CMP_UNITS, OUT_UNITS, FF1_UNITS, FF2_UNITS = 14, 4, 8, 8, 32, 32
LAYER_UNITS = IN2_UNITS + UP_UNITS + CMP_UNITS + OUT_UNITS + FF1_UNITS + FF2_UNITS

CONST = {}
_at = 0
for _name, _n in [("ones", 128), ("blk64", 128), ("ident", 128), ("time", 256), ("lane", 128), ("rot64", 128),
                  ("rot32", 128), ("cosA", 256), ("sinA", 256), ("cosB", 256), ("sinB", 256),
                  ("mask1", 256), ("cmp_add", 32), ("cmp_mul", 32)]:
    CONST[_name] = (_at, _at + _n)
    _at += _n
NCONST = _at
NEARLY = CONST["rot64"][0]
ARENA = 32768

PAR1 = {}
_at = 0
for _name, _n in [("ln1", 8), ("ln2", 8), ("bgate", 16), ("lre", SC), ("lim", SC), ("lstep", SC),
                  ("dskip", UC), ("gq", 1), ("gk", 1), ("sinks", NH), ("final", 8), ("cs5", SC * 2 * 16)]:
    PAR1[_name] = (_at, _at + _n)
    _at += _n
NPAR1 = _at

PAR2 = {}
_at = 0
for _name, _n in [("attn", 8), ("mlp", 8), ("qn", 2), ("kvn", 1), ("nsa", 4), ("mla", 4), ("posk", 16),
                  ("posv", 16), ("w2k", 128), ("w2v", 128), ("wg", DC * 24)]:
    PAR2[_name] = (_at, _at + _n)
    _at += _n
NPAR2 = _at


class Banks:

    def __init__(self, full, drained, tensors):
        self.full, self.drained, self.tensors = full, drained, tensors
        self.reset()

    def reset(self):
        self.turn, self.done, self.jobs = 0, [0] * 8, {}

    def plan(self, names):
        for n in names:
            b = self.turn % 8
            self.turn += 1
            self.jobs[n] = (b, self.done[b])
            self.done[b] += 1

    def open(self, pe, name):
        b, before = self.jobs[name]
        if before:
            pe.wait_ge(self.drained[b], before)
        return self.tensors[b]

    def close(self, ins, name):
        ins.then_inc(self.full[self.jobs[name][0]], 1)

    def take(self, eng, name):
        b, before = self.jobs[name]
        eng.wait_ge(self.full[b], before + 1)
        return self.tensors[b]

    def give(self, ins, name):
        ins.then_inc(self.drained[self.jobs[name][0]], 1)

    def wait_drained(self, eng, name):
        b, before = self.jobs[name]
        eng.wait_ge(self.drained[b], before + 1)


class Ring:

    def __init__(self, loaded, used, rounded, rest, slots, hi, lo):
        self.loaded, self.used, self.rounded, self.rest = loaded, used, rounded, rest
        self.slots, self.hi, self.lo = slots, hi, lo
        self.reset()

    def reset(self):
        self.issued = self.taken = self.marks = 0
        self.last, self.number, self.order, self.unit_of = [], [], [], {}
        self.at = {"act": 0, "pool": 0}

    def plan(self, banks, jobs, split=False):
        for j in jobs:
            if j is None:
                self.marks += 1
                self.last.append((self.used, self.marks))
            elif not isinstance(j, str) and not isinstance(j[0], str):
                self.last.append(j)
            else:
                b, before = banks.jobs[j]
                self.unit_of[j] = len(self.last)
                self.last.append((banks.full[b], before + 1))
            self.number.append(len(self.order) if split else None)
            if split:
                self.order.append(len(self.last) - 1)

    def load(self, sp, source):
        u, s = self.issued, self.issued % SLOTS
        if u >= SLOTS:
            n = self.number[u - SLOTS]
            if n is None:
                sp.wait_ge(*self.last[u - SLOTS])
            else:
                sp.wait_ge(self.rest, n + 1)
        sp.dma_start(self.slots[:, s, :], source).then_inc(self.loaded[s], 16)
        self.issued += 1

    def round(self, act, count):
        for n in range(self.at["act"], min(self.at["act"] + count, len(self.order))):
            u = self.order[n]
            act.wait_ge(self.loaded[u % SLOTS], 16 * (u // SLOTS + 1))
            if n >= 2:
                act.wait_ge(*self.last[self.order[n - 2]])
            act.activation(self.hi[:, n % 2, :], self.slots[:, u % SLOTS, :], ACT.Copy).then_inc(self.rounded, 1)
            self.at["act"] = n + 1

    def feed(self, act, job):
        upto = self.unit_of[job] + 2
        self.round(act, sum(1 for u in self.order[self.at["act"]:] if u <= upto))

    def subtract(self, pool, count=None):
        end = len(self.order) if count is None else self.at["pool"] + count
        for n in range(self.at["pool"], end):
            pool.wait_ge(self.rounded, n + 1)
            if n >= 2:
                pool.wait_ge(*self.last[self.order[n - 2]])
            pool.tensor_tensor(self.lo[:, n % 2, :], self.slots[:, self.order[n] % SLOTS, :],
                               self.hi[:, n % 2, :].bitcast(F32), ALU.subtract).then_inc(self.rest, 1)
        self.at["pool"] = end

    def unit(self, pe):
        u, s = self.taken, self.taken % SLOTS
        pe.wait_ge(self.loaded[s], 16 * (u // SLOTS + 1))
        self.taken += 1
        return self.slots[:, s, :]

    def high(self, pe):
        n = self.number[self.taken]
        pe.wait_ge(self.rounded, n + 1)
        return self.hi[:, n % 2, :]

    def low(self, pe):
        n = self.number[self.taken]
        self.taken += 1
        pe.wait_ge(self.rest, n + 1)
        return self.lo[:, n % 2, :]


class Parts:

    def __init__(self, hi, lo_pool, lo_dve, high, low):
        self.sem_hi, self.sem_pool, self.sem_dve, self.high, self.low = hi, lo_pool, lo_dve, high, low
        self.reset()

    def reset(self):
        self.turn = {"act": 0, "pool": 0, "dve": 0, "pe": 0}

    def round(self, act, source, ready, before, chunks=1):
        for c in range(0, DC, chunks):
            act.wait_ge(ready, before + c // chunks + 1)
            act.activation(self.high[:, c:c + chunks, :], source[:, c:c + chunks, :], ACT.Copy)\
               .then_inc(self.sem_hi, chunks)
        self.turn["act"] += 1

    def subtract(self, eng, who, source):
        sem = self.sem_pool if who == "pool" else self.sem_dve
        for c in range(0, DC // 2) if who == "pool" else range(DC // 2, DC):
            eng.wait_ge(self.sem_hi, DC * self.turn[who] + 2 * (c // 2) + 2)
            eng.tensor_tensor(self.low[:, c, :], source[:, c, :], self.high[:, c, :].bitcast(F32), ALU.subtract)\
               .then_inc(sem, 1)
        self.turn[who] += 1

    def wait(self, pe):
        self.turn["pe"] += 1
        pe.wait_ge(self.sem_hi, DC * self.turn["pe"])
        pe.wait_ge(self.sem_pool, DC // 2 * self.turn["pe"])
        pe.wait_ge(self.sem_dve, DC // 2 * self.turn["pe"])


class Chain:

    def __init__(self, eng, sem, start=0):
        self.eng, self.sem, self.n = eng, sem, start

    def __call__(self, ins):
        self.n += 1
        ins.then_inc(self.sem, 1)
        self.eng.wait_ge(self.sem, self.n)


def build(nc, stop_after, xT, consts, par1, bias1, w1, keys, wu, wv, par2, w2, out):
    ctx = ExitStack()
    with ctx:
        def sb(name, cols, dt=F32):
            return ctx.enter_context(nc.sbuf_tensor(name, [P, cols], dt))

        def sem(name):
            return ctx.enter_context(nc.semaphore(name))

        h = sb("h", DC * T)
        slots = sb("slots", SLOTS * SLOT)
        cst = sb("cst", NEARLY)
        p1 = sb("p1", NPAR1)
        small = sb("small", 2304)
        xh, xl = sb("xh", DC * T, F32R), sb("xl", DC * T, F32R)
        wh, wl = sb("wh", 2 * SLOT, F32R), sb("wl", 2 * SLOT, F32R)
        eps, std, rst = sb("eps", 4), sb("std", 512), sb("rst", 512)
        memory = ctx.enter_context(ExitStack())
        arena = memory.enter_context(nc.sbuf_tensor("arena", [P, ARENA], F32))
        xhT, xlT = (x[:, :].rearrange("p (c t) -> p c t", t=T) for x in (xh, xl))
        whv, wlv = (x[:, :].rearrange("p (b n) -> p b n", b=2) for x in (wh, wl))

        hT = h[:, :].rearrange("p (c t) -> p c t", t=T)
        slots_v = slots[:, :].rearrange("p (s n) -> p s n", s=SLOTS)

        def const(name):
            a, b = CONST[name]
            return cst[:, a:b] if b <= NEARLY else late_cst[:, a - NEARLY:b - NEARLY]

        def par(name, table=PAR1):
            a, b = table[name]
            return (p1 if table is PAR1 else small)[:, a:b]

        ps = ctx.enter_context(nc.psum_tensor("ps", [P, 8 * 512], F32))
        psum = [ps[:, 512 * b:512 * b + 512] for b in range(8)]
        banks = Banks([sem(f"full{b}") for b in range(8)], [sem(f"drained{b}") for b in range(8)], psum)
        ring = Ring([sem(f"loaded{s}") for s in range(SLOTS)], sem("used"), sem("rounded"), sem("rest"),
                    slots_v, whv, wlv)
        parts = Parts(sem("parts_hi"), sem("parts_lo_pool"), sem("parts_lo_dve"), xhT, xlT)

        def part(a, b):
            return arena[:, a:b]

        def view(at, *dims):
            v = part(at, at + int(np.prod(dims)))
            if len(dims) == 2:
                return v.rearrange("p (a b) -> p a b", b=dims[1])
            if len(dims) == 3:
                return v.rearrange("p (a b c) -> p a b c", b=dims[1], c=dims[2])
            return v

        def two(ap, w=T):
            return ap.rearrange("p (a b) -> p a b", b=w)

        def sum_squares(pe, name, squares, chunks, ready=None, matrix="ones"):
            bank = banks.open(pe, name)
            if ready:
                pe.wait_ge(*ready)
            for c in range(chunks):
                ins = pe.matmul(bank[:, 0:T], const(matrix), squares[:, c, :],
                                start=(c == 0), stop=(c == chunks - 1))
            banks.close(ins, name)

        def linear(pe, name):
            bank = banks.open(pe, name)
            for j in range(2):
                out = bank[:, j * T:(j + 1) * T]
                w = ring.high(pe).rearrange("p (k n) -> p k n", k=DC)
                for k in range(DC):
                    pe.matmul(out, w[:, k, :], xhT[:, k, :], start=(k == 0), stop=False)
                    pe.matmul(out, w[:, k, :], xlT[:, k, :], start=False, stop=False)
                w = ring.low(pe).rearrange("p (k n) -> p k n", k=DC)
                for k in range(DC):
                    ins = pe.matmul(out, w[:, k, :], xhT[:, k, :], start=False, stop=(k == DC - 1))
                if j == 0:
                    ins.then_inc(ring.used, 1)
            banks.close(ins, name)

        def linear_part(pe, name, weights, source, cols):
            kc = weights.shape[1]
            bank = banks.open(pe, name)
            for j, c0 in enumerate(cols):
                for k in range(kc):
                    ins = pe.matmul(bank[:, j * T:(j + 1) * T], weights[:, k, c0:c0 + P], source[:, k, :],
                                    start=(k == 0), stop=(k == kc - 1))
            banks.close(ins, name)

        def values(pe, name, source):
            bank = banks.open(pe, name)
            for j in range(2):
                w = ring.unit(pe).rearrange("p (k n) -> p k n", k=DC)
                for t in range(TT):
                    for k in range(DC):
                        ins = pe.matmul(bank[:, t * T + j * P:t * T + (j + 1) * P], source[:, k, t * P:(t + 1) * P],
                                        w[:, k, :], start=(k == 0), stop=(k == DC - 1))
                if j == 0:
                    ins.then_inc(ring.used, 1)
            banks.close(ins, name)

        def pairs_of(names):
            return [x for n in names for x in (None, n)]

        def root_of_mean(eng, bank, n, std, width=T):
            return eng.activation(std, bank[:, 0:width], ACT.Sqrt, bias=eps[:, 0:1], scale=1.0 / n)


        gates = view(0, 16, T)
        uT = view(4096, UC, T)
        mix = view(5120, 8, T)
        V1 = view(9216, TT, T)
        qT = view(9728, 8, T)
        KZ = view(11776, 4, 2 * T)
        qraw = view(13824, 10, T)
        qsq = view(16384, 10, T)
        kn = view(18944, 2, T)
        sq = view(19456, 8, T)
        bias_v = view(22016, NH, T)
        xnT = view(26112, 8, T)

        loaded_x, loaded_c, loaded_b = sem("loaded_x"), sem("loaded_c"), sem("loaded_b")
        s_sq, s_std, s_xn, s_zero, s_qsq, s_gates, s_dve, s_kz = (
            sem(n) for n in ("sq1", "std1", "xn1", "zero", "qsq", "gates", "dve1", "kz"))

        banks.plan(["ms"] + [("u", i) for i in range(2)] + [("q", i) for i in range(4)] + ["k", "v"]
                   + [("qn", i) for i in range(5)] + [("g", i) for i in range(8)])

        ring.plan(banks, pairs_of([("u", 0), ("u", 1), ("q", 0), ("q", 1), ("q", 2), ("q", 3), "k"]), True)
        ring.plan(banks, pairs_of(["v"]))
        ring.plan(banks, pairs_of([("g", i) for i in range(8)]), True)

        with nc.Block() as block:
            @block.sync
            def _(sp):
                sp.dma_start(h[:, :], xT).then_inc(loaded_x, 16)
                sp.dma_start(cst[:, :], consts[:, 0:NEARLY]).then_inc(loaded_c, 16)
                sp.dma_start(p1[:, :], par1).then_inc(loaded_c, 16)
                for u in range(32 + SLOTS):
                    ring.load(sp, w1[u, :, :])
                sp.dma_start(bias_v, bias1.rearrange("p (a b) -> p a b", b=T)).then_inc(loaded_b, 16)
                sp.wait_ge(loaded_b, 16)

            @block.gpsimd
            def _(pool):
                pool.memset(eps[:, 0:1], EPS).then_inc(s_zero, 1)
                pool.memset(eps[:, 1:2], 0.0).then_inc(s_zero, 1)
                pool.memset(KZ, 0.0).then_inc(s_zero, 1)
                ring.subtract(pool, 2)
                parts.subtract(pool, "pool", xnT)
                ring.subtract(pool)

            @block.scalar
            def _(act):
                act.wait_ge(loaded_x, 16)
                act.activation(sq, hT, ACT.Square).then_inc(s_sq, 1)
                ring.round(act, 2)
                act.wait_ge(s_zero, 2)
                b = banks.take(act, "ms")
                act.wait_ge(loaded_c, 32)
                ins = root_of_mean(act, b, D, std[:, 0:T])
                banks.give(ins, "ms")
                parts.round(act, xnT, s_xn, 0)
                for i in range(4):
                    ring.feed(act, ("q", i))
                    b = banks.take(act, ("q", i))
                    act.activation(qsq[:, 2 * i:2 * i + 2, :], two(b[:, :]), ACT.Square).then_inc(s_qsq, 1)
                    banks.give(act.activation(qraw[:, 2 * i:2 * i + 2, :], two(b[:, :]), ACT.Copy), ("q", i))
                ring.feed(act, "k")
                b = banks.take(act, "k")
                act.activation(qsq[:, 8:10, :], two(b[:, :]), ACT.Square).then_inc(s_qsq, 1)
                banks.give(act.activation(qraw[:, 8:10, :], two(b[:, :]), ACT.Copy), "k")
                for i in range(5):
                    b = banks.take(act, ("qn", i))
                    if i:
                        act.wait_ge(s_kz, i)
                    else:
                        act.wait_ge(s_dve, 1)
                    banks.give(root_of_mean(act, b, HD, std[:, :], 512), ("qn", i))
                for i in range(8):
                    ring.feed(act, ("g", i))
                    b = banks.take(act, ("g", i))
                    for j in range(2):
                        ins = act.activation(gates[:, 2 * i + j, :], b[:, j * T:(j + 1) * T], ACT.Sigmoid,
                                             bias=par("bgate")[:, 2 * i + j:2 * i + j + 1])
                    banks.give(ins, ("g", i))

            @block.vector
            def _(dve):
                link = Chain(dve, s_dve)
                banks.wait_drained(dve, "ms")
                link(dve.reciprocal(rst[:, 0:T], std[:, 0:T]))
                for c in range(DC):
                    dve.scalar_tensor_tensor(xnT[:, c, :], hT[:, c, :], par("ln1")[:, c:c + 1], rst[:, 0:T],
                                             ALU.mult, ALU.mult).then_inc(s_xn, 1)
                parts.subtract(dve, "dve", xnT)
                for i in range(2):
                    b = banks.take(dve, ("u", i))
                    banks.give(dve.tensor_copy(uT[:, 2 * i:2 * i + 2, :], two(b[:, :])), ("u", i))
                b = banks.take(dve, "v")
                banks.give(dve.tensor_copy(V1, two(b[:, :])), "v")
                for i in range(5):
                    banks.wait_drained(dve, ("qn", i))
                    dve.reciprocal(rst[:, :], std[:, :]).then_inc(s_kz, 1)
                    dve.wait_ge(s_kz, i + 1)
                    dst = qT[:, 2 * i:2 * i + 2, :] if i < 4 else kn
                    link(dve.scalar_tensor_tensor(dst, qraw[:, 2 * i:2 * i + 2, :], par("gq" if i < 4 else "gk"),
                                                  two(rst[:, :]), ALU.mult, ALU.mult))
                dve.wait_ge(s_zero, 3)
                for kv in range(NKV):
                    src = kn[64 * (kv % 2):64 * (kv % 2) + 64, kv // 2, :]
                    for v in range(2):
                        dve.tensor_copy(KZ[64 * v:64 * v + 64, kv, v * T:(v + 1) * T], src)

            @block.tensor
            def _(pe):
                pe.wait_ge(loaded_c, 32)
                sum_squares(pe, "ms", sq, DC, (s_sq, 1))
                parts.wait(pe)
                for i in range(16):
                    name = (("u", i) if i < 2 else ("q", i - 2) if i < 6 else "k" if i == 6
                            else "v" if i == 7 else ("g", i - 8))
                    if i == 7:
                        values(pe, name, xnT)
                    else:
                        linear(pe, name)
                    if i == 7:
                        for n in range(5):
                            b = banks.open(pe, ("qn", n))
                            pe.wait_ge(s_qsq, n + 1)
                            banks.close(pe.matmul(b[:, :], const("blk64"), qsq[:, 2 * n:2 * n + 2, :],
                                                  start=True, stop=True), ("qn", n))

        def attention_tensor_scores(pe, pairs, name):
            for t in range(TT):
                for c, (queries, keys) in enumerate(pairs):
                    bank = banks.open(pe, (name, t, c))
                    w = P * (t + 1)
                    if len(keys) == 1:
                        ins = pe.matmul(bank[:, 0:2 * w], queries[0][:, t * P:(t + 1) * P], keys[0][:, :, 0:w],
                                        start=True, stop=True)
                    else:
                        for j in range(2):
                            ins = pe.matmul(bank[:, j * w:(j + 1) * w], queries[j][:, t * P:(t + 1) * P],
                                            keys[j][:, 0:w], start=True, stop=True)
                    banks.close(ins, (name, t, c))

        def attention_tensor_transposes(pe, S0, S1, head, name):
            bank = banks.open(pe, (name, head))
            pe.transpose(bank[:, 0:128], S0[:, head, :], const("ident"))
            pe.transpose(bank[:, 128:256], S1[:, head, 0:P], const("ident"))
            banks.close(pe.transpose(bank[:, 256:384], S1[:, head, P:T], const("ident")), (name, head))

        def attention_vector_scores(dve, S0, S1, npairs, scales, biases, name, t):
            S = (S0, S1)[t]
            w = P * (t + 1)
            for c in range(npairs):
                b = banks.take(dve, (name, t, c))
                banks.give(dve.scalar_tensor_tensor(S[:, 2 * c:2 * c + 2, :], two(b[:, 0:2 * w], w), scales(c),
                                                    biases(t, c), ALU.mult, ALU.add), (name, t, c))
            banks.wait_drained(dve, (name, t, npairs - 1))

        def bcast(ap, n):
            return ap.rearrange("p (a o) -> p a o", o=1).broadcast_to([P, ap.shape[1], n])

        S0 = view(13824, NH, P)
        S1 = view(26112, NH, T)
        PT = view(15872, NH, 384)
        st = arena[:, 30720:30720 + 6 * TT * NH].rearrange("p (k t n) -> p k t n", k=6, t=TT)
        MX, NM, DEN, ES, RC, _SP = (st[:, i] for i in range(6))
        s_mx, s_den, s_es, s_p, s_dve2, s_o = (sem(n) for n in ("mx2", "den2", "es2", "p2", "dve2", "out_hi2"))
        banks.plan([("s", t, c) for t in range(TT) for c in range(8)])
        for c in range(8):
            banks.plan([("t", 2 * c), ("t", 2 * c + 1), ("o", c)])

        with nc.Block() as block:
            @block.vector
            def _(dve):
                link = Chain(dve, s_dve2)
                for t in range(TT):
                    S = (S0, S1)[t]
                    attention_vector_scores(
                        dve, S0, S1, 8, lambda c: HD ** -0.5,
                        lambda t, c: bias_v[:, 2 * c:2 * c + 2, P * (1 - t):T], "s", t)
                    link(dve.tensor_reduce(MX[:, t, :], S, AX.X, ALU.max))
                    link(dve.tensor_tensor(MX[:, t, :], MX[:, t, :], par("sinks"), ALU.max))
                    dve.tensor_scalar(NM[:, t, :], MX[:, t, :], -1.0, None, ALU.mult).then_inc(s_mx, 1)
                    dve.wait_ge(s_mx, 2 * t + 1)
                    dve.tensor_tensor(ES[:, t, :], NM[:, t, :], par("sinks"), ALU.add).then_inc(s_mx, 1)
                for t in range(TT):
                    S = (S0, S1)[t]
                    dve.wait_ge(s_es, t + 1)
                    link(dve.tensor_tensor(DEN[:, t, :], DEN[:, t, :], ES[:, t, :], ALU.add))
                    link(dve.reciprocal(RC[:, t, :], DEN[:, t, :]))
                    dve.tensor_tensor(S, S, bcast(RC[:, t, :], P * (t + 1)), ALU.mult).then_inc(s_p, 1)
                for c in range(8):
                    b = banks.take(dve, ("o", c))
                    dve.wait_ge(s_o, c + 1)
                    banks.give(dve.tensor_tensor(xlT[:, c, :], b[:, 0:T], xhT[:, c, :].bitcast(F32), ALU.subtract),
                               ("o", c))

            @block.scalar
            def _(act):
                for t in range(TT):
                    S = (S0, S1)[t]
                    act.wait_ge(s_mx, 2 * t + 2)
                    for hd in range(NH):
                        act.activation(S[:, hd, :], S[:, hd, :], ACT.Exp, bias=NM[:, t, hd:hd + 1],
                                       accum_out=DEN[:, t, hd:hd + 1]).then_inc(s_den, 1)
                    act.wait_ge(s_den, NH * (t + 1))
                    act.activation(ES[:, t, :], ES[:, t, :], ACT.Exp).then_inc(s_es, 1)
                for c in range(8):
                    for j in range(2):
                        b = banks.take(act, ("t", 2 * c + j))
                        banks.give(act.activation(PT[:, 2 * c + j, :], b[:, 0:384], ACT.Copy), ("t", 2 * c + j))
                    if c:
                        b = banks.take(act, ("o", c - 1))
                        act.activation(xhT[:, c - 1, :], b[:, 0:T], ACT.Copy).then_inc(s_o, 1)
                b = banks.take(act, ("o", 7))
                act.activation(xhT[:, 7, :], b[:, 0:T], ACT.Copy).then_inc(s_o, 1)

            @block.tensor
            def _(pe):
                attention_tensor_scores(
                    pe, [((qT[:, c, :],), (KZ[:, c // 2, :].rearrange("p (v t) -> p v t", v=2),)) for c in range(8)], "s")
                pe.wait_ge(s_p, TT)
                for c in range(8):
                    for j in range(2):
                        attention_tensor_transposes(pe, S0, S1, 2 * c + j, "t")
                    bank = banks.open(pe, ("o", c))
                    for j in range(2):
                        hd = 2 * c + j
                        banks.wait_drained(pe, ("t", hd))
                        v = V1[:, :, 64 * (hd // 4):64 * (hd // 4) + 64]
                        rows = slice(64 * j, 64 * j + 64)
                        pe.matmul(bank[rows, 0:T], v[:, 0, :], PT[:, hd, 0:T], start=True, stop=False)
                        ins = pe.matmul(bank[rows, P:T], v[:, 1, :], PT[:, hd, T:384], start=False, stop=True)
                    banks.close(ins, ("o", c))

        CZ = view(9728, SC * 2, P)
        cosT, sinT, fr, kk, ta, tb, wr, wi, gr, gi = (view(13824 + 1024 * i, 4, T) for i in range(10))
        s5 = arena[:, 30720:30720 + 24 * SC].rearrange("p (k n) -> p k n", n=SC)
        s5c = arena[:, 31104:31104 + 1536].rearrange("p (k n) -> p k n", k=6)
        MAGIC = 12582912.0
        TWO_PI = 2.0 * np.pi
        TURN = float(np.float32(TWO_PI * (1 - 1e-7)))
        (STEP, LS, TH, TAU, MAG, SIN, COS, TAUC, NR, NI, DN, CRE, CIM, TA, TB, KA, RDN) = range(17)
        s_a3, s_v3, s_tab, s_fr, s_g, s_gel, s_zero3, s_rot = (
            sem(n) for n in ("a3", "v3", "tab3", "fr3", "g3", "gel3", "zero3", "rot3"))
        s_b, s_y = sem("b3"), sem("y3")
        ring.plan(banks, [(s_b, uc + 1) for uc in range(UC)])

        def psum4(first):
            return ps[:, 512 * first:512 * first + 2048].rearrange("p (b n) -> p b n", n=512)

        with nc.Block() as block:
            @block.sync
            def _(sp):
                for _ in range(UC):
                    ring.load(sp, w1[ring.issued, :, :])

            @block.gpsimd
            def _(pool):
                pool.memset(CZ, 0.0).then_inc(s_zero3, 1)

            @block.scalar
            def _(act):
                link = Chain(act, s_a3)
                link(act.activation(s5[:, STEP], par("lstep"), ACT.Exp))
                act.wait_ge(s_v3, 2)
                link(act.activation(s5[:, MAG], s5[:, LS], ACT.Exp))
                act.wait_ge(s_v3, 9)
                act.activation(s5[:, SIN], s5[:, TAU], ACT.Sin, scale=TURN).then_inc(s_a3, 1)
                link_n = 3
                act.activation(s5[:, COS], s5[:, TAUC], ACT.Sin, scale=TURN).then_inc(s_a3, 1)
                for uc in range(UC):
                    act.wait_ge(s_fr, 2 * uc + 1)
                    act.activation(sinT, fr, ACT.Sin, scale=TURN).then_inc(s_tab, 1)
                    act.wait_ge(s_fr, 2 * uc + 2)
                    act.activation(cosT, kk, ACT.Sin, scale=TURN).then_inc(s_tab, 1)
                for uc in range(UC):
                    act.wait_ge(s_gel, uc + 1)
                    act.activation(uT[:, uc, :], uT[:, uc, :], ACT.Gelu).then_inc(s_a3, 1)

            @block.vector
            def _(dve):
                link = Chain(dve, s_v3)

                def col(i):
                    return s5[:, i]

                dve.wait_ge(s_a3, 1)
                link(dve.tensor_tensor(col(LS), par("lre"), col(STEP), ALU.mult))
                link(dve.tensor_tensor(col(TH), par("lim"), col(STEP), ALU.mult))
                link(dve.tensor_scalar(col(TAU), col(TH), 1.0 / TWO_PI, None, ALU.mult))
                link(dve.tensor_scalar(col(KA), col(TAU), MAGIC, None, ALU.add))
                link(dve.tensor_scalar(col(KA), col(KA), MAGIC, None, ALU.subtract))
                link(dve.tensor_tensor(col(TAU), col(TAU), col(KA), ALU.subtract))
                link(dve.tensor_scalar(col(KA), col(TAU), 0.25, None, ALU.is_ge))
                link(dve.tensor_scalar(col(TAUC), col(TAU), 0.25, None, ALU.add))
                link(dve.tensor_tensor(col(TAUC), col(TAUC), col(KA), ALU.subtract))
                link(dve.tensor_tensor(col(TA), par("lre"), par("lre"), ALU.mult))
                link(dve.tensor_tensor(col(TB), par("lim"), par("lim"), ALU.mult))
                link(dve.tensor_tensor(col(DN), col(TA), col(TB), ALU.add))
                link(dve.reciprocal(col(RDN), col(DN)))
                dve.wait_ge(s_a3, 4)
                link(dve.tensor_tensor(col(NR), col(MAG), col(COS), ALU.mult))
                link(dve.tensor_scalar(col(NR), col(NR), 1.0, None, ALU.subtract))
                link(dve.tensor_tensor(col(NI), col(MAG), col(SIN), ALU.mult))
                for out_col, x, y, op in ((CRE, NR, NI, ALU.add), (CIM, NI, NR, ALU.subtract)):
                    link(dve.tensor_tensor(col(TA), col(x), par("lre"), ALU.mult))
                    link(dve.tensor_tensor(col(TB), col(y), par("lim"), ALU.mult))
                    link(dve.tensor_tensor(col(TA), col(TA), col(TB), op))
                    link(dve.tensor_tensor(col(out_col), col(TA), col(RDN), ALU.mult))
                cs = par("cs5").rearrange("p (s k c) -> p k s c", k=2, c=16)

                def c5(i):
                    return s5c[:, i].rearrange("p (s c) -> p s c", c=16)

                link(dve.tensor_tensor(c5(0), cs[:, 0], bcast(col(CRE), 16), ALU.mult))
                link(dve.tensor_tensor(c5(1), cs[:, 1], bcast(col(CIM), 16), ALU.mult))
                link(dve.tensor_tensor(c5(2), cs[:, 0], bcast(col(CIM), 16), ALU.mult))
                link(dve.tensor_tensor(c5(3), cs[:, 1], bcast(col(CRE), 16), ALU.mult))
                link(dve.tensor_tensor(c5(4), c5(0), c5(1), ALU.subtract))
                link(dve.scalar_tensor_tensor(s5c[:, 5], s5c[:, 2], -1.0, s5c[:, 3], ALU.mult, ALU.subtract))
                dve.wait_ge(s_zero3, 1)
                for g in range(2):
                    for r in range(2):
                        for q in range(4):
                            dst = CZ[64 * g:64 * g + 64, :, :].rearrange("p (u q k) n -> p k q u n", q=4, k=2)
                            src = s5c[64 * g:64 * g + 64, 4 + r].rearrange("p (u q c) -> p q u c", q=4, c=16)
                            col0 = 32 * q + 16 * g
                            ins = dve.tensor_copy(dst[:, r, q, :, col0:col0 + 16], src[:, q])
                link(ins)

                def tables():
                    for i in range(4):
                        tau = col(TAU)[:, 4 * uc + i:4 * uc + i + 1]
                        ins = dve.tensor_scalar(kk[:, i, :], const("time"), tau, MAGIC, ALU.mult, ALU.add)
                    link(ins)
                    link(dve.tensor_scalar(kk, kk, MAGIC, None, ALU.subtract))
                    for i in range(4):
                        tau = col(TAU)[:, 4 * uc + i:4 * uc + i + 1]
                        ins = dve.scalar_tensor_tensor(fr[:, i, :], const("time"), tau, kk[:, i, :],
                                                       ALU.mult, ALU.subtract)
                    ins.then_inc(s_fr, 1)
                    dve.wait_ge(s_fr, 2 * uc + 1)
                    link(dve.tensor_scalar(kk, fr, 0.25, None, ALU.is_ge))
                    dve.scalar_tensor_tensor(kk, fr, 0.25, kk, ALU.add, ALU.subtract).then_inc(s_fr, 1)

                for uc in range(UC):
                    tables()
                    re, im = psum4(0)[:, :, 0:T], psum4(0)[:, :, T:2 * T]
                    dve.wait_ge(s_b, uc + 1)
                    dve.wait_ge(s_tab, 2 * uc + 2)
                    dve.tensor_tensor(ta, re, cosT, ALU.mult)
                    link(dve.tensor_tensor(tb, im, sinT, ALU.mult))
                    link(dve.tensor_tensor(wr, ta, tb, ALU.add))
                    dve.tensor_tensor(ta, im, cosT, ALU.mult)
                    link(dve.tensor_tensor(tb, re, sinT, ALU.mult))
                    dve.tensor_tensor(wi, ta, tb, ALU.subtract).then_inc(s_rot, 1)
                    dve.wait_ge(s_rot, uc + 1)
                    for i in range(4):
                        mag = col(MAG)[:, 4 * uc + i:4 * uc + i + 1].broadcast_to([P, T])
                        dve.tensor_tensor_scan(gr[:, i, :], mag, wr[:, i, :], 0.0, ALU.mult, ALU.add)
                        ins = dve.tensor_tensor_scan(gi[:, i, :], mag, wi[:, i, :], 0.0, ALU.mult, ALU.add)
                    link(ins)
                    dve.tensor_tensor(ta, gr, cosT, ALU.mult)
                    link(dve.tensor_tensor(tb, gi, sinT, ALU.mult))
                    link(dve.tensor_tensor(wr, ta, tb, ALU.subtract))
                    dve.tensor_tensor(ta, gr, sinT, ALU.mult)
                    link(dve.tensor_tensor(tb, gi, cosT, ALU.mult))
                    dve.tensor_tensor(wi, ta, tb, ALU.add).then_inc(s_g, 1)
                    dve.wait_ge(s_y, uc + 1)
                    dve.scalar_tensor_tensor(uT[:, uc, :], uT[:, uc, :], par("dskip")[:, uc:uc + 1],
                                             psum[4 + uc % 2][:, 0:T],
                                             ALU.mult, ALU.add).then_inc(s_gel, 1)

            @block.tensor
            def _(pe):
                for uc in range(UC):
                    w = ring.unit(pe).rearrange("p (q k n) -> p q k n", q=4, k=2)
                    if uc:
                        pe.wait_ge(s_rot, uc)
                    for i in range(4):
                        for k in range(2):
                            ins = pe.matmul(psum[i][:, k * T:(k + 1) * T], w[:, i, k, :], uT[:, uc, :],
                                            start=True, stop=True)
                    ins.then_inc(s_b, 1)
                    bank = psum[4 + uc % 2]
                    if uc >= 2:
                        pe.wait_ge(s_gel, uc - 1)
                    pe.wait_ge(s_g, uc + 1)
                    for i in range(4):
                        for k, src in enumerate((wr, wi)):
                            ins = pe.matmul(bank[:, 0:T], CZ[:, 2 * (4 * uc + i) + k, :], src[:, i, :],
                                            start=(i + k == 0), stop=(i + k == 4))
                    ins.then_inc(s_y, 1)

        gluT = view(9728, 4, T)
        sig = view(10752, 4, T)
        tmp = view(11776, 2, T)
        sq4 = view(12288, 8, T)
        s_mix, s_sq4, s_v4, s_xn2 = (sem(n) for n in ("mix4", "sq4", "v4", "xn2"))
        banks.plan([("gb", i) for i in range(2)] + [("ga", i) for i in range(2)] + [("ya", i) for i in range(4)]
                   + [("ys", i) for i in range(4)] + [("out", i) for i in range(4)] + ["ms2"])
        ring.plan(banks, [("gb", 0), ("gb", 1), ("ga", 0), ("ga", 1)])
        ring.plan(banks, pairs_of([("ya", i) for i in range(4)]), True)
        ring.plan(banks, [("ys", i) for i in range(4)])
        ring.plan(banks, pairs_of([("out", i) for i in range(4)]), True)
        xn2 = view(30720, 8, T)

        with nc.Block() as block:
            @block.sync
            def _(sp):
                while ring.issued < 60 + SLOTS:
                    ring.load(sp, w1[ring.issued, :, :])

            @block.gpsimd
            def _(pool):
                ring.subtract(pool, 10)
                parts.subtract(pool, "pool", mix)
                ring.subtract(pool)
                parts.subtract(pool, "pool", xn2)

            @block.scalar
            def _(act):
                for i in range(2):
                    b = banks.take(act, ("gb", i))
                    banks.give(act.activation(sig[:, 2 * i:2 * i + 2, :], two(b[:, :]), ACT.Sigmoid), ("gb", i))
                ring.round(act, 10)
                parts.round(act, mix, s_mix, 0, 2)
                for i in range(4):
                    ring.feed(act, ("out", i))
                    banks.wait_drained(act, ("out", i))
                    act.activation(sq4[:, 2 * i:2 * i + 2, :], hT[:, 2 * i:2 * i + 2, :], ACT.Square).then_inc(s_sq4, 1)
                b = banks.take(act, "ms2")
                banks.give(root_of_mean(act, b, D, std[:, 0:T]), "ms2")
                parts.round(act, xn2, s_xn2, 0)

            @block.vector
            def _(dve):
                link = Chain(dve, s_v4)
                for i in range(2):
                    b = banks.take(dve, ("ga", i))
                    banks.wait_drained(dve, ("gb", i))
                    banks.give(dve.tensor_tensor(gluT[:, 2 * i:2 * i + 2, :], two(b[:, :]), sig[:, 2 * i:2 * i + 2, :],
                                                 ALU.mult), ("ga", i))
                for i in range(4):
                    b = banks.take(dve, ("ya", i))
                    banks.give(dve.tensor_tensor(mix[:, 2 * i:2 * i + 2, :], two(b[:, :]),
                                                 gates[:, 8 + 2 * i:10 + 2 * i, :], ALU.mult), ("ya", i))
                for i in range(4):
                    b = banks.take(dve, ("ys", i))
                    if i:
                        dve.wait_ge(s_mix, i)
                    banks.give(dve.tensor_tensor(tmp, two(b[:, :]), gates[:, 2 * i:2 * i + 2, :], ALU.mult), ("ys", i))
                    banks.wait_drained(dve, ("ys", i))
                    dve.tensor_tensor(mix[:, 2 * i:2 * i + 2, :], mix[:, 2 * i:2 * i + 2, :], tmp,
                                      ALU.add).then_inc(s_mix, 1)
                parts.subtract(dve, "dve", mix)
                for i in range(4):
                    b = banks.take(dve, ("out", i))
                    banks.give(dve.tensor_tensor(hT[:, 2 * i:2 * i + 2, :], hT[:, 2 * i:2 * i + 2, :], two(b[:, :]),
                                                 ALU.add), ("out", i))
                banks.wait_drained(dve, "ms2")
                link(dve.reciprocal(rst[:, 0:T], std[:, 0:T]))
                for c in range(DC):
                    dve.scalar_tensor_tensor(xn2[:, c, :], hT[:, c, :], par("ln2")[:, c:c + 1], rst[:, 0:T],
                                             ALU.mult, ALU.mult).then_inc(s_xn2, 1)
                parts.subtract(dve, "dve", xn2)

            @block.tensor
            def _(pe):
                for name in ("gb", "ga"):
                    for i in range(2):
                        linear_part(pe, (name, i), ring.unit(pe).rearrange("p (k n) -> p k n", k=4), uT, (0, P))
                for i in range(4):
                    linear(pe, ("ya", i))
                banks.wait_drained(pe, ("ga", 1))
                for i in range(4):
                    linear_part(pe, ("ys", i), ring.unit(pe).rearrange("p (k n) -> p k n", k=4), gluT, (0, P))
                parts.wait(pe)
                for i in range(4):
                    linear(pe, ("out", i))
                sum_squares(pe, "ms2", sq4, DC, (s_sq4, 4))

        U = 16384
        qp = view(U, PH, T)
        keys_v = view(U + 2048, PH, T)
        cand = view(U, TT, PH, 256)
        s_v = view(U + 4096, TT, PH * 2, NSUB)
        eq = view(U + 4096, PH * TOPK, TOPK)
        sel = view(U + 6144, PH * TOPK, TOPK)
        f5 = arena[:, U + 8192:U + 8192 + 3456]
        idx = arena[:, U + 11648:U + 12160].bitcast(U32)
        vals = f5[:, 0:512].rearrange("p (t g n) -> p t g n", t=TT, n=TOPK)
        idxf = f5[:, 512:1024].rearrange("p (t g n) -> p t g n", t=TT, n=TOPK)
        best = f5[:, 1024:1280].rearrange("p (g n) -> p g n", n=TOPK)
        gate = f5[:, 1280:1536].rearrange("p (g n) -> p g n", n=TOPK)
        rank = f5[:, 1536:2048].rearrange("p (k t n) -> p k t n", k=2, t=TT)
        chosen = f5[:, 2048:2560].rearrange("p (k t n) -> p k t n", k=2, t=TT)
        gsum = f5[:, 2560:2576]
        iota16 = const("lane")[:, 0:TOPK]
        ranku = f5[:, 2688:3200].bitcast(U32).rearrange("p (k n) -> p k n", k=2)
        per_slot = small[:, 0:768].rearrange("p (k t) -> p k t", k=3)
        I1, I2, GT = per_slot[:, 0], per_slot[:, 1], per_slot[:, 2]
        idx_v = idx.rearrange("p (t g n) -> p t g n", t=TT, n=TOPK)
        pos = f5[:, 3200:3456].bitcast(U32).rearrange("p (g n) -> p g n", n=TOPK)
        s_keys, s_v5, s_e5, s_x5, s_sel, s_tr, s_slot = (
            sem(n) for n in ("keys5", "v5", "e5", "x5", "sel5", "transposed", "per_slot"))
        banks.plan([("pq", i) for i in range(4)] + [("ps", i) for i in range(8)])
        ring.plan(banks, pairs_of([("pq", i) for i in range(4)]), True)

        A = view(0, NE2, T)
        HALF = NE2 // 2
        ROWS_BEFORE = 68 // SLOTS
        GROUPS = T // 4
        OH1 = small[:, 768:1792].rearrange("p (b t n) -> p b t n", b=2, t=4)
        OH2 = small[:, 1792:2304].rearrange("p (b t n) -> p b t n", b=2, t=4)
        w_hi, w_lo, hi_done, lo_done, e_hi, e_lo, a_drained, g_one, g_full, g_done, s_h8 = (
            sem(n) for n in ("w_hi", "w_lo", "hi_done", "lo_done", "e_hi", "e_lo", "a_drained",
                             "onehot", "grid_full", "grid_done", "h8"))

        with nc.Block() as block:
            @block.sync
            def _(sp):
                sp.dma_start(keys_v, keys.rearrange("p (h n) -> p h n", h=PH)).then_inc(s_keys, 16)
                while ring.issued < 68:
                    ring.load(sp, w1[ring.issued, :, :])
                for j in range(SLOTS):
                    sp.wait_ge(ring.rest, ring.number[64 + j] + 1)
                    sp.dma_start(slots_v[:, j, :], wu[j, :, :]).then_inc(ring.loaded[j], 16)
                with sp.Fori(0, NE2 // SLOTS - 1) as it:
                    for j in range(SLOTS):
                        sp.wait_ge(w_lo, it * SLOTS + (j + 1))
                        sp.dma_start(slots_v[:, j, :], wu[it * SLOTS + (SLOTS + j), :, :]).then_inc(ring.loaded[j], 16)
                with sp.Fori(0, NE2 // SLOTS) as it:
                    for j in range(SLOTS):
                        sp.wait_ge(w_lo, it * SLOTS + (NE2 - SLOTS + j + 1))
                        sp.dma_start(slots_v[:, j, :], wv[it * SLOTS + j, :, :]).then_inc(ring.loaded[j], 16)
                sp.wait_ge(s_keys, 16)

            @block.scalar
            def _(act):
                def round_row(it, n, early=False):
                    s = n % SLOTS
                    act.wait_ge(ring.loaded[s], it * (8 // SLOTS * 16) + 16 * (ROWS_BEFORE + n // SLOTS + 1))
                    if not early:
                        act.wait_ge(hi_done, it * 8 + (n - 1))
                        act.wait_ge(w_lo, it * 8 + (n - 1))
                    act.activation(whv[:, n % 2, :], slots_v[:, s, :], ACT.Copy).then_inc(w_hi, 1)

                def up_rows(it, first):
                    for j in range(8):
                        round_row(it, first + j + 2)
                        if j % 2:
                            act.wait_ge(lo_done, it * 8 + (first + j + 1))
                            act.activation(A[:, bass.ds(it * 8 + (first + j - 1), 2), :], two(psum[j // 2]),
                                           ACT.Gelu).then_inc(a_drained, 1)

                def round_a(it, row):
                    act.activation(xhT[:, row % 4, :], A[:, bass.ds(it * 8 + row, 1), :].rearrange("p o t -> p (o t)"),
                                   ACT.Copy).then_inc(e_hi, 1)

                def down_rows(it, first, last):
                    for j in range(8):
                        if first + j + 2 < NE2 or not last:
                            round_row(it, NE2 + first + j + 2)
                        if not (last and j >= 6):
                            if first + j >= 2 or not isinstance(it, int):
                                act.wait_ge(lo_done, it * 8 + (NE2 + first + j - 1))
                            round_a(it, first + j + 2)

                ring.round(act, 2)
                for i in range(4):
                    ring.feed(act, ("pq", i))
                    b = banks.take(act, ("pq", i))
                    banks.give(act.activation(qp[:, 2 * i:2 * i + 2, :], two(b[:, :]), ACT.Copy), ("pq", i))
                for i in range(8):
                    b = banks.take(act, ("ps", i))
                    dst = s_v[:, i // 4, 4 * (i % 4):4 * (i % 4) + 4, :]
                    banks.give(act.activation(dst, two(b[:, :], P), ACT.Copy), ("ps", i))
                round_row(0, 0, True)
                round_row(0, 1, True)
                with act.Fori(0, HALF // 8 - 1) as it:
                    up_rows(it, 0)
                act.wait_ge(s_x5, 1)
                act.activation(gate, gate, ACT.Exp).then_inc(s_e5, 1)
                up_rows(0, HALF - 8)
                for k in range(3):
                    act.wait_ge(s_tr, k + 1)
                    act.activation(per_slot[:, k], psum[4 + k][:, 0:T], ACT.Copy).then_inc(s_slot, 1)
                with act.Fori(0, HALF // 8) as it:
                    up_rows(it, HALF)
                for half in range(2):
                    act.wait_ge(g_done, GROUPS * (half + 1))
                    first = half * HALF
                    act.wait_ge(lo_done, NE2 + max(first - 2, 0))
                    round_a(0, first)
                    round_a(0, first + 1)
                    with act.Fori(0, HALF // 8 - 1) as it:
                        down_rows(it, first, False)
                    down_rows(0, first + HALF - 8, True)

            @block.gpsimd
            def _(pool):
                def rest_row(it, n, early=False):
                    pool.wait_ge(w_hi, it * 8 + (n + 1))
                    if not early:
                        pool.wait_ge(lo_done, it * 8 + (n - 1))
                    pool.tensor_tensor(wlv[:, n % 2, :], slots_v[:, n % SLOTS, :], whv[:, n % 2, :].bitcast(F32),
                                       ALU.subtract).then_inc(w_lo, 1)

                def rest_a(it, row):
                    pool.wait_ge(e_hi, it * 8 + (row + 1))
                    pool.tensor_tensor(xlT[:, row % 4, :], A[:, bass.ds(it * 8 + row, 1), :].rearrange("p o t -> p (o t)"),
                                       xhT[:, row % 4, :].bitcast(F32), ALU.subtract).then_inc(e_lo, 1)

                def down_rows(it, first, last):
                    for j in range(8):
                        if first + j + 2 < NE2 or not last:
                            rest_row(it, NE2 + first + j + 2)
                            rest_a(it, first + j + 2)

                ring.subtract(pool)
                pool.wait_ge(*ring.last[67])
                rest_row(0, 0, True)
                rest_row(0, 1, True)
                with pool.Fori(0, NE2 // 8) as it:
                    for j in range(8):
                        rest_row(it, j + 2)
                rest_a(0, 0)
                rest_a(0, 1)
                with pool.Fori(0, NE2 // 8 - 1) as it:
                    down_rows(it, 0, False)
                down_rows(0, NE2 - 8, True)

            @block.vector
            def _(dve):
                link = Chain(dve, s_v5)
                low = -3e38

                def top16(rows, values, indices):
                    for a in (0, 8):
                        for r, v, i in zip(rows, values, indices):
                            ins = dve.max(v[:, a:a + 8], r)
                        link(ins)
                        for r, v, i in zip(rows, values, indices):
                            ins = dve.max_index(i[:, a:a + 8], v[:, a:a + 8], r)
                        if a == 0:
                            link(ins)
                            for r, v, i in zip(rows, values, indices):
                                ins = dve.match_replace(r, v[:, 0:8], r, low)
                            link(ins)
                    link(ins)

                for t in range(TT):
                    for i in range(4):
                        banks.wait_drained(dve, ("ps", 4 * t + i))
                    top16([s_v[:, t, g, :] for g in range(16)], [vals[:, t, g, :] for g in range(16)],
                          [idx_v[:, t, g, :] for g in range(16)])
                    if t == 0:
                        for i in range(4, 8):
                            banks.wait_drained(dve, ("ps", i))
                    pair = vals[:, t].rearrange("p (h k) n -> p h k n", k=2)
                    first = pair[:, :, 0, :].rearrange("p h (n o) -> p h n o", o=1).broadcast_to([P, PH, 16, 16])
                    second = pair[:, :, 1, :].rearrange("p h (o n) -> p h o n", o=1).broadcast_to([P, PH, 16, 16])
                    link(dve.tensor_tensor(cand[:, t].rearrange("p h (i j) -> p h i j", j=16), first, second, ALU.add))
                    top16([cand[:, t, g, :] for g in range(PH)], [best[:, PH * t + g, :] for g in range(PH)],
                          [pos[:, PH * t + g, :] for g in range(PH)])
                dve.tensor_copy(idxf, idx_v)
                dve.tensor_tensor(gate, best, best[:, :, 0:1].broadcast_to([P, TT * PH, TOPK]),
                                  ALU.subtract).then_inc(s_x5, 1)
                posf = pos.rearrange("p g n -> p (g n)")
                dve.tensor_scalar(ranku[:, 0], posf, 4, None, ALU.logical_shift_right)
                link(dve.tensor_scalar(ranku[:, 1], posf, 15, None, ALU.bitwise_and))
                link(dve.tensor_copy(rank, ranku.rearrange("p k (t n) -> p k t n", t=TT)))
                for t in range(TT):
                    pair = idxf[:, t].rearrange("p (h k) n -> p h k n", k=2)
                    for k in range(2):
                        link(dve.tensor_tensor(
                            eq, bcast(rank[:, k, t, :], TOPK),
                            iota16.rearrange("p (o n) -> p o n", o=1).broadcast_to([P, P, TOPK]), ALU.is_equal))
                        place = pair[:, :, k, :].rearrange("p h (o n) -> p h o n", o=1).broadcast_to([P, PH, 16, 16])
                        link(dve.tensor_tensor(sel.rearrange("p (h r) n -> p h r n", h=PH),
                                               eq.rearrange("p (h r) n -> p h r n", h=PH), place, ALU.mult))
                        dve.tensor_reduce(chosen[:, k, t, :], sel, AX.X, ALU.add).then_inc(s_sel, 1)
                dve.wait_ge(s_e5, 1)
                link(dve.tensor_reduce(gsum, gate, AX.X, ALU.add))
                link(dve.reciprocal(gsum, gsum))
                dve.tensor_tensor(gate, gate, bcast(gsum, TOPK), ALU.mult).then_inc(s_sel, 1)

                def build(half, it, n, early=False):
                    b = n % 2
                    if not early:
                        dve.wait_ge(g_full, it * 4 + (GROUPS * half + n - 1))
                    for t in range(4):
                        at = bass.ds(it * 16 + (n * 4 + t), 1)
                        dve.tensor_scalar(OH1[:, b, t, :], const("lane"), I1[:, at], GT[:, at], ALU.is_equal, ALU.mult)
                        ins = dve.tensor_scalar(OH2[:, b, t, :], const("lane")[:, HALF * half:HALF * (half + 1)],
                                                I2[:, at], None, ALU.is_equal)
                    ins.then_inc(g_one, 1)

                def spread(half, it, n):
                    dve.wait_ge(g_full, it * 4 + (GROUPS * half + n + 1))
                    a = A[:, HALF * half:HALF * (half + 1), bass.ds(it * 16 + n * 4, 4)]
                    dve.tensor_tensor(a, psum[4 + n % 4][:, 0:4 * HALF].rearrange("p (t e) -> p e t", t=4), a,
                                      ALU.mult).then_inc(g_done, 1)

                dve.wait_ge(s_slot, 3)
                for half in range(2):
                    dve.wait_ge(a_drained, HALF // 2 * (half + 1))
                    build(half, 0, 0, half == 0)
                    build(half, 0, 1, half == 0)
                    spread(half, 0, 0)
                    with dve.Fori(0, GROUPS // 4 - 1) as it:
                        for j in range(4):
                            build(half, it, j + 2)
                            spread(half, it, j + 1)
                    for n in range(GROUPS - 4, GROUPS - 1):
                        if n + 2 < GROUPS:
                            build(half, 0, n + 2)
                        spread(half, 0, n + 1)
                dve.wait_ge(lo_done, 2 * NE2)
                for b in range(4):
                    dve.tensor_tensor(hT[:, 2 * b:2 * b + 2, :], hT[:, 2 * b:2 * b + 2, :], two(psum[b]),
                                      ALU.add).then_inc(s_h8, 1)

            @block.tensor
            def _(pe):
                for i in range(4):
                    linear(pe, ("pq", i))
                pe.wait_ge(s_keys, 16)
                for i in range(8):
                    bank = banks.open(pe, ("ps", i))
                    t = i // 4
                    for j in range(2):
                        hd = 2 * (i % 4) + j
                        if j == 0:
                            banks.wait_drained(pe, ("pq", i % 4))
                        ins = pe.matmul(bank[:, j * T:(j + 1) * T], qp[:, hd, t * P:(t + 1) * P], keys_v[:, hd, :],
                                        start=True, stop=True)
                    banks.close(ins, ("ps", i))

                def grid(half, it, n):
                    number = GROUPS * half + n
                    if number >= 4 or not isinstance(it, int):
                        pe.wait_ge(g_done, it * 4 + (number - 3))
                    pe.wait_ge(g_one, it * 4 + (number + 1))
                    for t in range(4):
                        ins = pe.matmul(psum[4 + n % 4][:, t * HALF:(t + 1) * HALF], OH1[:, n % 2, t, :],
                                        OH2[:, n % 2, t, :], start=True, stop=True)
                    ins.then_inc(g_full, 1)

                def up_rows(it, first, early, gated):
                    for j in range(8):
                        if j % 2 == 0 and not early:
                            pe.wait_ge(a_drained, it * 4 + (first // 2 + j // 2 - 3))
                        out = psum[j // 2][:, (j % 2) * T:(j % 2 + 1) * T]
                        hi, lo = (x[:, j % 2, :].rearrange("p (k n) -> p k n", k=DC) for x in (whv, wlv))
                        pe.wait_ge(w_hi, it * 8 + (first + j + 1))
                        for k in range(DC):
                            pe.matmul(out, hi[:, k, :], xhT[:, k, :], start=(k == 0), stop=False)
                            ins = pe.matmul(out, hi[:, k, :], xlT[:, k, :], start=False, stop=False)
                        ins.then_inc(hi_done, 1)
                        pe.wait_ge(w_lo, it * 8 + (first + j + 1))
                        for k in range(DC):
                            ins = pe.matmul(out, lo[:, k, :], xhT[:, k, :], start=False, stop=(k == DC - 1))
                        ins.then_inc(lo_done, 1)
                        if gated:
                            grid(0, it * 2, j)

                def down_rows(it, first, early, gated):
                    for j in range(8):
                        hi, lo = whv[:, j % 2, :], wlv[:, j % 2, :]
                        a_hi, a_lo = xhT[:, j % 4, :], xlT[:, j % 4, :]
                        pe.wait_ge(w_hi, it * 8 + (NE2 + first + j + 1))
                        pe.wait_ge(e_hi, it * 8 + (first + j + 1))
                        pe.wait_ge(e_lo, it * 8 + (first + j + 1))
                        for c in range(DC):
                            out = psum[c // 2][:, (c % 2) * T:(c % 2 + 1) * T]
                            pe.matmul(out, hi[:, c * P:(c + 1) * P], a_hi, start=(early and j == 0 and c % 2 == 0),
                                      stop=False, skip_group_check=True)
                            ins = pe.matmul(out, hi[:, c * P:(c + 1) * P], a_lo, start=False, stop=False,
                                            skip_group_check=True)
                        ins.then_inc(hi_done, 1)
                        pe.wait_ge(w_lo, it * 8 + (NE2 + first + j + 1))
                        for c in range(DC):
                            ins = pe.matmul(psum[c // 2][:, (c % 2) * T:(c % 2 + 1) * T], lo[:, c * P:(c + 1) * P], a_hi,
                                            start=False, stop=False, skip_group_check=True)
                        ins.then_inc(lo_done, 1)
                        if gated:
                            grid(1, it * 2, j)

                for i in range(8):
                    banks.wait_drained(pe, ("ps", i))
                up_rows(0, 0, True, False)
                with pe.Fori(1, HALF // 8) as it:
                    up_rows(it, 0, False, False)
                gate_t = gate.rearrange("p (t h) n -> p t (h n)", t=TT)
                for k in range(3):
                    pe.wait_ge(s_sel, 4 if k < 2 else 5)
                    for t in range(TT):
                        src = chosen[:, k, t, :] if k < 2 else gate_t[:, t, :]
                        ins = pe.transpose(psum[4 + k][:, t * P:(t + 1) * P], src, const("ident"))
                    ins.then_inc(s_tr, 1)
                pe.wait_ge(s_slot, 3)
                up_rows(0, HALF, False, True)
                with pe.Fori(1, HALF // 8) as it:
                    up_rows(it, HALF, False, True)
                pe.wait_ge(a_drained, HALF)
                down_rows(0, 0, True, True)
                with pe.Fori(1, HALF // 8) as it:
                    down_rows(it, 0, False, True)
                with pe.Fori(0, HALF // 8) as it:
                    down_rows(it, HALF, False, False)
        if stop_after == "peer":
            return

        banks.reset()
        ring.reset()
        parts.reset()
        memory.close()
        LOW = 13632
        late_cst = sb("late_cst", NCONST - NEARLY)
        low_part = sb("layer", LOW)
        upper = ctx.enter_context(ExitStack())
        high_part = upper.enter_context(nc.sbuf_tensor("layer_upper", [P, 31088 - LOW], F32))

        def part(a, b):
            return low_part[:, a:b] if b <= LOW else high_part[:, a - LOW:b - LOW]

        xnT = view(24000, 8, T)
        raw = view(0, 8, T)
        qA = view(2048, 4, T)
        KZ2 = part(3072, 5120).rearrange("p (b g v t) -> p b g v t", b=2, g=2, v=2)
        KZC = part(5120, 5184).rearrange("p (g v i) -> p g v i", g=2, v=2)
        kcr = part(5184, 5440)
        X = part(5440, 6464).rearrange("p (k l n) -> p k l n", k=2, l=16)
        Z = part(6464, 7488).rearrange("p (k g t) -> p k g t", k=2, g=2)
        cq, cqn = view(7488, 2, T), view(8000, 2, T)
        ckr = view(8512, 2, T)
        ckvn = part(9024, 9280)
        kpe = part(9280, 9536)
        qMr, qM, KM = view(9536, 8, T), view(11584, 8, T), view(13632, 8, T)
        V2, Vm = view(15680, TT, T), view(16192, TT, 512)
        GA = part(17216, 17264).rearrange("p (t h b) -> p t h b", t=TT, b=3)
        hid = part(17264, 17392).rearrange("p (k c n) -> p k c n", k=2, c=2)
        vcmp = view(17392, 2, 64)
        ra, rb = view(17520, 2, T), view(18032, 2, T)
        sqL = view(18544, 8, T)
        sqc = view(20592, 3, T)
        SA0, SA1 = view(18544, 24, P), view(21616, 24, T)
        PTR = view(27760, 8, 384)
        Sc = part(30832, 31088).rearrange("p (t h i) -> p t h i", t=TT, h=8)
        PTC = view(0, 8, T)
        aT = view(9536, 8, T)
        sqo = view(2048, 8, T)
        relu = view(4096, 4, T).rearrange("p (b c) t -> p b c t", b=2)
        fx = view(6144, 8, T)
        squared = view(8192, 2, T)
        mixT = view(11584, 8, T)
        st2 = small[:, 512:512 + 192].rearrange("p (k t n) -> p k t n", k=4, t=TT)
        MX2, NM2, DEN2, RC2 = (st2[:, i] for i in range(4))
        stc = small[:, 704:704 + 48].rearrange("p (k t n) -> p k t n", k=3, t=TT)

        def p2(name):
            return par(name, PAR2)

        names = ("lpar", "lsq", "lxn", "lzero", "lstep", "lsqc", "lrope", "lX", "lcx", "lkzc", "lmsq", "lmskv", "lku",
                 "amx", "aden", "ap", "avec", "acv", "acx", "acp", "az", "fsq", "fmix", "frelu", "fhid", "fsqr", "fhigh", "fvec", "fh",
                 "fsq2", "fxn2", "lcopies")
        L = {n: sem(n) for n in names}
        loop_sems = ring.loaded + [ring.used, ring.rounded, ring.rest, parts.sem_hi, parts.sem_pool, parts.sem_dve] + banks.full + banks.drained + list(L.values())

        banks.plan(["ms", ("in", 0), ("in", 1), ("in", 2), ("in", 3), ("in", 4), ("in", 5), "V", "G",
                    "rc", "msq", "mskv", ("rp", 0), ("rp", 1), ("rp", 2), "rk"]
                   + [("uq", i) for i in range(4)] + [("uk", i) for i in range(4)] + [("uv", t) for t in range(TT)]
                   + [("ck", 0), ("ck", 1), ("cv", 0), ("cv", 1)] + [("rq", i) for i in range(4)] + ["k2", "v2"])
        ring.plan(banks, pairs_of([("in", i) for i in range(6)]), True)
        ring.plan(banks, pairs_of(["V"])
                  + [("uq", 1), ("uq", 3), ("uk", 3), ("uv", 1)] + [None] * 3 + [("ck", 1)] + [None] * 3 + [("cv", 1)])

        pair_jobs = []
        for c in range(8):
            if c < 4:
                pair_jobs.append(([("tc", c)], [2 * c, 2 * c + 1, 8 + 2 * c, 9 + 2 * c]))
            else:
                pair_jobs.append(([], [8 + 2 * c, 9 + 2 * c]))
        banks.plan(["sc"] + [("s2", t, c) for t in range(TT) for c in range(12)])
        for c, (tc, heads) in enumerate(pair_jobs):
            banks.plan(tc + [("t2", hd) for hd in heads] + [("o2", c)])
        order = [hd for _, heads in pair_jobs for hd in heads]
        slot = {hd: i % 8 for i, hd in enumerate(order)}

        banks.plan(["mo0", "mo1"] + [("wo", i) for i in range(4)] + ["mf"] + [("f1", i) for i in range(16)]
                   + [("f2", b) for b in range(4)])
        ring.plan(banks, pairs_of([("wo", i) for i in range(4)] + [("f1", i) for i in range(16)])
                  + [None] * 31 + [("f2", 3)], True)
        late = sem("late_constants")

        with nc.Block() as block:
            @block.sync
            def _(sp):
                sp.dma_start(late_cst[:, :], consts[:, NEARLY:NCONST]).then_inc(late, 16)
                sp.wait_ge(late, 16)

        with nc.Fori(0, LAYERS) as layer:
            with nc.Block() as block:
                @block.gpsimd
                def _(pool):
                    for x in loop_sems:
                        pool.sem_clear(x)

            with nc.Block() as block:
                @block.sync
                def _(sp):
                    sp.dma_start(small[:, 0:NPAR2], par2[layer, :, :]).then_inc(L["lpar"], 16)
                    for u in range(26 + SLOTS):
                        ring.load(sp, w2[layer, u, :, :])

                @block.gpsimd
                def _(pool):
                    pool.memset(KZ2, 0.0).then_inc(L["lzero"], 1)
                    pool.memset(part(5120, 5184), 0.0).then_inc(L["lzero"], 1)
                    pool.memset(vcmp, 0.0).then_inc(L["lzero"], 1)
                    ring.subtract(pool, 2)
                    parts.subtract(pool, "pool", xnT)
                    ring.subtract(pool, 10)

                @block.scalar
                def _(act):
                    act.activation(sqL, hT, ACT.Square).then_inc(L["lsq"], 1)
                    b = banks.take(act, "ms")
                    banks.give(root_of_mean(act, b, D, std[:, 0:T]), "ms")
                    ring.round(act, 2)
                    parts.round(act, xnT, L["lxn"], 0)
                    for i in range(4):
                        ring.feed(act, ("in", i))
                        b = banks.take(act, ("in", i))
                        banks.give(act.activation(raw[:, 2 * i:2 * i + 2, :], two(b[:, :]), ACT.Copy), ("in", i))
                    ring.round(act, 12 - ring.at["act"])
                    b = banks.take(act, ("in", 4))
                    act.activation(sqc[:, 0:2, :], two(b[:, :]), ACT.Square).then_inc(L["lsqc"], 1)
                    banks.give(act.activation(cq, two(b[:, :]), ACT.Copy), ("in", 4))
                    b = banks.take(act, ("in", 5))
                    act.activation(sqc[:, 2, :], b[:, 0:T], ACT.Square).then_inc(L["lsqc"], 1)
                    banks.give(act.activation(ckr, two(b[:, :]), ACT.Copy), ("in", 5))
                    b = banks.take(act, "V")
                    banks.give(act.activation(V2, two(b[:, :]), ACT.Copy), "V")
                    b = banks.take(act, "G")
                    banks.give(act.activation(part(17216, 17264), b[:, 0:48], ACT.Sigmoid), "G")
                    b = banks.take(act, "msq")
                    act.wait_ge(L["lstep"], 1)
                    banks.give(root_of_mean(act, b, 256, std[:, 0:T]), "msq")
                    b = banks.take(act, "mskv")
                    banks.give(root_of_mean(act, b, 128, std[:, T:2 * T]), "mskv")
                    for i in range(4):
                        b = banks.take(act, ("uq", i))
                        banks.give(act.activation(qMr[:, 2 * i:2 * i + 2, :], two(b[:, :]), ACT.Copy), ("uq", i))
                    for t in range(TT):
                        b = banks.take(act, ("uv", t))
                        banks.give(act.activation(Vm[:, t, :], b[:, :], ACT.Copy), ("uv", t))
                    for k, n in enumerate(("ck", "cv")):
                        for c in range(2):
                            b = banks.take(act, (n, c))
                            banks.give(act.activation(hid[:, k, c, 0:30], b[:, 0:30], ACT.Silu), (n, c))

                @block.vector
                def _(dve):
                    link = Chain(dve, L["lstep"])
                    banks.wait_drained(dve, "ms")
                    link(dve.reciprocal(rst[:, 0:T], std[:, 0:T]))
                    dve.wait_ge(L["lpar"], 16)
                    for c in range(DC):
                        dve.scalar_tensor_tensor(xnT[:, c, :], hT[:, c, :], p2("attn")[:, c:c + 1], rst[:, 0:T],
                                                 ALU.mult, ALU.mult).then_inc(L["lxn"], 1)
                    parts.subtract(dve, "dve", xnT)

                    def rope(job, source, tag, outs):
                        n = source.shape[1]
                        cos, sin = (const(f + tag).rearrange("p (o t) -> p o t", o=1).broadcast_to([P, n, T])
                                    for f in ("cos", "sin"))
                        b = banks.take(dve, job)
                        dve.tensor_tensor(ra[:, 0:n, :], source, cos, ALU.mult).then_inc(L["lcopies"], 1)
                        banks.give(dve.tensor_tensor(rb[:, 0:n, :], two(b[:, 0:n * T]), sin, ALU.mult), job)
                        banks.wait_drained(dve, job)
                        ropes.append(1)
                        dve.wait_ge(L["lcopies"], len(ropes))
                        link(outs(ra[:, 0:n, :], rb[:, 0:n, :]))

                    ropes = []

                    def add_to(dst):
                        return lambda x, y: dve.tensor_tensor(dst, x, y, ALU.add)

                    def windows(k, source):
                        for g in range(2):
                            dve.tensor_copy(Z[0:64, k, g, :], source[64 * g:64 * g + 64, :])
                            ins = dve.tensor_copy(Z[64:128, k, g, 0:T - 1], source[64 * g:64 * g + 64, 1:T])
                        link(ins)
                        z = Z[:, k].rearrange("p g (i l two) -> p l g i two", l=8, two=2)[:, :, :, :, 0]
                        pos = p2("posk" if k == 0 else "posv")
                        for half in range(2):
                            add = pos[:, 8 * half:8 * half + 8].rearrange("p (l a b) -> p l a b", a=1, b=1)\
                                .broadcast_to([P, 8, 2, NCMP])
                            dve.tensor_tensor(X[:, k, 8 * half:8 * half + 8, 0:30].rearrange("p l (g i) -> p l g i", g=2),
                                              z[:, :, :, half:half + NCMP], add, ALU.add).then_inc(L["lX"], 1)

                    rope("rc", raw[:, 4:5, :], "A", add_to(kcr.rearrange("p (o t) -> p o t", o=1)))
                    dve.memset(Z[64:128, :, :, T - 1:T], 0.0)
                    windows(0, kcr)
                    banks.wait_drained(dve, ("in", 2))
                    windows(1, raw[:, 5, :])
                    banks.wait_drained(dve, "msq")
                    banks.wait_drained(dve, "mskv")
                    link(dve.reciprocal(rst[:, :], std[:, :]))
                    for c in range(2):
                        dve.scalar_tensor_tensor(cqn[:, c, :], cq[:, c, :], p2("qn")[:, c:c + 1], rst[:, 0:T],
                                                 ALU.mult, ALU.mult).then_inc(L["lcx"], 1)
                    dve.scalar_tensor_tensor(ckvn, ckr[:, 0, :], p2("kvn"), rst[:, T:2 * T],
                                             ALU.mult, ALU.mult).then_inc(L["lcx"], 1)
                    for i in range(2):
                        rope(("rp", i), raw[:, 2 * i:2 * i + 2, :], "A", add_to(qA[:, 2 * i:2 * i + 2, :]))
                    dve.wait_ge(L["lzero"], 3)

                    def split_keys(x, y):
                        for g in range(2):
                            r = slice(64 * g, 64 * g + 64)
                            for v in range(2):
                                ins = dve.tensor_tensor(KZ2[64 * v:64 * v + 64, :, g, v, :], x[r], y[r], ALU.add)
                        return ins

                    rope(("rp", 2), raw[:, 6:8, :], "A", split_keys)
                    rope("rk", ckr[:, 1:2, :], "B", add_to(kpe.rearrange("p (o t) -> p o t", o=1)))
                    kpe2 = kpe.rearrange("p (o t) -> p o t", o=1).broadcast_to([P, 2, T])
                    for i in range(4):
                        b = banks.take(dve, ("uk", i))
                        banks.give(dve.tensor_tensor(KM[:, 2 * i:2 * i + 2, :], two(b[:, :]), kpe2, ALU.add), ("uk", i))
                    for i in range(4):
                        rope(("rq", i), qMr[:, 2 * i:2 * i + 2, :], "B", add_to(qM[:, 2 * i:2 * i + 2, :]))
                    b = banks.take(dve, "k2")
                    src = b[0:64, 0:30].rearrange("p (g i) -> p g i", g=2)
                    dve.tensor_copy(KZC[0:64, :, 0, 0:NCMP], src)
                    banks.give(dve.tensor_copy(KZC[64:128, :, 1, 0:NCMP], src), "k2")
                    b = banks.take(dve, "v2")
                    banks.give(dve.tensor_copy(vcmp[0:NCMP], two(b[0:NCMP, 0:128], 64)), "v2")

                @block.tensor
                def _(pe):
                    sum_squares(pe, "ms", sqL, DC, (L["lsq"], 1))
                    parts.wait(pe)
                    for i in range(6):
                        linear(pe, ("in", i))
                    values(pe, "V", xnT)
                    bank = banks.open(pe, "G")
                    wg = p2("wg").rearrange("p (k n) -> p k n", k=DC)
                    for t in range(TT):
                        for k in range(DC):
                            ins = pe.matmul(bank[:, t * 24:(t + 1) * 24], xnT[:, k, t * P:(t + 1) * P], wg[:, k, :],
                                            start=(k == 0), stop=(k == DC - 1))
                    banks.close(ins, "G")

                    def rotate(job, matrix, source, after):
                        n = source.shape[1]
                        bank = banks.open(pe, job)
                        banks.wait_drained(pe, after)
                        banks.close(pe.matmul(bank[:, 0:n * T], const(matrix), source, start=True, stop=True), job)

                    rotate("rc", "rot64", raw[:, 4:5, :], ("in", 2))
                    sum_squares(pe, "msq", sqc, 2, (L["lsqc"], 1))
                    sum_squares(pe, "mskv", sqc[:, 2:3, :], 1, (L["lsqc"], 2))
                    for i in range(2):
                        rotate(("rp", i), "rot64", raw[:, 2 * i:2 * i + 2, :], ("in", i))
                    rotate(("rp", 2), "rot64", raw[:, 6:8, :], ("in", 3))
                    rotate("rk", "rot32", ckr[:, 1:2, :], ("in", 5))
                    pe.wait_ge(L["lcx"], 3)
                    for i in range(4):
                        if i % 2 == 0:
                            w = ring.unit(pe).rearrange("p (k n) -> p k n", k=2)
                        c = 2 * (i % 2) * P
                        linear_part(pe, ("uq", i), w, cqn, (c, c + P))
                    w = ring.unit(pe)
                    for i in range(4):
                        bank = banks.open(pe, ("uk", i))
                        for j in range(2):
                            ins = pe.matmul(bank[:, j * T:(j + 1) * T], w[:, (2 * i + j) * P:(2 * i + j + 1) * P], ckvn,
                                            start=True, stop=True)
                        banks.close(ins, ("uk", i))
                    w = ring.unit(pe)
                    for t in range(TT):
                        bank = banks.open(pe, ("uv", t))
                        banks.close(pe.matmul(bank[:, :], ckvn[:, t * P:(t + 1) * P], w[:, 0:512],
                                              start=True, stop=True), ("uv", t))
                    for k, n in enumerate(("ck", "cv")):
                        two_banks = [banks.open(pe, (n, c)) for c in range(2)]
                        pe.wait_ge(L["lX"], 2 * k + 2)
                        for part in range(4):
                            w = ring.unit(pe).rearrange("p (l n) -> p l n", n=T)
                            for lp in range(4):
                                for c in range(2):
                                    ins = pe.matmul(two_banks[c][:, 0:30], w[:, lp, c * P:(c + 1) * P],
                                                    X[:, k, 4 * part + lp, 0:30], start=(part + lp == 0),
                                                    stop=(part == 3 and lp == 3))
                                    if part == 3 and lp == 3:
                                        banks.close(ins, (n, c))
                            if part < 3:
                                ins.then_inc(ring.used, 1)
                    for i in range(4):
                        rotate(("rq", i), "rot32", qMr[:, 2 * i:2 * i + 2, :], ("uq", i))
                    banks.wait_drained(pe, ("cv", 1))
                    bank = banks.open(pe, "k2")
                    w2k = p2("w2k").rearrange("p (c n) -> p c n", c=2)
                    w2v = p2("w2v").rearrange("p (c n) -> p c n", c=2)
                    for c in range(2):
                        ins = pe.matmul(bank[0:64, 0:30], w2k[:, c, :], hid[:, 0, c, 0:30], start=(c == 0), stop=(c == 1))
                    banks.close(ins, "k2")
                    bank = banks.open(pe, "v2")
                    for g in range(2):
                        for c in range(2):
                            ins = pe.matmul(bank[0:NCMP, 64 * g:64 * g + 64], hid[:, 1, c, NCMP * g:NCMP * g + NCMP],
                                            w2v[:, c, :], start=(c == 0), stop=(c == 1))
                    banks.close(ins, "v2")

            with nc.Block() as block:
                @block.gpsimd
                def _(pool):
                    pool.memset(PTC, 0.0).then_inc(L["az"], 1)

                @block.vector
                def _(dve):
                    link = Chain(dve, L["avec"])
                    b = banks.take(dve, "sc")
                    bc = b[:, 0:TT * 8 * NCMP].rearrange("p (t h i) -> p t h i", t=TT, h=8)
                    S = Sc[:, :, :, 0:NCMP]
                    for t in range(TT):
                        add = const("cmp_add")[:, 16 * t:16 * t + NCMP].rearrange("p (o i) -> p o i", o=1)\
                            .broadcast_to([P, 8, NCMP])
                        ins = dve.scalar_tensor_tensor(S[:, t], bc[:, t], 64 ** -0.5, add, ALU.mult, ALU.add)
                    banks.give(ins, "sc")
                    banks.wait_drained(dve, "sc")
                    link(dve.tensor_reduce(stc[:, 0], S, AX.X, ALU.max))
                    for t in range(TT):
                        ins = dve.tensor_tensor(S[:, t], S[:, t], bcast(stc[:, 0, t], NCMP), ALU.subtract)
                        ins.then_inc(L["acv"], 1)

                    def compressed():
                        dve.wait_ge(L["acx"], TT)
                        for t in range(TT):
                            mul = const("cmp_mul")[:, 16 * t:16 * t + NCMP].rearrange("p (o i) -> p o i", o=1)\
                                .broadcast_to([P, 8, NCMP])
                            ins = dve.tensor_tensor(S[:, t], S[:, t], mul, ALU.mult)
                        link(ins)
                        link(dve.tensor_reduce(stc[:, 1], S, AX.X, ALU.add))
                        link(dve.tensor_scalar(stc[:, 1], stc[:, 1], 1e-30, None, ALU.max))
                        link(dve.reciprocal(stc[:, 2], stc[:, 1]))
                        link(dve.tensor_tensor(stc[:, 2], stc[:, 2], GA[:, :, :, 0], ALU.mult))
                        for t in range(TT):
                            dve.tensor_tensor(S[:, t], S[:, t], bcast(stc[:, 2, t], NCMP), ALU.mult).then_inc(L["acp"], 1)

                    for t in range(TT):
                        w = P * (t + 1)
                        attention_vector_scores(
                            dve, SA0, SA1, 12, lambda c: (64 if c < 8 else 96) ** -0.5,
                            lambda t, c: const("mask1")[:, P * (1 - t):T].rearrange("p (o s) -> p o s", o=1)
                            .broadcast_to([P, 2, P * (t + 1)]), "s2", t)
                        dve.tensor_reduce(NM2[:, t, :], (SA0, SA1)[t], AX.X, ALU.max, negate=True)\
                            .then_inc(L["amx"], 1)
                    compressed()
                    for t in range(TT):
                        S2 = (SA0, SA1)[t]
                        dve.wait_ge(L["aden"], 24 * (t + 1))
                        link(dve.reciprocal(RC2[:, t, :], DEN2[:, t, :]))
                        dve.tensor_tensor(RC2[:, t, 0:8], RC2[:, t, 0:8], GA[:, t, :, 1], ALU.mult)
                        link(dve.tensor_tensor(RC2[:, t, 8:16], RC2[:, t, 8:16], GA[:, t, :, 2], ALU.mult))
                        dve.tensor_tensor(S2, S2, bcast(RC2[:, t, :], P * (t + 1)), ALU.mult).then_inc(L["ap"], 1)

                @block.scalar
                def _(act):
                    act.wait_ge(L["acv"], TT)
                    for t in range(TT):
                        act.activation(Sc[:, t, :, 0:NCMP], Sc[:, t, :, 0:NCMP], ACT.Exp).then_inc(L["acx"], 1)
                    for t in range(TT):
                        S2 = (SA0, SA1)[t]
                        act.wait_ge(L["amx"], t + 1)
                        for hd in range(24):
                            act.activation(S2[:, hd, :], S2[:, hd, :], ACT.Exp, bias=NM2[:, t, hd:hd + 1],
                                           accum_out=DEN2[:, t, hd:hd + 1]).then_inc(L["aden"], 1)
                    act.wait_ge(L["az"], 1)

                    def output(c):
                        b = banks.take(act, ("o2", c))
                        banks.give(act.activation(aT[:, c, :], b[:, 0:T], ACT.Copy), ("o2", c))

                    for c, (tc, heads) in enumerate(pair_jobs):
                        for job in tc:
                            b = banks.take(act, job)
                            banks.give(act.activation(PTC[0:NCMP, 2 * c:2 * c + 2, :], two(b[0:NCMP, :]), ACT.Copy), job)
                        for hd in heads:
                            b = banks.take(act, ("t2", hd))
                            banks.give(act.activation(PTR[:, slot[hd], :], b[:, 0:384], ACT.Copy), ("t2", hd))
                        if c:
                            output(c - 1)
                    output(7)

                @block.tensor
                def _(pe):
                    bank = banks.open(pe, "sc")
                    for t in range(TT):
                        for c in range(4):
                            a = (t * 8 + 2 * c) * NCMP
                            ins = pe.matmul(bank[:, a:a + 2 * NCMP], qA[:, c, t * P:(t + 1) * P],
                                            KZC[:, c // 2, :, 0:NCMP], start=True, stop=True)
                    banks.close(ins, "sc")
                    pairs = [((qA[:, c % 4, :],), (KZ2[:, c // 4, (c % 4) // 2],)) for c in range(8)]
                    pairs += [((qM[:, 2 * c, :], qM[:, 2 * c + 1, :]), (KM[:, 2 * c, :], KM[:, 2 * c + 1, :]))
                              for c in range(4)]
                    attention_tensor_scores(pe, pairs, "s2")
                    pe.wait_ge(L["acp"], TT)
                    pe.wait_ge(L["ap"], TT)
                    for c, (tc, heads) in enumerate(pair_jobs):
                        for job in tc:
                            bank = banks.open(pe, job)
                            for j in range(2):
                                for t in range(TT):
                                    a = (2 * j + t) * P
                                    ins = pe.transpose(bank[0:NCMP, a:a + P], Sc[:, t, 2 * c + j, 0:NCMP], const("ident"))
                            banks.close(ins, job)
                        for hd in heads:
                            attention_tensor_transposes(pe, SA0, SA1, hd, "t2")
                        for hd in heads:
                            banks.wait_drained(pe, ("t2", hd))
                        bank = banks.open(pe, ("o2", c))
                        for j in range(2):
                            rows = slice(64 * j, 64 * j + 64)
                            own = [hd for hd in heads if hd % 2 == j]
                            if c < 4:
                                banks.wait_drained(pe, ("tc", c))
                                pe.matmul(bank[rows, 0:T], vcmp[:, c // 2, :], PTC[:, 2 * c + j, :],
                                          start=True, stop=False)
                            for n, hd in enumerate(own):
                                if c < 4:
                                    col = P * (hd // 8) + 64 * (c // 2)
                                    v = V2[:, :, col:col + 64]
                                else:
                                    v = Vm[:, :, 64 * (hd - 16):64 * (hd - 15)]
                                pe.matmul(bank[rows, 0:T], v[:, 0, :], PTR[:, slot[hd], 0:T],
                                          start=(c >= 4), stop=False)
                                ins = pe.matmul(bank[rows, P:T], v[:, 1, :], PTR[:, slot[hd], T:384],
                                                start=False, stop=(n == len(own) - 1))
                        banks.close(ins, ("o2", c))

            upper.close()
            hidden_parts = ctx.enter_context(ExitStack())
            hidden_hi, hidden_lo = (
                hidden_parts.enter_context(nc.sbuf_tensor(n, [P, FF * T // P], F32R))[:, :]
                .rearrange("p (c t) -> p c t", t=T) for n in ("hidden_hi", "hidden_lo"))
            with nc.Block() as block:
                @block.sync
                def _(sp):
                    while ring.issued < LAYER_UNITS:
                        ring.load(sp, w2[layer, ring.issued, :, :])

                @block.gpsimd
                def _(pool):
                    ring.subtract(pool, 2)
                    parts.subtract(pool, "pool", mixT)
                    ring.subtract(pool, 8)
                    parts.subtract(pool, "pool", fx)
                    ring.subtract(pool)

                @block.scalar
                def _(act):
                    act.activation(sqo, aT, ACT.Square).then_inc(L["fsq"], 1)
                    ring.round(act, 2)
                    for k in range(2):
                        b = banks.take(act, f"mo{k}")
                        banks.give(root_of_mean(act, b, 512, std[:, T * k:T * k + T]), f"mo{k}")
                    parts.round(act, mixT, L["fmix"], 0)
                    for i in range(4):
                        ring.feed(act, ("wo", i))
                        banks.wait_drained(act, ("wo", i))
                        act.activation(sqo[:, 2 * i:2 * i + 2, :], hT[:, 2 * i:2 * i + 2, :], ACT.Square)\
                           .then_inc(L["fsq2"], 1)
                    b = banks.take(act, "mf")
                    act.wait_ge(L["fmix"], DC)
                    banks.give(root_of_mean(act, b, D, std[:, 0:T]), "mf")
                    parts.round(act, fx, L["fxn2"], 0)
                    for i in range(16):
                        ring.feed(act, ("f1", i))
                        b = banks.take(act, ("f1", i))
                        if i >= 2:
                            act.wait_ge(L["fsqr"], i - 1)
                        banks.give(act.activation(relu[:, i % 2], two(b[:, :]), ACT.Relu), ("f1", i))
                    ring.round(act, FF2_UNITS)

                @block.vector
                def _(dve):
                    link = Chain(dve, L["fvec"])
                    for k in range(2):
                        banks.wait_drained(dve, f"mo{k}")
                    link(dve.reciprocal(rst[:, :], std[:, :]))
                    for k, n in enumerate(("nsa", "mla")):
                        for c in range(4):
                            dve.scalar_tensor_tensor(mixT[:, 4 * k + c, :], aT[:, 4 * k + c, :], p2(n)[:, c:c + 1],
                                                     rst[:, T * k:T * k + T], ALU.mult, ALU.mult).then_inc(L["fmix"], 1)
                    parts.subtract(dve, "dve", mixT)
                    for i in range(4):
                        b = banks.take(dve, ("wo", i))
                        banks.give(dve.tensor_tensor(hT[:, 2 * i:2 * i + 2, :], hT[:, 2 * i:2 * i + 2, :], two(b[:, :]),
                                                     ALU.add), ("wo", i))
                    banks.wait_drained(dve, "mf")
                    dve.wait_ge(L["fmix"], DC)
                    link(dve.reciprocal(rst[:, 0:T], std[:, 0:T]))
                    for c in range(DC):
                        dve.scalar_tensor_tensor(fx[:, c, :], hT[:, c, :], p2("mlp")[:, c:c + 1], rst[:, 0:T],
                                                 ALU.mult, ALU.mult).then_inc(L["fxn2"], 1)
                    parts.subtract(dve, "dve", fx)
                    for i in range(16):
                        banks.wait_drained(dve, ("f1", i))
                        if i:
                            dve.wait_ge(L["fhid"], i)
                        dve.tensor_tensor(squared, relu[:, i % 2], relu[:, i % 2], ALU.mult).then_inc(L["fsqr"], 1)
                        dve.wait_ge(L["fsqr"], i + 1)
                        pair = slice(2 * i, 2 * i + 2)
                        dve.tensor_copy(hidden_hi[:, pair, :], squared).then_inc(L["fhigh"], 1)
                        dve.wait_ge(L["fhigh"], i + 1)
                        dve.tensor_tensor(hidden_lo[:, pair, :], squared, hidden_hi[:, pair, :].bitcast(F32),
                                          ALU.subtract).then_inc(L["fhid"], 1)
                    for b in range(4):
                        bank = banks.take(dve, ("f2", b))
                        banks.give(dve.tensor_tensor(hT[:, 2 * b:2 * b + 2, :], hT[:, 2 * b:2 * b + 2, :], two(bank[:, :]),
                                                     ALU.add), ("f2", b))

                @block.tensor
                def _(pe):
                    for k in range(2):
                        sum_squares(pe, f"mo{k}", sqo[:, 4 * k:4 * k + 4, :], 4, (L["fsq"], 1))
                    parts.wait(pe)
                    for i in range(4):
                        linear(pe, ("wo", i))
                    sum_squares(pe, "mf", sqo, DC, (L["fsq2"], 4))
                    parts.wait(pe)
                    for i in range(16):
                        linear(pe, ("f1", i))
                    out_banks = [banks.open(pe, ("f2", b)) for b in range(4)]
                    for u in range(FF2_UNITS):
                        w = ring.high(pe)
                        pe.wait_ge(L["fhid"], u // 2 + 1)
                        for c in range(DC):
                            out_c = out_banks[c // 2][:, (c % 2) * T:(c % 2 + 1) * T]
                            pe.matmul(out_c, w[:, c * P:(c + 1) * P], hidden_hi[:, u, :],
                                      start=(u == 0 and c % 2 == 0), stop=False, skip_group_check=True)
                            pe.matmul(out_c, w[:, c * P:(c + 1) * P], hidden_lo[:, u, :], start=False, stop=False,
                                      skip_group_check=True)
                        w = ring.low(pe)
                        for c in range(DC):
                            ins = pe.matmul(out_banks[c // 2][:, (c % 2) * T:(c % 2 + 1) * T],
                                            w[:, c * P:(c + 1) * P], hidden_hi[:, u, :],
                                            start=False, stop=(u == FF2_UNITS - 1), skip_group_check=True)
                            if u == FF2_UNITS - 1 and c % 2:
                                banks.close(ins, ("f2", c // 2))
                        if u < FF2_UNITS - 1:
                            ins.then_inc(ring.used, 1)

        e_sq, e_ms, e_std, e_rst, e_y, e_out = (sem(n) for n in ("end_sq", "end_ms", "end_std", "end_rst", "end_y", "end_out"))
        with nc.Block() as block:
            @block.scalar
            def _(act):
                act.activation(sqo, hT, ACT.Square).then_inc(e_sq, 1)
                act.wait_ge(e_ms, 1)
                root_of_mean(act, psum[0], D, std[:, 0:T]).then_inc(e_std, 1)

            @block.tensor
            def _(pe):
                pe.wait_ge(e_sq, 1)
                for c in range(DC):
                    ins = pe.matmul(psum[0][:, 0:T], const("ones"), sqo[:, c, :], start=(c == 0), stop=(c == DC - 1))
                ins.then_inc(e_ms, 1)

            @block.vector
            def _(dve):
                dve.wait_ge(e_std, 1)
                dve.reciprocal(rst[:, 0:T], std[:, 0:T]).then_inc(e_rst, 1)
                dve.wait_ge(e_rst, 1)
                for c in range(DC):
                    dve.scalar_tensor_tensor(fx[:, c, :], hT[:, c, :], par("final")[:, c:c + 1], rst[:, 0:T],
                                             ALU.mult, ALU.mult).then_inc(e_y, 1)

            @block.sync
            def _(sp):
                for half in range(2):
                    sp.wait_ge(e_y, DC // 2 * (half + 1))
                    cols = slice(half * D, (half + 1) * D)
                    sp.dma_start(out[:, cols], fx[:, half * DC // 2:(half + 1) * DC // 2, :]).then_inc(e_out, 16)
                sp.wait_ge(e_out, 32)


def _blocks(w, k, n):
    rows, cols = w.shape
    return w.reshape(k, P, cols // n, n).transpose(2, 1, 0, 3).reshape(cols // n, P, k * n)


def _tall(v):
    return v.reshape(-1, P).T


def _constants():
    c = np.zeros((P, NCONST), np.float32)

    def put(name, a):
        lo, hi = CONST[name]
        c[:a.shape[0], lo:lo + a.shape[1]] = a

    i = np.arange(P)
    put("ones", np.ones((P, P)))
    put("blk64", (i[:, None] // 64 == i[None, :] // 64).astype(np.float32))
    put("ident", np.eye(P))
    for name, dim, starts in (("rot64", 64, (0, 64)), ("rot32", 32, (64,))):
        r = np.zeros((P, P), np.float32)
        for s in starts:
            for d in range(dim // 2):
                r[s + d + dim // 2, s + d] = -1.0
                r[s + d, s + d + dim // 2] = 1.0
        put(name, r)
    for tag, dim, starts in (("A", 64, (0, 64)), ("B", 32, (64,))):
        inv = (np.float32(1.0) / (np.float32(10000.0) ** (np.arange(0, dim, 2, dtype=np.float32) / np.float32(dim))))
        ang = np.arange(T, dtype=np.float32)[:, None] * inv.astype(np.float32)[None, :]
        ang = np.concatenate([ang, ang], axis=-1).T
        cos, sin = np.ones((P, T), np.float32), np.zeros((P, T), np.float32)
        for s in starts:
            cos[s:s + dim], sin[s:s + dim] = np.cos(ang), np.sin(ang)
        put("cos" + tag, cos)
        put("sin" + tag, sin)
    put("mask1", np.concatenate([np.zeros((P, P)), np.where(i[None, :] <= i[:, None], 0.0, NEG)], axis=1))
    end = np.arange(NCMP) * 16 + 31
    ok = np.stack([end[None, :] <= (i[:, None] + P * t) for t in range(TT)], axis=1)
    wide = np.zeros((P, TT, 16), np.float32)
    wide[:, :, :NCMP] = np.where(ok, 0.0, NEG)
    put("cmp_add", wide.reshape(P, 32).copy())
    wide[:, :, :NCMP] = ok
    put("cmp_mul", wide.reshape(P, 32))
    put("time", np.tile(np.arange(T, dtype=np.float32), (P, 1)))
    put("lane", np.tile(i.astype(np.float32), (P, 1)))
    return c


def _lay(inputs):
    a = {k: np.asarray(v) for k, v in inputs.items()}
    f = np.float32
    out = {}
    out["xT"] = a["x"][0].T.reshape(DC, P, T).transpose(1, 0, 2).reshape(P, DC * T)
    out["consts"] = _constants()

    par = np.zeros((P, NPAR1), f)

    def put(name, v, table=PAR1, dst=None):
        lo, hi = table[name]
        (par if dst is None else dst)[:, lo:lo + v.shape[1]] = v

    put("ln1", _tall(a["ln1_g"][0]))
    put("ln2", _tall(a["ln2_g"][0]))
    put("bgate", _tall(a["b_gate"][0]))
    for name, key in (("lre", "s5_lambda_re"), ("lim", "s5_lambda_im")):
        put(name, a[key][0].reshape(SC, P).T)
    put("lstep", np.repeat(a["s5_log_step"][0].reshape(SC, 2), 64, axis=1).T)
    put("dskip", _tall(a["s5_d"][0].reshape(-1)))
    put("gq", np.tile(a["q_norm_g"][0], 2)[:, None])
    put("gk", np.tile(a["k_norm_g"][0], 2)[:, None])
    put("sinks", np.tile(a["attn_sinks"][0], (P, 1)))
    put("final", _tall(a["final_norm_2"]))
    cs = np.stack([a["s5_c_re"][0], a["s5_c_im"][0]], axis=1)
    cs = cs.reshape(SC, 2, 2, 16, 64).transpose(1, 4, 0, 2, 3).reshape(P, SC * 32)
    put("cs5", cs)
    out["par1"] = par

    dist = np.arange(P)[:, None] + P - np.arange(2 * P)[None, :]
    d = np.maximum(dist, 0)
    d_f = np.maximum(d, 1).astype(f)
    large = 16 + (np.log(d_f / f(16)) / f(np.log(8.0)) * f(16)).astype(np.int32)
    bucket = np.where(d < 16, d, np.minimum(large, 31))
    table = a["rel_bias_table"][bucket].transpose(0, 2, 1)
    ok = (dist >= 0) & (dist < 128)
    out["bias1"] = np.where(ok[:, None, :], table, f(NEG)).reshape(P, NH * T)

    bs = np.zeros((UC, 4, 2, P, P), f)
    for k, key in enumerate(("s5_b_re", "s5_b_im")):
        b = a[key][0]
        for g in range(G1):
            sc, half = g // 2, g % 2
            uc, q = sc // 4, sc % 4
            r0 = 32 * q + 16 * half
            bs[uc, q, k, r0:r0 + 16, 64 * half:64 * half + 64] = b[g].T
    bs = bs.transpose(0, 3, 1, 2, 4).reshape(UC, P, SLOT)
    glu = _blocks(a["s5_w_glu"][0], 4, 256)
    out["w1"] = np.concatenate([
        _blocks(a["w_in"][0], DC, P), bs, glu[2:], glu[:2], _blocks(a["w_attn_branch"][0], DC, P),
        _blocks(a["w_s5_branch"][0], 4, 256), _blocks(a["w_out"][0], DC, P),
        _blocks(a["peer_w_query"][0], DC, P)])
    sk = a["peer_sub_keys"][0]
    keys = np.zeros((2, 64, PH, 2, NSUB), f)
    for k in range(2):
        keys[k, :, :, k, :] = sk[:, k].transpose(2, 0, 1)
    out["keys"] = keys.reshape(P, PH * T)
    u = a["peer_u"][0].reshape(NSUB, NE2, DC, P)
    out["wu"] = np.ascontiguousarray(u.transpose(1, 3, 2, 0)).reshape(NE2, P, SLOT)
    v = a["peer_v"][0].reshape(NSUB, NE2, SLOT)
    out["wv"] = np.ascontiguousarray(v.transpose(1, 0, 2))
    _lay_layers(a, out)
    return {k: np.ascontiguousarray(v, dtype=v.dtype) for k, v in out.items()}


def _lay_layers(a, out):
    f = np.float32
    pars, units = [], []
    for l in range(LAYERS):
        par = np.zeros((P, NPAR2), f)

        def put(name, v):
            lo, hi = PAR2[name]
            par[:, lo:lo + v.shape[1]] = v

        for name, key in (("attn", "attn_norm_2"), ("mlp", "mlp_norm_2"), ("qn", "mla_q_norm_2"),
                          ("kvn", "mla_kv_norm_2"), ("nsa", "nsa_out_norm_2"), ("mla", "mla_out_norm_2")):
            put(name, _tall(a[key][l]))
        for name, key in (("posk", "cmp_pos_k_2"), ("posv", "cmp_pos_v_2")):
            put(name, a[key][l].reshape(16, P).T)
        for name, key in (("w2k", "cmp_w2_k_2"), ("w2v", "cmp_w2_v_2")):
            put(name, a[key][l].reshape(2, P, 64).transpose(1, 0, 2).reshape(P, 128))
        w = a["w_in_2"][l]
        q, kc, vc, ks, vs, kw, vw, g, cq, ckv, kr = np.split(w, np.cumsum([512] + [128] * 6 + [24, 256, 128]), axis=1)
        put("wg", g.reshape(DC, P, 24).transpose(1, 0, 2).reshape(P, DC * 24))
        krp = np.zeros((D, P), f)
        krp[:, 64:96] = kr
        w_in = np.concatenate([q, kc, vc, ks, kw, cq, ckv, krp, vs, vw], axis=1)
        wq = np.zeros((256, 8, P), f)
        wq[:, :, :96] = a["w_q_up_2"][l].reshape(256, 8, 96)
        wkv = a["w_kv_up_2"][l].reshape(P, 8, P)
        up = np.zeros((2, P, SLOT), f)
        up[0].reshape(P, 8, P)[:, :, :64] = wkv[:, :, :64]
        up[1, :, 0:512] = wkv[:, :, 64:].reshape(P, 512)
        tall = [a[k][l].reshape(-1, SLOT // a[k].shape[2], P, a[k].shape[2]).transpose(0, 2, 1, 3).reshape(-1, P, SLOT)
                for k in ("cmp_w1_k_2", "cmp_w1_v_2", "w_ff2_2")]
        units.append(np.concatenate([
            _blocks(w_in, DC, P), _blocks(wq.reshape(256, 1024), 2, 512), up, tall[0], tall[1],
            _blocks(a["w_out_2"][l], DC, P), _blocks(a["w_ff1_2"][l], DC, P), tall[2]]))
        pars.append(par)
    out["par2"] = np.stack(pars)
    out["w2"] = np.stack(units)


_INS = ["xT", "consts", "par1", "bias1", "w1", "keys", "wu", "wv", "par2", "w2"]


def kernel(**inputs):
    import concourse.bacc as _bacc
    from concourse.bass_utils import run_bass_kernel_spmd as _run

    arrays = _lay(inputs)
    nc = _bacc.Bacc("TRN2", target_bir_lowering=False, num_devices=1)
    args = [nc.dram_tensor(n, arrays[n].shape, mybir.dt.from_np(arrays[n].dtype), kind="ExternalInput").ap() for n in _INS]
    out = nc.dram_tensor("yT", (P, DC * T), F32, kind="ExternalOutput").ap()
    build(nc, None, *args, out)
    r = _run(nc, [{n: arrays[n] for n in _INS}], core_ids=[0])
    y = np.asarray(r.results[0]["yT"]).reshape(P, DC, T).transpose(2, 1, 0).reshape(1, T, D)
    return y
```

```python
import numpy as np
import concourse.bass as bass
from concourse import mybir
from contextlib import ExitStack

F32 = mybir.dt.float32
U32 = mybir.dt.uint32
F32R = mybir.dt.float32r
ALU = mybir.AluOpType
ACT = mybir.ActivationFunctionType
AX = mybir.AxisListType

P = 128
T = 256
TT = T // P
D = 1024
DC = D // P
EPS = 1e-6
NEG = -1e30

SLOTS = 4
SLOT = 1024

G1 = 32
SC = 16
UC = 4

NH, NKV, HD = 16, 4, 64

PH, TOPK, NSUB = 8, 16, 128
NE2 = NSUB

LAYERS = 2
NCMP = 15
FF = 4096
FC = FF // P
IN2_UNITS, UP_UNITS, CMP_UNITS, OUT_UNITS, FF1_UNITS, FF2_UNITS = 14, 4, 8, 8, 32, 32
LAYER_UNITS = IN2_UNITS + UP_UNITS + CMP_UNITS + OUT_UNITS + FF1_UNITS + FF2_UNITS

CONST = {}
_at = 0
for _name, _n in [("ones", 128), ("blk64", 128), ("ident", 128), ("time", 256), ("lane", 128), ("rot64", 128),
                  ("rot32", 128), ("cosA", 256), ("sinA", 256), ("cosB", 256), ("sinB", 256),
                  ("mask1", 256), ("cmp_add", 32), ("cmp_mul", 32)]:
    CONST[_name] = (_at, _at + _n)
    _at += _n
NCONST = _at
NEARLY = CONST["rot64"][0]
ARENA = 32768

PAR1 = {}
_at = 0
for _name, _n in [("ln1", 8), ("ln2", 8), ("bgate", 16), ("lre", SC), ("lim", SC), ("lstep", SC),
                  ("dskip", UC), ("gq", 1), ("gk", 1), ("sinks", NH), ("final", 8), ("cs5", SC * 2 * 16)]:
    PAR1[_name] = (_at, _at + _n)
    _at += _n
NPAR1 = _at

PAR2 = {}
_at = 0
for _name, _n in [("attn", 8), ("mlp", 8), ("qn", 2), ("kvn", 1), ("nsa", 4), ("mla", 4), ("posk", 16),
                  ("posv", 16), ("w2k", 128), ("w2v", 128), ("wg", DC * 24)]:
    PAR2[_name] = (_at, _at + _n)
    _at += _n
NPAR2 = _at


class Banks:

    def __init__(self, full, drained, tensors):
        self.full, self.drained, self.tensors = full, drained, tensors
        self.reset()

    def reset(self):
        self.turn, self.done, self.jobs = 0, [0] * 8, {}

    def plan(self, names, over=tuple(range(8))):
        for n in names:
            b = over[self.turn % len(over)]
            self.turn += 1
            self.jobs[n] = (b, self.done[b])
            self.done[b] += 1

    def open(self, pe, name):
        b, before = self.jobs[name]
        if before:
            pe.wait_ge(self.drained[b], before)
        return self.tensors[b]

    def close(self, ins, name):
        ins.then_inc(self.full[self.jobs[name][0]], 1)

    def take(self, eng, name):
        b, before = self.jobs[name]
        eng.wait_ge(self.full[b], before + 1)
        return self.tensors[b]

    def give(self, ins, name):
        ins.then_inc(self.drained[self.jobs[name][0]], 1)

    def wait_drained(self, eng, name):
        b, before = self.jobs[name]
        eng.wait_ge(self.drained[b], before + 1)


class Ring:

    def __init__(self, loaded, used, rounded, rest, slots, hi, lo):
        self.loaded, self.used, self.rounded, self.rest = loaded, used, rounded, rest
        self.slots, self.hi, self.lo = slots, hi, lo
        self.reset()

    def reset(self):
        self.issued = self.taken = self.marks = 0
        self.last, self.number, self.order, self.unit_of = [], [], [], {}
        self.at = {"act": 0, "pool": 0}

    def plan(self, banks, jobs, split=False):
        for j in jobs:
            if j is None:
                self.marks += 1
                self.last.append((self.used, self.marks))
            elif not isinstance(j, str) and not isinstance(j[0], str):
                self.last.append(j)
            else:
                b, before = banks.jobs[j]
                self.unit_of[j] = len(self.last)
                self.last.append((banks.full[b], before + 1))
            self.number.append(len(self.order) if split else None)
            if split:
                self.order.append(len(self.last) - 1)

    def load(self, sp, source):
        u, s = self.issued, self.issued % SLOTS
        if u >= SLOTS:
            n = self.number[u - SLOTS]
            if n is None:
                sp.wait_ge(*self.last[u - SLOTS])
            else:
                sp.wait_ge(self.rest, n + 1)
        sp.dma_start(self.slots[:, s, :], source).then_inc(self.loaded[s], 16)
        self.issued += 1

    def round(self, act, count):
        for n in range(self.at["act"], min(self.at["act"] + count, len(self.order))):
            u = self.order[n]
            act.wait_ge(self.loaded[u % SLOTS], 16 * (u // SLOTS + 1))
            if n >= 2:
                act.wait_ge(*self.last[self.order[n - 2]])
            act.activation(self.hi[:, n % 2, :], self.slots[:, u % SLOTS, :], ACT.Copy).then_inc(self.rounded, 1)
            self.at["act"] = n + 1

    def feed(self, act, job):
        upto = self.unit_of[job] + 2
        self.round(act, sum(1 for u in self.order[self.at["act"]:] if u <= upto))

    def subtract(self, pool, count=None):
        end = len(self.order) if count is None else self.at["pool"] + count
        for n in range(self.at["pool"], end):
            pool.wait_ge(self.rounded, n + 1)
            if n >= 2:
                pool.wait_ge(*self.last[self.order[n - 2]])
            pool.tensor_tensor(self.lo[:, n % 2, :], self.slots[:, self.order[n] % SLOTS, :],
                               self.hi[:, n % 2, :].bitcast(F32), ALU.subtract).then_inc(self.rest, 1)
        self.at["pool"] = end

    def unit(self, pe):
        u, s = self.taken, self.taken % SLOTS
        pe.wait_ge(self.loaded[s], 16 * (u // SLOTS + 1))
        self.taken += 1
        return self.slots[:, s, :]

    def high(self, pe):
        n = self.number[self.taken]
        pe.wait_ge(self.rounded, n + 1)
        return self.hi[:, n % 2, :]

    def low(self, pe):
        n = self.number[self.taken]
        self.taken += 1
        pe.wait_ge(self.rest, n + 1)
        return self.lo[:, n % 2, :]


class Parts:

    def __init__(self, hi, lo_pool, lo_dve, high, low):
        self.sem_hi, self.sem_pool, self.sem_dve, self.high, self.low = hi, lo_pool, lo_dve, high, low
        self.reset()

    def reset(self):
        self.turn = {"act": 0, "pool": 0, "dve": 0, "pe": 0}

    def round(self, act, source, ready, before, chunks=1):
        for c in range(0, DC, chunks):
            act.wait_ge(ready, before + c // chunks + 1)
            act.activation(self.high[:, c:c + chunks, :], source[:, c:c + chunks, :], ACT.Copy)\
               .then_inc(self.sem_hi, chunks)
        self.turn["act"] += 1

    def subtract(self, eng, who, source):
        sem = self.sem_pool if who == "pool" else self.sem_dve
        for c in range(0, DC // 2) if who == "pool" else range(DC // 2, DC):
            eng.wait_ge(self.sem_hi, DC * self.turn[who] + 2 * (c // 2) + 2)
            eng.tensor_tensor(self.low[:, c, :], source[:, c, :], self.high[:, c, :].bitcast(F32), ALU.subtract)\
               .then_inc(sem, 1)
        self.turn[who] += 1

    def wait_high(self, pe):
        self.turn["pe"] += 1
        pe.wait_ge(self.sem_hi, DC * self.turn["pe"])

    def wait_low(self, pe):
        pe.wait_ge(self.sem_pool, DC // 2 * self.turn["pe"])
        pe.wait_ge(self.sem_dve, DC // 2 * self.turn["pe"])


class Chain:

    def __init__(self, eng, sem, start=0):
        self.eng, self.sem, self.n = eng, sem, start

    def __call__(self, ins):
        self.n += 1
        ins.then_inc(self.sem, 1)
        self.eng.wait_ge(self.sem, self.n)


def build(nc, stop_after, xT, consts, par1, bias1, w1, keys, wu, wv, par2, w2, out):
    ctx = ExitStack()
    with ctx:
        def sb(name, cols, dt=F32):
            return ctx.enter_context(nc.sbuf_tensor(name, [P, cols], dt))

        def sem(name):
            return ctx.enter_context(nc.semaphore(name))

        h = sb("h", DC * T)
        slots = sb("slots", SLOTS * SLOT)
        cst = sb("cst", NEARLY)
        p1 = sb("p1", NPAR1)
        small = sb("small", 2304)
        xh, xl = sb("xh", DC * T, F32R), sb("xl", DC * T, F32R)
        wh, wl = sb("wh", 2 * SLOT, F32R), sb("wl", 2 * SLOT, F32R)
        eps, std, rst = sb("eps", 4), sb("std", 512), sb("rst", 512)
        memory = ctx.enter_context(ExitStack())
        arena = memory.enter_context(nc.sbuf_tensor("arena", [P, ARENA], F32))
        xhT, xlT = (x[:, :].rearrange("p (c t) -> p c t", t=T) for x in (xh, xl))
        whv, wlv = (x[:, :].rearrange("p (b n) -> p b n", b=2) for x in (wh, wl))

        hT = h[:, :].rearrange("p (c t) -> p c t", t=T)
        slots_v = slots[:, :].rearrange("p (s n) -> p s n", s=SLOTS)

        def const(name):
            a, b = CONST[name]
            return cst[:, a:b] if b <= NEARLY else late_cst[:, a - NEARLY:b - NEARLY]

        def par(name, table=PAR1):
            a, b = table[name]
            return (p1 if table is PAR1 else small)[:, a:b]

        ps = ctx.enter_context(nc.psum_tensor("ps", [P, 8 * 512], F32))
        psum = [ps[:, 512 * b:512 * b + 512] for b in range(8)]
        banks = Banks([sem(f"full{b}") for b in range(8)], [sem(f"drained{b}") for b in range(8)], psum)
        ring = Ring([sem(f"loaded{s}") for s in range(SLOTS)], sem("used"), sem("rounded"), sem("rest"),
                    slots_v, whv, wlv)
        parts = Parts(sem("parts_hi"), sem("parts_lo_pool"), sem("parts_lo_dve"), xhT, xlT)

        def part(a, b):
            return arena[:, a:b]

        def view(at, *dims):
            v = part(at, at + int(np.prod(dims)))
            if len(dims) == 2:
                return v.rearrange("p (a b) -> p a b", b=dims[1])
            if len(dims) == 3:
                return v.rearrange("p (a b c) -> p a b c", b=dims[1], c=dims[2])
            return v

        def two(ap, w=T):
            return ap.rearrange("p (a b) -> p a b", b=w)

        def sum_squares(pe, name, squares, chunks, ready=None, matrix="ones"):
            bank = banks.open(pe, name)
            if ready:
                pe.wait_ge(*ready)
            for c in range(chunks):
                ins = pe.matmul(bank[:, 0:T], const(matrix), squares[:, c, :],
                                start=(c == 0), stop=(c == chunks - 1))
            banks.close(ins, name)

        def linear(pe, name, fresh=False):
            if fresh:
                parts.wait_high(pe)
            bank = banks.open(pe, name)
            for j in range(2):
                out = bank[:, j * T:(j + 1) * T]
                w = ring.high(pe).rearrange("p (k n) -> p k n", k=DC)
                for k in range(DC):
                    pe.matmul(out, w[:, k, :], xhT[:, k, :], start=(k == 0), stop=False)
                if fresh and j == 0:
                    parts.wait_low(pe)
                for k in range(DC):
                    pe.matmul(out, w[:, k, :], xlT[:, k, :], start=False, stop=False)
                w = ring.low(pe).rearrange("p (k n) -> p k n", k=DC)
                for k in range(DC):
                    ins = pe.matmul(out, w[:, k, :], xhT[:, k, :], start=False, stop=(k == DC - 1))
                if j == 0:
                    ins.then_inc(ring.used, 1)
            banks.close(ins, name)

        def linear_part(pe, name, weights, source, cols):
            kc = weights.shape[1]
            bank = banks.open(pe, name)
            for j, c0 in enumerate(cols):
                for k in range(kc):
                    ins = pe.matmul(bank[:, j * T:(j + 1) * T], weights[:, k, c0:c0 + P], source[:, k, :],
                                    start=(k == 0), stop=(k == kc - 1))
            banks.close(ins, name)

        def values(pe, name, source):
            bank = banks.open(pe, name)
            for j in range(2):
                w = ring.unit(pe).rearrange("p (k n) -> p k n", k=DC)
                for t in range(TT):
                    for k in range(DC):
                        ins = pe.matmul(bank[:, t * T + j * P:t * T + (j + 1) * P], source[:, k, t * P:(t + 1) * P],
                                        w[:, k, :], start=(k == 0), stop=(k == DC - 1))
                if j == 0:
                    ins.then_inc(ring.used, 1)
            banks.close(ins, name)

        def pairs_of(names):
            return [x for n in names for x in (None, n)]

        def root_of_mean(eng, bank, n, std, width=T):
            return eng.activation(std, bank[:, 0:width], ACT.Sqrt, bias=eps[:, 0:1], scale=1.0 / n)


        def attention_tensor_scores(pe, pairs, name, t, chunks):
            for c in chunks:
                queries, keys = pairs[c]
                bank = banks.open(pe, (name, t, c))
                w = P * (t + 1)
                if len(keys) == 1:
                    ins = pe.matmul(bank[:, 0:2 * w], queries[0][:, t * P:(t + 1) * P], keys[0][:, :, 0:w],
                                    start=True, stop=True)
                else:
                    for j in range(2):
                        ins = pe.matmul(bank[:, j * w:(j + 1) * w], queries[j][:, t * P:(t + 1) * P],
                                        keys[j][:, 0:w], start=True, stop=True)
                banks.close(ins, (name, t, c))

        def attention_tensor_transposes(pe, S0, S1, head, name):
            bank = banks.open(pe, (name, head))
            pe.transpose(bank[:, 0:128], S0[:, head, :], const("ident"))
            pe.transpose(bank[:, 128:256], S1[:, head, 0:P], const("ident"))
            banks.close(pe.transpose(bank[:, 256:384], S1[:, head, P:T], const("ident")), (name, head))

        def attention_vector_scores(dve, S0, S1, chunks, scales, biases, name, t):
            S = (S0, S1)[t]
            w = P * (t + 1)
            for c in chunks:
                b = banks.take(dve, (name, t, c))
                banks.give(dve.scalar_tensor_tensor(S[:, 2 * c:2 * c + 2, :], two(b[:, 0:2 * w], w), scales(c),
                                                    biases(t, c), ALU.mult, ALU.add), (name, t, c))
            banks.wait_drained(dve, (name, t, chunks[-1]))

        def bcast(ap, n):
            return ap.rearrange("p (a o) -> p a o", o=1).broadcast_to([P, ap.shape[1], n])

        gates = view(0, 16, T)
        uT = view(4096, UC, T)
        V1 = view(5120, TT, T)
        qT = view(5632, 8, T)
        KZ = view(7680, 4, 2 * T)
        mix = view(5632, 8, T)
        CZ = view(9728, SC * 2, P)
        tables = view(13824, 4, 4, T)
        S0 = view(17920, NH, P)
        S1 = view(19968, NH, T)
        PT = view(24064, 8, 384)
        bias_v = view(27136, NH, T)
        work = [view(27136 + 1024 * i, 4, T) for i in range(4)]
        kn = view(31232, 2, T)
        araw = view(31744, 4, T)
        qraw, qsq = view(17920, 10, T), view(20480, 10, T)
        sq, xnT = view(23040, 8, T), view(25088, 8, T)
        gluT, sig, tmp = view(9728, 4, T), view(10752, 4, T), view(11776, 2, T)
        sq4, xn2 = view(12288, 8, T), view(17920, 8, T)
        st = small[:, 0:6 * TT * NH].rearrange("p (k t n) -> p k t n", k=6, t=TT)
        MX, NM, DEN, ES, RC = (st[:, i] for i in range(5))
        s5 = small[:, 192:192 + 24 * SC].rearrange("p (k n) -> p k n", n=SC)
        s5c = small[:, 576:576 + 1536].rearrange("p (k n) -> p k n", k=6)
        MAGIC = 12582912.0
        TWO_PI = 2.0 * np.pi
        TURN = float(np.float32(TWO_PI * (1 - 1e-7)))
        (STEP, LS, TH, TAU, MAG, SIN, COS, TAUC, NR, NI, DN, CRE, CIM, TA, TB, KA, RDN) = range(17)

        loaded_x, loaded_c, loaded_b = sem("loaded_x"), sem("loaded_c"), sem("loaded_b")
        s_sq, s_xn, s_zero, s_qsq, s_dve, s_rec, s_qk = (
            sem(n) for n in ("sq1", "xn1", "zero", "qsq", "dve1", "reciprocals", "heads_ready"))
        s_mx, s_den, s_es, s_p, s_oc = (sem(n) for n in ("mx2", "den2", "es2", "p2", "out_lo2"))
        s_a3, s_tab, s_fr, s_g, s_gel, s_gelu, s_rot = (
            sem(n) for n in ("a3", "tab3", "fr3", "g3", "gel3", "gelu3", "rot3"))
        s_b, s_y = sem("b3"), sem("y3")
        s_ya, s_mix, s_sq4, s_xn2 = (sem(n) for n in ("gated4", "mix4", "sq4", "xn2"))

        banks.plan(["ms", ("u", 0), ("u", 1), ("q", 0), ("q", 1), ("qn", 0), ("q", 2), ("qn", 1), ("q", 3), ("qn", 2),
                    "k", ("qn", 3), "v", ("qn", 4), ("g", 0), ("g", 1), ("g", 2)]
                   + [("s", t, c) for t in range(TT) for c in range(8)])
        before_s5 = list(banks.done)
        three = (5, 6, 7)
        banks.plan([("g", i) for i in range(3, 8)] + [("t", 0), ("t", 1)], three)
        for c in range(8):
            banks.plan(([("t", 2 * c + 2), ("t", 2 * c + 3)] if c < 7 else []) + [("o", c)], three)
        banks.plan([("ya", i) for i in range(4)], three)
        banks.plan([("gb", i) for i in range(2)] + [("ga", i) for i in range(2)]
                   + [("ys", i) for i in range(4)] + [("out", i) for i in range(4)] + ["ms2"])
        ring.plan(banks, pairs_of([("u", 0), ("u", 1), ("q", 0), ("q", 1), ("q", 2), ("q", 3), "k"]), True)
        ring.plan(banks, pairs_of(["v"]))
        ring.plan(banks, pairs_of([("g", 0), ("g", 1), ("g", 2)]), True)
        ring.plan(banks, [(s_b, 1)])
        ring.plan(banks, pairs_of([("g", 3), ("g", 4), ("g", 5)]), True)
        ring.plan(banks, [(s_b, 2)])
        ring.plan(banks, pairs_of([("g", 6), ("g", 7)]), True)
        ring.plan(banks, [(s_b, 3), (s_b, 4)])
        ring.plan(banks, pairs_of([("ya", i) for i in range(4)]), True)
        ring.plan(banks, [("gb", 0), ("gb", 1), ("ga", 0), ("ga", 1)] + [("ys", i) for i in range(4)])
        ring.plan(banks, pairs_of([("out", i) for i in range(4)]), True)
        roles = [[0, 1, 2, 3]]
        for _ in range(UC - 1):
            x, y, z, w = roles[-1]
            roles.append([y, w, z, x])
        PEER_UNITS = 60

        def psum4(first):
            return ps[:, 512 * first:512 * first + 2048].rearrange("p (b n) -> p b n", n=512)

        with nc.Block() as block:
            @block.sync
            def _(sp):
                sp.dma_start(h[:, :], xT).then_inc(loaded_x, 16)
                sp.dma_start(cst[:, :], consts[:, 0:NEARLY]).then_inc(loaded_c, 16)
                sp.dma_start(p1[:, :], par1).then_inc(loaded_c, 16)
                for u in range(PEER_UNITS + SLOTS):
                    ring.load(sp, w1[u, :, :])
                    if u == 2 * SLOTS:
                        sp.dma_start(bias_v, bias1.rearrange("p (a b) -> p a b", b=T)).then_inc(loaded_b, 16)

            @block.gpsimd
            def _(pool):
                pool.memset(eps[:, 0:1], EPS).then_inc(s_zero, 1)
                pool.memset(KZ, 0.0).then_inc(s_zero, 1)
                pool.memset(CZ, 0.0).then_inc(s_zero, 1)
                ring.subtract(pool, 2)
                parts.subtract(pool, "pool", xnT)
                ring.subtract(pool, 28)
                ring.subtract(pool, 2)
                for c in range(8):
                    banks.wait_drained(pool, ("o", c))
                    pool.tensor_tensor(xlT[:, c, :], araw[:, c % 4, :], xhT[:, c, :].bitcast(F32),
                                       ALU.subtract).then_inc(s_oc, 1)
                for i in range(4):
                    if i < 3:
                        ring.subtract(pool, 2)
                    banks.wait_drained(pool, ("ya", i))
                    pair = mix[:, 2 * i:2 * i + 2, :]
                    pool.tensor_tensor(pair, pair, gates[:, 8 + 2 * i:10 + 2 * i, :], ALU.mult).then_inc(s_ya, 1)
                parts.subtract(pool, "pool", mix)
                ring.subtract(pool)
                parts.subtract(pool, "pool", xn2)

            @block.scalar
            def _(act):
                link = Chain(act, s_a3)
                act.wait_ge(loaded_x, 16)
                act.activation(sq, hT, ACT.Square).then_inc(s_sq, 1)
                act.wait_ge(loaded_c, 32)
                link(act.activation(s5[:, STEP], par("lstep"), ACT.Exp))
                ring.round(act, 2)
                act.wait_ge(s_dve, 2)
                link(act.activation(s5[:, MAG], s5[:, LS], ACT.Exp))
                act.wait_ge(s_dve, 9)
                act.activation(s5[:, SIN], s5[:, TAU], ACT.Sin, scale=TURN).then_inc(s_a3, 1)
                act.activation(s5[:, COS], s5[:, TAUC], ACT.Sin, scale=TURN).then_inc(s_a3, 1)
                act.wait_ge(s_zero, 1)
                b = banks.take(act, "ms")
                banks.give(root_of_mean(act, b, D, std[:, 0:T]), "ms")
                parts.round(act, xnT, s_xn, 0)

                def raw_and_square(job, i):
                    ring.feed(act, job)
                    b = banks.take(act, job)
                    act.activation(qsq[:, 2 * i:2 * i + 2, :], two(b[:, :]), ACT.Square).then_inc(s_qsq, 1)
                    banks.give(act.activation(qraw[:, 2 * i:2 * i + 2, :], two(b[:, :]), ACT.Copy), job)

                def head_root(i):
                    b = banks.take(act, ("qn", i))
                    act.wait_ge(s_rec, i + 1)
                    banks.give(root_of_mean(act, b, HD, std[:, :], 512), ("qn", i))

                def gate(i):
                    b = banks.take(act, ("g", i))
                    for j in range(2):
                        ins = act.activation(gates[:, 2 * i + j, :], b[:, j * T:(j + 1) * T], ACT.Sigmoid,
                                             bias=par("bgate")[:, 2 * i + j:2 * i + j + 1])
                    banks.give(ins, ("g", i))

                def table(uc):
                    act.wait_ge(s_fr, uc + 1)
                    for k in range(2):
                        t = tables[:, 2 * (uc % 2) + k].rearrange("p a t -> p (a t)")
                        act.activation(t, t, ACT.Sin, scale=TURN).then_inc(s_tab, 1)

                raw_and_square(("q", 0), 0)
                raw_and_square(("q", 1), 1)
                for i in range(1, 4):
                    head_root(i - 1)
                    raw_and_square(("q", i + 1) if i < 3 else "k", i + 1)
                ring.feed(act, ("g", 0))
                head_root(3)
                head_root(4)
                gate(0)
                table(0)
                ring.feed(act, ("g", 1))
                gate(1)
                table(1)
                ring.feed(act, ("g", 2))
                gate(2)
                for t in range(TT):
                    S = (S0, S1)[t]
                    act.wait_ge(s_mx, 2 * t + 2)
                    for hd in range(NH):
                        if t == 1 and hd % 8 == 0:
                            ring.feed(act, ("g", 3 + hd // 8))
                        act.activation(S[:, hd, :], S[:, hd, :], ACT.Exp, bias=NM[:, t, hd:hd + 1],
                                       accum_out=DEN[:, t, hd:hd + 1]).then_inc(s_den, 1)
                    act.wait_ge(s_den, NH * (t + 1))
                    act.activation(ES[:, t, :], ES[:, t, :], ACT.Exp).then_inc(s_es, 1)
                for i in range(3, 8):
                    ring.feed(act, ("g", i))
                    gate(i)
                ring.round(act, 2)
                table(2)

                def transposed(hd):
                    b = banks.take(act, ("t", hd))
                    banks.give(act.activation(PT[:, hd % 8, :], b[:, 0:384], ACT.Copy), ("t", hd))

                transposed(0)
                transposed(1)
                for c in range(8):
                    if c < 7:
                        transposed(2 * c + 2)
                        transposed(2 * c + 3)
                    b = banks.take(act, ("o", c))
                    act.activation(xhT[:, c, :], b[:, 0:T], ACT.Copy)
                    if c >= 4:
                        act.wait_ge(s_oc, c - 3)
                    banks.give(act.activation(araw[:, c % 4, :], b[:, 0:T], ACT.Copy), ("o", c))
                    if c == 2:
                        table(3)
                ring.feed(act, ("ya", 0))
                for i in range(4):
                    if i:
                        ring.feed(act, ("ya", i))
                    b = banks.take(act, ("ya", i))
                    banks.give(act.activation(mix[:, 2 * i:2 * i + 2, :], two(b[:, :]), ACT.Copy), ("ya", i))
                for uc in range(UC):
                    act.wait_ge(s_gel, uc + 1)
                    act.activation(uT[:, uc, :], uT[:, uc, :], ACT.Gelu).then_inc(s_gelu, 1)
                for i in range(2):
                    b = banks.take(act, ("gb", i))
                    banks.give(act.activation(sig[:, 2 * i:2 * i + 2, :], two(b[:, :]), ACT.Sigmoid), ("gb", i))
                ring.round(act, 2)
                parts.round(act, mix, s_mix, 0, 2)
                for i in range(4):
                    ring.feed(act, ("out", i))
                    banks.wait_drained(act, ("out", i))
                    act.activation(sq4[:, 2 * i:2 * i + 2, :], hT[:, 2 * i:2 * i + 2, :], ACT.Square).then_inc(s_sq4, 1)
                b = banks.take(act, "ms2")
                banks.give(root_of_mean(act, b, D, std[:, 0:T]), "ms2")
                parts.round(act, xn2, s_xn2, 0)

            @block.vector
            def _(dve):
                link = Chain(dve, s_dve)

                def col(i):
                    return s5[:, i]

                dve.wait_ge(s_a3, 1)
                link(dve.tensor_tensor(col(LS), par("lre"), col(STEP), ALU.mult))
                link(dve.tensor_tensor(col(TH), par("lim"), col(STEP), ALU.mult))
                link(dve.tensor_scalar(col(TAU), col(TH), 1.0 / TWO_PI, None, ALU.mult))
                link(dve.tensor_scalar(col(KA), col(TAU), MAGIC, None, ALU.add))
                link(dve.tensor_scalar(col(KA), col(KA), MAGIC, None, ALU.subtract))
                link(dve.tensor_tensor(col(TAU), col(TAU), col(KA), ALU.subtract))
                link(dve.tensor_scalar(col(KA), col(TAU), 0.25, None, ALU.is_ge))
                link(dve.tensor_scalar(col(TAUC), col(TAU), 0.25, None, ALU.add))
                link(dve.tensor_tensor(col(TAUC), col(TAUC), col(KA), ALU.subtract))
                banks.wait_drained(dve, "ms")
                dve.reciprocal(rst[:, 0:T], std[:, 0:T]).then_inc(s_rec, 1)
                dve.wait_ge(s_rec, 1)
                for c in range(DC):
                    dve.scalar_tensor_tensor(xnT[:, c, :], hT[:, c, :], par("ln1")[:, c:c + 1], rst[:, 0:T],
                                             ALU.mult, ALU.mult).then_inc(s_xn, 1)
                parts.subtract(dve, "dve", xnT)
                link(dve.tensor_tensor(col(TA), par("lre"), par("lre"), ALU.mult))
                link(dve.tensor_tensor(col(TB), par("lim"), par("lim"), ALU.mult))
                link(dve.tensor_tensor(col(DN), col(TA), col(TB), ALU.add))
                link(dve.reciprocal(col(RDN), col(DN)))
                dve.wait_ge(s_a3, 4)
                link(dve.tensor_tensor(col(NR), col(MAG), col(COS), ALU.mult))
                link(dve.tensor_scalar(col(NR), col(NR), 1.0, None, ALU.subtract))
                link(dve.tensor_tensor(col(NI), col(MAG), col(SIN), ALU.mult))
                for out_col, x, y, op in ((CRE, NR, NI, ALU.add), (CIM, NI, NR, ALU.subtract)):
                    link(dve.tensor_tensor(col(TA), col(x), par("lre"), ALU.mult))
                    link(dve.tensor_tensor(col(TB), col(y), par("lim"), ALU.mult))
                    link(dve.tensor_tensor(col(TA), col(TA), col(TB), op))
                    link(dve.tensor_tensor(col(out_col), col(TA), col(RDN), ALU.mult))
                cs = par("cs5").rearrange("p (s k c) -> p k s c", k=2, c=16)

                def c5(i):
                    return s5c[:, i].rearrange("p (s c) -> p s c", c=16)

                link(dve.tensor_tensor(c5(0), cs[:, 0], bcast(col(CRE), 16), ALU.mult))
                link(dve.tensor_tensor(c5(1), cs[:, 1], bcast(col(CIM), 16), ALU.mult))
                link(dve.tensor_tensor(c5(2), cs[:, 0], bcast(col(CIM), 16), ALU.mult))
                link(dve.tensor_tensor(c5(3), cs[:, 1], bcast(col(CRE), 16), ALU.mult))
                link(dve.tensor_tensor(c5(4), c5(0), c5(1), ALU.subtract))
                link(dve.scalar_tensor_tensor(s5c[:, 5], s5c[:, 2], -1.0, s5c[:, 3], ALU.mult, ALU.subtract))
                dve.wait_ge(s_zero, 3)
                for g in range(2):
                    for r in range(2):
                        for q in range(4):
                            dst = CZ[64 * g:64 * g + 64, :, :].rearrange("p (u q k) n -> p k q u n", q=4, k=2)
                            src = s5c[64 * g:64 * g + 64, 4 + r].rearrange("p (u q c) -> p q u c", q=4, c=16)
                            col0 = 32 * q + 16 * g
                            ins = dve.tensor_copy(dst[:, r, q, :, col0:col0 + 16], src[:, q])
                link(ins)

                def angles(uc):
                    fr, kk = tables[:, 2 * (uc % 2)], tables[:, 2 * (uc % 2) + 1]
                    for i in range(4):
                        tau = col(TAU)[:, 4 * uc + i:4 * uc + i + 1]
                        ins = dve.tensor_scalar(kk[:, i, :], const("time"), tau, MAGIC, ALU.mult, ALU.add)
                    link(ins)
                    link(dve.tensor_scalar(kk, kk, MAGIC, None, ALU.subtract))
                    for i in range(4):
                        tau = col(TAU)[:, 4 * uc + i:4 * uc + i + 1]
                        ins = dve.scalar_tensor_tensor(fr[:, i, :], const("time"), tau, kk[:, i, :],
                                                       ALU.mult, ALU.subtract)
                    link(ins)
                    link(dve.tensor_scalar(kk, fr, 0.25, None, ALU.is_ge))
                    dve.scalar_tensor_tensor(kk, fr, 0.25, kk, ALU.add, ALU.subtract).then_inc(s_fr, 1)

                def normed(i):
                    banks.wait_drained(dve, ("qn", i))
                    dve.reciprocal(rst[:, :], std[:, :]).then_inc(s_rec, 1)
                    dve.wait_ge(s_rec, i + 2)
                    dst = qT[:, 2 * i:2 * i + 2, :] if i < 4 else kn
                    link(dve.scalar_tensor_tensor(dst, qraw[:, 2 * i:2 * i + 2, :], par("gq" if i < 4 else "gk"),
                                                  two(rst[:, :]), ALU.mult, ALU.mult))

                for i in range(2):
                    b = banks.take(dve, ("u", i))
                    banks.give(dve.tensor_copy(uT[:, 2 * i:2 * i + 2, :], two(b[:, :])), ("u", i))
                angles(0)
                normed(0)
                angles(1)
                for i in range(1, 4):
                    normed(i)
                b = banks.take(dve, "v")
                banks.give(dve.tensor_copy(V1, two(b[:, :])), "v")
                normed(4)
                for kv in range(NKV):
                    src = kn[64 * (kv % 2):64 * (kv % 2) + 64, kv // 2, :]
                    for v in range(2):
                        ins = dve.tensor_copy(KZ[64 * v:64 * v + 64, kv, v * T:(v + 1) * T], src)
                ins.then_inc(s_qk, 1)

                dve.wait_ge(loaded_b, 16)
                for t in range(TT):
                    S = (S0, S1)[t]
                    attention_vector_scores(
                        dve, S0, S1, range(8), lambda c: HD ** -0.5,
                        lambda t, c: bias_v[:, 2 * c:2 * c + 2, P * (1 - t):T], "s", t)
                    link(dve.tensor_reduce(MX[:, t, :], S, AX.X, ALU.max))
                    link(dve.tensor_tensor(MX[:, t, :], MX[:, t, :], par("sinks"), ALU.max))
                    dve.tensor_scalar(NM[:, t, :], MX[:, t, :], -1.0, None, ALU.mult).then_inc(s_mx, 1)
                    dve.wait_ge(s_mx, 2 * t + 1)
                    dve.tensor_tensor(ES[:, t, :], NM[:, t, :], par("sinks"), ALU.add).then_inc(s_mx, 1)

                def finish(uc):
                    dve.wait_ge(s_y, uc + 1)
                    dve.scalar_tensor_tensor(uT[:, uc, :], uT[:, uc, :], par("dskip")[:, uc:uc + 1],
                                             psum[4][:, 0:T], ALU.mult, ALU.add).then_inc(s_gel, 1)

                for uc in range(UC):
                    x, y, z, w = (work[i] for i in roles[uc])
                    sin, cos = tables[:, 2 * (uc % 2)], tables[:, 2 * (uc % 2) + 1]
                    re, im = psum4(0)[:, :, 0:T], psum4(0)[:, :, T:2 * T]
                    dve.wait_ge(s_b, uc + 1)
                    dve.wait_ge(s_tab, 2 * uc + 2)
                    if uc:
                        dve.wait_ge(s_g, uc)
                    dve.tensor_tensor(x, re, cos, ALU.mult)
                    link(dve.tensor_tensor(y, im, sin, ALU.mult))
                    link(dve.tensor_tensor(x, x, y, ALU.add))
                    if uc:
                        dve.wait_ge(s_y, uc)
                    dve.tensor_tensor(y, im, cos, ALU.mult)
                    dve.tensor_tensor(z, re, sin, ALU.mult).then_inc(s_rot, 1)
                    dve.wait_ge(s_rot, uc + 1)
                    link(dve.tensor_tensor(y, y, z, ALU.subtract))
                    if uc:
                        finish(uc - 1)
                    for i in range(4):
                        mag = col(MAG)[:, 4 * uc + i:4 * uc + i + 1].broadcast_to([P, T])
                        dve.tensor_tensor_scan(x[:, i, :], mag, x[:, i, :], 0.0, ALU.mult, ALU.add)
                        ins = dve.tensor_tensor_scan(y[:, i, :], mag, y[:, i, :], 0.0, ALU.mult, ALU.add)
                    link(ins)
                    dve.tensor_tensor(z, x, cos, ALU.mult)
                    link(dve.tensor_tensor(w, y, sin, ALU.mult))
                    link(dve.tensor_tensor(z, z, w, ALU.subtract))
                    dve.tensor_tensor(x, x, sin, ALU.mult)
                    link(dve.tensor_tensor(y, y, cos, ALU.mult))
                    dve.tensor_tensor(x, x, y, ALU.add).then_inc(s_g, 1)
                    if uc == 0:
                        for t in range(TT):
                            S = (S0, S1)[t]
                            dve.wait_ge(s_es, t + 1)
                            link(dve.tensor_tensor(DEN[:, t, :], DEN[:, t, :], ES[:, t, :], ALU.add))
                            link(dve.reciprocal(RC[:, t, :], DEN[:, t, :]))
                            dve.tensor_tensor(S, S, bcast(RC[:, t, :], P * (t + 1)), ALU.mult).then_inc(s_p, 1)
                    if uc + 2 < UC:
                        angles(uc + 2)
                finish(UC - 1)

                for i in range(2):
                    b = banks.take(dve, ("ga", i))
                    banks.wait_drained(dve, ("gb", i))
                    banks.give(dve.tensor_tensor(gluT[:, 2 * i:2 * i + 2, :], two(b[:, :]), sig[:, 2 * i:2 * i + 2, :],
                                                 ALU.mult), ("ga", i))
                for i in range(4):
                    b = banks.take(dve, ("ys", i))
                    if i:
                        dve.wait_ge(s_mix, i)
                    banks.give(dve.tensor_tensor(tmp, two(b[:, :]), gates[:, 2 * i:2 * i + 2, :], ALU.mult), ("ys", i))
                    banks.wait_drained(dve, ("ys", i))
                    dve.wait_ge(s_ya, i + 1)
                    dve.tensor_tensor(mix[:, 2 * i:2 * i + 2, :], mix[:, 2 * i:2 * i + 2, :], tmp,
                                      ALU.add).then_inc(s_mix, 1)
                parts.subtract(dve, "dve", mix)
                for i in range(4):
                    b = banks.take(dve, ("out", i))
                    banks.give(dve.tensor_tensor(hT[:, 2 * i:2 * i + 2, :], hT[:, 2 * i:2 * i + 2, :], two(b[:, :]),
                                                 ALU.add), ("out", i))
                banks.wait_drained(dve, "ms2")
                dve.reciprocal(rst[:, 0:T], std[:, 0:T]).then_inc(s_rec, 1)
                dve.wait_ge(s_rec, 7)
                for c in range(DC):
                    dve.scalar_tensor_tensor(xn2[:, c, :], hT[:, c, :], par("ln2")[:, c:c + 1], rst[:, 0:T],
                                             ALU.mult, ALU.mult).then_inc(s_xn2, 1)
                parts.subtract(dve, "dve", xn2)

            @block.tensor
            def _(pe):
                def head_sums(n):
                    b = banks.open(pe, ("qn", n))
                    pe.wait_ge(s_qsq, n + 1)
                    banks.close(pe.matmul(b[:, :], const("blk64"), qsq[:, 2 * n:2 * n + 2, :], start=True, stop=True),
                                ("qn", n))

                def s5_inputs(uc):
                    w = ring.unit(pe).rearrange("p (q k n) -> p q k n", q=4, k=2)
                    if uc:
                        pe.wait_ge(s_rot, uc)
                    for i in range(4):
                        for k in range(2):
                            ins = pe.matmul(psum[i][:, k * T:(k + 1) * T], w[:, i, k, :], uT[:, uc, :],
                                            start=True, stop=True)
                    ins.then_inc(s_b, 1)

                def s5_outputs(uc):
                    if uc:
                        pe.wait_ge(s_gel, uc)
                    pe.wait_ge(s_g, uc + 1)
                    real, imaginary = roles[uc][2], roles[uc][0]
                    for i in range(4):
                        for k, src in enumerate((real, imaginary)):
                            ins = pe.matmul(psum[4][:, 0:T], CZ[:, 2 * (4 * uc + i) + k, :], work[src][:, i, :],
                                            start=(i + k == 0), stop=(i + k == 4))
                    ins.then_inc(s_y, 1)

                def transposes(hd):
                    attention_tensor_transposes(pe, S0, S1, hd, "t")

                def attend(c):
                    if c < 7:
                        transposes(2 * c + 2)
                        transposes(2 * c + 3)
                    bank = banks.open(pe, ("o", c))
                    for j in range(2):
                        hd = 2 * c + j
                        banks.wait_drained(pe, ("t", hd))
                        v = V1[:, :, 64 * (hd // 4):64 * (hd // 4) + 64]
                        rows = slice(64 * j, 64 * j + 64)
                        pe.matmul(bank[rows, 0:T], v[:, 0, :], PT[:, hd % 8, 0:T], start=True, stop=False)
                        ins = pe.matmul(bank[rows, P:T], v[:, 1, :], PT[:, hd % 8, T:384], start=False, stop=True)
                    banks.close(ins, ("o", c))

                pe.wait_ge(loaded_c, 32)
                sum_squares(pe, "ms", sq, DC, (s_sq, 1))
                linear(pe, ("u", 0), True)
                for name in (("u", 1), ("q", 0), ("q", 1)):
                    linear(pe, name)
                head_sums(0)
                linear(pe, ("q", 2))
                head_sums(1)
                linear(pe, ("q", 3))
                head_sums(2)
                linear(pe, "k")
                head_sums(3)
                values(pe, "v", xnT)
                head_sums(4)
                for i in range(3):
                    linear(pe, ("g", i))
                pe.wait_ge(s_qk, 1)
                pairs = [((qT[:, c, :],), (KZ[:, c // 2, :].rearrange("p (v t) -> p v t", v=2),)) for c in range(8)]
                for t in range(TT):
                    attention_tensor_scores(pe, pairs, "s", t, range(8))
                for b in range(5):
                    pe.wait_ge(banks.drained[b], before_s5[b])
                s5_inputs(0)
                for i in range(3, 6):
                    linear(pe, ("g", i))
                s5_inputs(1)
                linear(pe, ("g", 6))
                linear(pe, ("g", 7))
                s5_outputs(0)
                pe.wait_ge(s_p, TT)
                transposes(0)
                transposes(1)
                for c in range(4):
                    attend(c)
                s5_inputs(2)
                s5_outputs(1)
                attend(4)
                s5_inputs(3)
                attend(5)
                attend(6)
                s5_outputs(2)
                attend(7)
                banks.wait_drained(pe, ("o", 7))
                pe.wait_ge(s_oc, 8)
                for i in range(4):
                    linear(pe, ("ya", i))
                s5_outputs(3)
                pe.wait_ge(s_gelu, UC)
                for name in ("gb", "ga"):
                    for i in range(2):
                        linear_part(pe, (name, i), ring.unit(pe).rearrange("p (k n) -> p k n", k=4), uT, (0, P))
                banks.wait_drained(pe, ("ga", 1))
                for i in range(4):
                    linear_part(pe, ("ys", i), ring.unit(pe).rearrange("p (k n) -> p k n", k=4), gluT, (0, P))
                for i in range(4):
                    linear(pe, ("out", i), i == 0)
                sum_squares(pe, "ms2", sq4, DC, (s_sq4, 4))

        U = 16384
        qp = view(U, PH, T)
        keys_v = view(U + 2048, PH, T)
        cand = view(U, TT, PH, 256)
        s_v = view(U + 4096, TT, PH * 2, NSUB)
        eq = view(U + 4096, PH * TOPK, TOPK)
        sel = view(U + 6144, PH * TOPK, TOPK)
        f5 = arena[:, U + 8192:U + 8192 + 3456]
        idx = arena[:, U + 11648:U + 12160].bitcast(U32)
        vals = f5[:, 0:512].rearrange("p (t g n) -> p t g n", t=TT, n=TOPK)
        idxf = f5[:, 512:1024].rearrange("p (t g n) -> p t g n", t=TT, n=TOPK)
        best = f5[:, 1024:1280].rearrange("p (g n) -> p g n", n=TOPK)
        gate = f5[:, 1280:1536].rearrange("p (g n) -> p g n", n=TOPK)
        rank = f5[:, 1536:2048].rearrange("p (k t n) -> p k t n", k=2, t=TT)
        chosen = f5[:, 2048:2560].rearrange("p (k t n) -> p k t n", k=2, t=TT)
        gsum = f5[:, 2560:2576]
        iota16 = const("lane")[:, 0:TOPK]
        ranku = f5[:, 2688:3200].bitcast(U32).rearrange("p (k n) -> p k n", k=2)
        per_slot = small[:, 0:768].rearrange("p (k t) -> p k t", k=3)
        I1, I2, GT = per_slot[:, 0], per_slot[:, 1], per_slot[:, 2]
        idx_v = idx.rearrange("p (t g n) -> p t g n", t=TT, n=TOPK)
        pos = f5[:, 3200:3456].bitcast(U32).rearrange("p (g n) -> p g n", n=TOPK)
        s_keys, s_v5, s_e5, s_x5, s_sel, s_tr, s_slot = (
            sem(n) for n in ("keys5", "v5", "e5", "x5", "sel5", "transposed", "per_slot"))
        banks.plan([("pq", i) for i in range(4)] + [("ps", i) for i in range(8)])
        ring.plan(banks, pairs_of([("pq", i) for i in range(4)]), True)

        A = view(0, NE2, T)
        HALF = NE2 // 2
        ROWS_BEFORE = 68 // SLOTS
        GROUPS = T // 4
        OH1 = small[:, 768:1792].rearrange("p (b t n) -> p b t n", b=2, t=4)
        OH2 = small[:, 1792:2304].rearrange("p (b t n) -> p b t n", b=2, t=4)
        w_hi, w_lo, hi_done, lo_done, e_hi, e_lo, e_lo2, a_drained, g_one, g_full, g_done, s_h8 = (
            sem(n) for n in ("w_hi", "w_lo", "hi_done", "lo_done", "e_hi", "e_lo", "e_lo2", "a_drained",
                             "onehot", "grid_full", "grid_done", "h8"))

        with nc.Block() as block:
            @block.sync
            def _(sp):
                sp.dma_start(keys_v, keys.rearrange("p (h n) -> p h n", h=PH)).then_inc(s_keys, 16)
                while ring.issued < 68:
                    ring.load(sp, w1[ring.issued, :, :])
                for j in range(SLOTS):
                    sp.wait_ge(ring.rest, ring.number[64 + j] + 1)
                    sp.dma_start(slots_v[:, j, :], wu[j, :, :]).then_inc(ring.loaded[j], 16)
                with sp.Fori(0, NE2 // SLOTS - 1) as it:
                    for j in range(SLOTS):
                        sp.wait_ge(w_lo, it * SLOTS + (j + 1))
                        sp.dma_start(slots_v[:, j, :], wu[it * SLOTS + (SLOTS + j), :, :]).then_inc(ring.loaded[j], 16)
                with sp.Fori(0, NE2 // SLOTS) as it:
                    for j in range(SLOTS):
                        sp.wait_ge(w_lo, it * SLOTS + (NE2 - SLOTS + j + 1))
                        sp.dma_start(slots_v[:, j, :], wv[it * SLOTS + j, :, :]).then_inc(ring.loaded[j], 16)
                sp.wait_ge(s_keys, 16)

            @block.scalar
            def _(act):
                def round_row(it, n, early=False):
                    s = n % SLOTS
                    act.wait_ge(ring.loaded[s], it * (8 // SLOTS * 16) + 16 * (ROWS_BEFORE + n // SLOTS + 1))
                    if not early:
                        act.wait_ge(hi_done, it * 8 + (n - 1))
                        act.wait_ge(w_lo, it * 8 + (n - 1))
                    act.activation(whv[:, n % 2, :], slots_v[:, s, :], ACT.Copy).then_inc(w_hi, 1)

                def up_rows(it, first):
                    for j in range(8):
                        round_row(it, first + j + 2)
                        if j % 2:
                            act.wait_ge(lo_done, it * 8 + (first + j + 1))
                            act.activation(A[:, bass.ds(it * 8 + (first + j - 1), 2), :], two(psum[j // 2]),
                                           ACT.Gelu).then_inc(a_drained, 1)

                def round_a(it, row):
                    act.activation(xhT[:, row % 4, :], A[:, bass.ds(it * 8 + row, 1), :].rearrange("p o t -> p (o t)"),
                                   ACT.Copy).then_inc(e_hi, 1)

                def down_rows(it, first, last):
                    for j in range(8):
                        if first + j + 2 < NE2 or not last:
                            round_row(it, NE2 + first + j + 2)
                        if not (last and j >= 6):
                            if first + j >= 2 or not isinstance(it, int):
                                act.wait_ge(lo_done, it * 8 + (NE2 + first + j - 1))
                            round_a(it, first + j + 2)

                ring.round(act, 2)
                for i in range(4):
                    ring.feed(act, ("pq", i))
                    b = banks.take(act, ("pq", i))
                    banks.give(act.activation(qp[:, 2 * i:2 * i + 2, :], two(b[:, :]), ACT.Copy), ("pq", i))
                for i in range(8):
                    b = banks.take(act, ("ps", i))
                    dst = s_v[:, i // 4, 4 * (i % 4):4 * (i % 4) + 4, :]
                    banks.give(act.activation(dst, two(b[:, :], P), ACT.Copy), ("ps", i))
                round_row(0, 0, True)
                round_row(0, 1, True)
                with act.Fori(0, HALF // 8 - 1) as it:
                    up_rows(it, 0)
                act.wait_ge(s_x5, 1)
                act.activation(gate, gate, ACT.Exp).then_inc(s_e5, 1)
                up_rows(0, HALF - 8)
                for k in range(3):
                    act.wait_ge(s_tr, k + 1)
                    act.activation(per_slot[:, k], psum[4 + k][:, 0:T], ACT.Copy).then_inc(s_slot, 1)
                with act.Fori(0, HALF // 8) as it:
                    up_rows(it, HALF)
                for half in range(2):
                    act.wait_ge(g_done, GROUPS * (half + 1))
                    first = half * HALF
                    act.wait_ge(lo_done, NE2 + max(first - 2, 0))
                    round_a(0, first)
                    round_a(0, first + 1)
                    with act.Fori(0, HALF // 8 - 1) as it:
                        down_rows(it, first, False)
                    down_rows(0, first + HALF - 8, True)

            @block.gpsimd
            def _(pool):
                def rest_row(it, n, early=False):
                    pool.wait_ge(w_hi, it * 8 + (n + 1))
                    if not early:
                        pool.wait_ge(lo_done, it * 8 + (n - 1))
                    pool.tensor_tensor(wlv[:, n % 2, :], slots_v[:, n % SLOTS, :], whv[:, n % 2, :].bitcast(F32),
                                       ALU.subtract).then_inc(w_lo, 1)

                def rest_a(it, row):
                    pool.wait_ge(e_hi, it * 8 + (row + 1))
                    pool.tensor_tensor(xlT[:, row % 4, :], A[:, bass.ds(it * 8 + row, 1), :].rearrange("p o t -> p (o t)"),
                                       xhT[:, row % 4, :].bitcast(F32), ALU.subtract).then_inc(e_lo, 1)

                def down_rows(it, first, last):
                    for j in range(8):
                        if first + j + 2 < NE2 or not last:
                            rest_row(it, NE2 + first + j + 2)
                        if first < HALF and not (last and j >= 6):
                            rest_a(it, first + j + 2)

                ring.subtract(pool)
                pool.wait_ge(*ring.last[67])
                rest_row(0, 0, True)
                rest_row(0, 1, True)
                with pool.Fori(0, NE2 // 8) as it:
                    for j in range(8):
                        rest_row(it, j + 2)
                rest_a(0, 0)
                rest_a(0, 1)
                with pool.Fori(0, HALF // 8 - 1) as it:
                    down_rows(it, 0, False)
                down_rows(0, HALF - 8, True)
                with pool.Fori(0, HALF // 8 - 1) as it:
                    down_rows(it, HALF, False)
                down_rows(0, NE2 - 8, True)

            @block.vector
            def _(dve):
                link = Chain(dve, s_v5)
                low = -3e38

                def top16(rows, values, indices):
                    for a in (0, 8):
                        for r, v, i in zip(rows, values, indices):
                            ins = dve.max(v[:, a:a + 8], r)
                        link(ins)
                        for r, v, i in zip(rows, values, indices):
                            ins = dve.max_index(i[:, a:a + 8], v[:, a:a + 8], r)
                        if a == 0:
                            link(ins)
                            for r, v, i in zip(rows, values, indices):
                                ins = dve.match_replace(r, v[:, 0:8], r, low)
                            link(ins)
                    link(ins)

                for t in range(TT):
                    for i in range(4):
                        banks.wait_drained(dve, ("ps", 4 * t + i))
                    top16([s_v[:, t, g, :] for g in range(16)], [vals[:, t, g, :] for g in range(16)],
                          [idx_v[:, t, g, :] for g in range(16)])
                    if t == 0:
                        for i in range(4, 8):
                            banks.wait_drained(dve, ("ps", i))
                    pair = vals[:, t].rearrange("p (h k) n -> p h k n", k=2)
                    first = pair[:, :, 0, :].rearrange("p h (n o) -> p h n o", o=1).broadcast_to([P, PH, 16, 16])
                    second = pair[:, :, 1, :].rearrange("p h (o n) -> p h o n", o=1).broadcast_to([P, PH, 16, 16])
                    link(dve.tensor_tensor(cand[:, t].rearrange("p h (i j) -> p h i j", j=16), first, second, ALU.add))
                    top16([cand[:, t, g, :] for g in range(PH)], [best[:, PH * t + g, :] for g in range(PH)],
                          [pos[:, PH * t + g, :] for g in range(PH)])
                dve.tensor_copy(idxf, idx_v)
                dve.tensor_tensor(gate, best, best[:, :, 0:1].broadcast_to([P, TT * PH, TOPK]),
                                  ALU.subtract).then_inc(s_x5, 1)
                posf = pos.rearrange("p g n -> p (g n)")
                dve.tensor_scalar(ranku[:, 0], posf, 4, None, ALU.logical_shift_right)
                link(dve.tensor_scalar(ranku[:, 1], posf, 15, None, ALU.bitwise_and))
                link(dve.tensor_copy(rank, ranku.rearrange("p k (t n) -> p k t n", t=TT)))
                for t in range(TT):
                    pair = idxf[:, t].rearrange("p (h k) n -> p h k n", k=2)
                    for k in range(2):
                        link(dve.tensor_tensor(
                            eq, bcast(rank[:, k, t, :], TOPK),
                            iota16.rearrange("p (o n) -> p o n", o=1).broadcast_to([P, P, TOPK]), ALU.is_equal))
                        place = pair[:, :, k, :].rearrange("p h (o n) -> p h o n", o=1).broadcast_to([P, PH, 16, 16])
                        link(dve.tensor_tensor(sel.rearrange("p (h r) n -> p h r n", h=PH),
                                               eq.rearrange("p (h r) n -> p h r n", h=PH), place, ALU.mult))
                        dve.tensor_reduce(chosen[:, k, t, :], sel, AX.X, ALU.add).then_inc(s_sel, 1)
                dve.wait_ge(s_e5, 1)
                link(dve.tensor_reduce(gsum, gate, AX.X, ALU.add))
                link(dve.reciprocal(gsum, gsum))
                dve.tensor_tensor(gate, gate, bcast(gsum, TOPK), ALU.mult).then_inc(s_sel, 1)

                def build(half, it, n, early=False):
                    b = n % 2
                    if not early:
                        dve.wait_ge(g_full, it * 4 + (GROUPS * half + n - 1))
                    for t in range(4):
                        at = bass.ds(it * 16 + (n * 4 + t), 1)
                        dve.tensor_scalar(OH1[:, b, t, :], const("lane"), I1[:, at], GT[:, at], ALU.is_equal, ALU.mult)
                        ins = dve.tensor_scalar(OH2[:, b, t, :], const("lane")[:, HALF * half:HALF * (half + 1)],
                                                I2[:, at], None, ALU.is_equal)
                    ins.then_inc(g_one, 1)

                def spread(half, it, n):
                    dve.wait_ge(g_full, it * 4 + (GROUPS * half + n + 1))
                    a = A[:, HALF * half:HALF * (half + 1), bass.ds(it * 16 + n * 4, 4)]
                    dve.tensor_tensor(a, psum[4 + n % 4][:, 0:4 * HALF].rearrange("p (t e) -> p e t", t=4), a,
                                      ALU.mult).then_inc(g_done, 1)

                dve.wait_ge(s_slot, 3)
                for half in range(2):
                    dve.wait_ge(a_drained, HALF // 2 * (half + 1))
                    build(half, 0, 0, half == 0)
                    build(half, 0, 1, half == 0)
                    spread(half, 0, 0)
                    with dve.Fori(0, GROUPS // 4 - 1) as it:
                        for j in range(4):
                            build(half, it, j + 2)
                            spread(half, it, j + 1)
                    for n in range(GROUPS - 4, GROUPS - 1):
                        if n + 2 < GROUPS:
                            build(half, 0, n + 2)
                        spread(half, 0, n + 1)
                with dve.Fori(0, HALF // 4) as it:
                    for j in range(4):
                        dve.wait_ge(e_hi, it * 4 + (HALF + j + 1))
                        dve.wait_ge(lo_done, it * 4 + (NE2 + HALF + j - 3))
                        row = A[:, bass.ds(it * 4 + (HALF + j), 1), :].rearrange("p o t -> p (o t)")
                        dve.tensor_tensor(xlT[:, j, :], row, xhT[:, j, :].bitcast(F32), ALU.subtract).then_inc(e_lo2, 1)
                dve.wait_ge(lo_done, 2 * NE2)
                for b in range(4):
                    dve.tensor_tensor(hT[:, 2 * b:2 * b + 2, :], hT[:, 2 * b:2 * b + 2, :], two(psum[b]),
                                      ALU.add).then_inc(s_h8, 1)

            @block.tensor
            def _(pe):
                for i in range(4):
                    linear(pe, ("pq", i))
                pe.wait_ge(s_keys, 16)
                for i in range(8):
                    bank = banks.open(pe, ("ps", i))
                    t = i // 4
                    for j in range(2):
                        hd = 2 * (i % 4) + j
                        if j == 0:
                            banks.wait_drained(pe, ("pq", i % 4))
                        ins = pe.matmul(bank[:, j * T:(j + 1) * T], qp[:, hd, t * P:(t + 1) * P], keys_v[:, hd, :],
                                        start=True, stop=True)
                    banks.close(ins, ("ps", i))

                def grid(half, it, n):
                    number = GROUPS * half + n
                    if number >= 4 or not isinstance(it, int):
                        pe.wait_ge(g_done, it * 4 + (number - 3))
                    pe.wait_ge(g_one, it * 4 + (number + 1))
                    for t in range(4):
                        ins = pe.matmul(psum[4 + n % 4][:, t * HALF:(t + 1) * HALF], OH1[:, n % 2, t, :],
                                        OH2[:, n % 2, t, :], start=True, stop=True)
                    ins.then_inc(g_full, 1)

                def up_rows(it, first, early, gated):
                    for j in range(8):
                        if j % 2 == 0 and not early:
                            pe.wait_ge(a_drained, it * 4 + (first // 2 + j // 2 - 3))
                        out = psum[j // 2][:, (j % 2) * T:(j % 2 + 1) * T]
                        hi, lo = (x[:, j % 2, :].rearrange("p (k n) -> p k n", k=DC) for x in (whv, wlv))
                        pe.wait_ge(w_hi, it * 8 + (first + j + 1))
                        for k in range(DC):
                            pe.matmul(out, hi[:, k, :], xhT[:, k, :], start=(k == 0), stop=False)
                            ins = pe.matmul(out, hi[:, k, :], xlT[:, k, :], start=False, stop=False)
                        ins.then_inc(hi_done, 1)
                        pe.wait_ge(w_lo, it * 8 + (first + j + 1))
                        for k in range(DC):
                            ins = pe.matmul(out, lo[:, k, :], xhT[:, k, :], start=False, stop=(k == DC - 1))
                        ins.then_inc(lo_done, 1)
                        if gated:
                            grid(0, it * 2, j)

                def down_rows(it, first, early, gated):
                    for j in range(8):
                        hi, lo = whv[:, j % 2, :], wlv[:, j % 2, :]
                        a_hi, a_lo = xhT[:, j % 4, :], xlT[:, j % 4, :]
                        pe.wait_ge(w_hi, it * 8 + (NE2 + first + j + 1))
                        pe.wait_ge(e_hi, it * 8 + (first + j + 1))
                        pe.wait_ge(*((e_lo, it * 8 + (j + 1)) if first == 0 else (e_lo2, it * 8 + (j + 1))))
                        for c in range(DC):
                            out = psum[c // 2][:, (c % 2) * T:(c % 2 + 1) * T]
                            pe.matmul(out, hi[:, c * P:(c + 1) * P], a_hi, start=(early and j == 0 and c % 2 == 0),
                                      stop=False, skip_group_check=True)
                            ins = pe.matmul(out, hi[:, c * P:(c + 1) * P], a_lo, start=False, stop=False,
                                            skip_group_check=True)
                        ins.then_inc(hi_done, 1)
                        pe.wait_ge(w_lo, it * 8 + (NE2 + first + j + 1))
                        for c in range(DC):
                            ins = pe.matmul(psum[c // 2][:, (c % 2) * T:(c % 2 + 1) * T], lo[:, c * P:(c + 1) * P], a_hi,
                                            start=False, stop=False, skip_group_check=True)
                        ins.then_inc(lo_done, 1)
                        if gated:
                            grid(1, it * 2, j)

                for i in range(8):
                    banks.wait_drained(pe, ("ps", i))
                up_rows(0, 0, True, False)
                with pe.Fori(1, HALF // 8) as it:
                    up_rows(it, 0, False, False)
                gate_t = gate.rearrange("p (t h) n -> p t (h n)", t=TT)
                for k in range(3):
                    pe.wait_ge(s_sel, 4 if k < 2 else 5)
                    for t in range(TT):
                        src = chosen[:, k, t, :] if k < 2 else gate_t[:, t, :]
                        ins = pe.transpose(psum[4 + k][:, t * P:(t + 1) * P], src, const("ident"))
                    ins.then_inc(s_tr, 1)
                pe.wait_ge(s_slot, 3)
                up_rows(0, HALF, False, True)
                with pe.Fori(1, HALF // 8) as it:
                    up_rows(it, HALF, False, True)
                pe.wait_ge(a_drained, HALF)
                down_rows(0, 0, True, True)
                with pe.Fori(1, HALF // 8) as it:
                    down_rows(it, 0, False, True)
                with pe.Fori(0, HALF // 8) as it:
                    down_rows(it, HALF, False, False)
        if stop_after == "peer":
            return

        banks.reset()
        ring.reset()
        parts.reset()
        memory.close()
        LOW = 13632
        late_cst = sb("late_cst", NCONST - NEARLY)
        low_part = sb("layer", LOW)
        upper = ctx.enter_context(ExitStack())
        high_part = upper.enter_context(nc.sbuf_tensor("layer_upper", [P, 31088 - LOW], F32))

        def part(a, b):
            return low_part[:, a:b] if b <= LOW else high_part[:, a - LOW:b - LOW]

        xnT = view(27760, 8, T)
        raw = view(0, 8, T)
        qA = view(2048, 4, T)
        KZ2 = part(3072, 5120).rearrange("p (b g v t) -> p b g v t", b=2, g=2, v=2)
        KZC = part(5120, 5184).rearrange("p (g v i) -> p g v i", g=2, v=2)
        kcr = part(5184, 5440)
        X = part(5440, 6464).rearrange("p (k l n) -> p k l n", k=2, l=16)
        Z = part(6464, 7488).rearrange("p (k g t) -> p k g t", k=2, g=2)
        cq, cqn = view(7488, 2, T), view(8000, 2, T)
        ckr = view(8512, 2, T)
        ckvn = part(9024, 9280)
        kpe = part(9280, 9536)
        qMr, qM, KM = view(9536, 8, T), view(11584, 8, T), view(13632, 8, T)
        V2, Vm = view(15680, TT, T), view(16192, TT, 512)
        GA = part(17216, 17264).rearrange("p (t h b) -> p t h b", t=TT, b=3)
        hid = part(17264, 17392).rearrange("p (k c n) -> p k c n", k=2, c=2)
        vcmp = view(17392, 2, 64)
        ra, rb = view(17520, 2, T), view(18032, 2, T)
        sqc = view(20592, 3, T)
        SA0, SA1 = view(18544, 24, P), view(21616, 24, T)
        PTR = view(27760, 8, 384)
        Sc = part(30832, 31088).rearrange("p (t h i) -> p t h i", t=TT, h=8)
        PTC = view(0, 8, T)
        aT = view(9536, 8, T)
        sqo = view(0, 8, T)
        relu = view(4096, 4, T).rearrange("p (b c) t -> p b c t", b=2)
        fx = view(6144, 8, T)
        squared = view(8192, 2, T)
        mixT = view(11584, 8, T)
        st2 = small[:, 512:512 + 192].rearrange("p (k t n) -> p k t n", k=4, t=TT)
        MX2, NM2, DEN2, RC2 = (st2[:, i] for i in range(4))
        stc = small[:, 704:704 + 48].rearrange("p (k t n) -> p k t n", k=3, t=TT)

        def p2(name):
            return par(name, PAR2)

        names = ("lpar", "lxn", "lzero", "lstep", "lsqc", "lX", "lcx", "amx", "aden", "ap", "avec", "acv", "acx",
                 "acp", "az", "fsq", "fmix", "fhid", "fsqr", "fhigh", "fvec", "fh", "fsq2", "fxn2", "lcopies")
        L = {n: sem(n) for n in names}
        loop_sems = ring.loaded + [ring.used, ring.rounded, ring.rest, parts.sem_hi, parts.sem_pool, parts.sem_dve] + banks.full + banks.drained + list(L.values())

        banks.plan(["ms", ("in", 0), ("in", 1), ("in", 2), ("in", 3), ("in", 4), ("in", 5), "G",
                    "rc", "msq", "mskv", ("rp", 0), ("rp", 1), ("rp", 2), "rk"]
                   + [("uq", i) for i in range(4)] + [("uk", i) for i in range(4)] + [("uv", t) for t in range(TT)]
                   + [("ck", 0), ("ck", 1), ("cv", 0), ("cv", 1)] + [("rq", i) for i in range(4)] + ["k2", "v2"])
        ring.plan(banks, pairs_of([("in", i) for i in range(6)]), True)
        ring.plan(banks, [("uq", 1), ("uq", 3), ("uk", 3), ("uv", 1)] + [None] * 3 + [("ck", 1)] + [None] * 3 + [("cv", 1)])

        MLA, SELECTED, WINDOW = 2, 0, 1
        scores_banks, output_banks = (0, 1, 2, 3, 4), (5, 6, 7)

        def plan_scores(group, t):
            banks.plan([("s2", t, c) for c in range(4 * group, 4 * group + 4)], scores_banks)

        banks.plan(["sc"], scores_banks)
        for group, t in ((MLA, 0), (MLA, 1), (SELECTED, 0), (SELECTED, 1), (WINDOW, 0)):
            plan_scores(group, t)
        banks.plan(["V"], output_banks)
        ring.plan(banks, pairs_of(["V"]))
        banks.plan([("t2", 16), ("t2", 17), ("t2", 18), ("t2", 19), ("o2", 4)], output_banks)
        plan_scores(WINDOW, 1)
        banks.plan([("t2", 20), ("t2", 21), ("o2", 5), ("t2", 22), ("t2", 23), ("o2", 6), ("o2", 7)], output_banks)
        nsa_heads = [[2 * c, 2 * c + 1, 8 + 2 * c, 9 + 2 * c] for c in range(4)]
        for c in range(5):
            if c < 4:
                banks.plan([("tc", c)] + [("t2", hd) for hd in nsa_heads[c]])
            if c:
                banks.plan([("o2", c - 1)])
        order = list(range(16, 24)) + [hd for heads in nsa_heads for hd in heads]
        slot = {hd: i % 8 for i, hd in enumerate(order)}

        banks.plan(["mo0", "mo1"] + [("wo", i) for i in range(4)] + [("f1", 0), ("f1", 1), "mf"]
                   + [("f1", i) for i in range(2, 16)]
                   + [("f2", b) for b in range(4)])
        ring.plan(banks, pairs_of([("wo", i) for i in range(4)] + [("f1", i) for i in range(16)])
                  + [None] * 31 + [("f2", 3)], True)
        late = sem("late_constants")

        with nc.Block() as block:
            @block.sync
            def _(sp):
                sp.dma_start(late_cst[:, :], consts[:, NEARLY:NCONST]).then_inc(late, 16)
                sp.wait_ge(late, 16)

            @block.scalar
            def _(act):
                act.activation(sqo, hT, ACT.Square)

        with nc.Fori(0, LAYERS) as layer:
            with nc.Block() as block:
                @block.gpsimd
                def _(pool):
                    for x in loop_sems:
                        pool.sem_clear(x)

            with nc.Block() as block:
                @block.sync
                def _(sp):
                    for u in range(24 + SLOTS):
                        if u == 2:
                            sp.dma_start(small[:, 0:NPAR2], par2[layer, :, :]).then_inc(L["lpar"], 16)
                        ring.load(sp, w2[layer, u, :, :])

                @block.gpsimd
                def _(pool):
                    pool.memset(KZ2, 0.0).then_inc(L["lzero"], 1)
                    pool.memset(part(5120, 5184), 0.0).then_inc(L["lzero"], 1)
                    pool.memset(vcmp, 0.0).then_inc(L["lzero"], 1)
                    ring.subtract(pool, 2)
                    parts.subtract(pool, "pool", xnT)
                    ring.subtract(pool, 10)

                @block.scalar
                def _(act):
                    ring.round(act, 2)
                    b = banks.take(act, "ms")
                    banks.give(root_of_mean(act, b, D, std[:, 0:T]), "ms")
                    parts.round(act, xnT, L["lxn"], 0)
                    for i in range(4):
                        ring.feed(act, ("in", i))
                        b = banks.take(act, ("in", i))
                        banks.give(act.activation(raw[:, 2 * i:2 * i + 2, :], two(b[:, :]), ACT.Copy), ("in", i))
                    ring.round(act, 12 - ring.at["act"])
                    b = banks.take(act, ("in", 4))
                    act.activation(sqc[:, 0:2, :], two(b[:, :]), ACT.Square).then_inc(L["lsqc"], 1)
                    banks.give(act.activation(cq, two(b[:, :]), ACT.Copy), ("in", 4))
                    b = banks.take(act, ("in", 5))
                    act.activation(sqc[:, 2, :], b[:, 0:T], ACT.Square).then_inc(L["lsqc"], 1)
                    banks.give(act.activation(ckr, two(b[:, :]), ACT.Copy), ("in", 5))
                    b = banks.take(act, "G")
                    banks.give(act.activation(part(17216, 17264), b[:, 0:48], ACT.Sigmoid), "G")
                    b = banks.take(act, "msq")
                    act.wait_ge(L["lstep"], 1)
                    banks.give(root_of_mean(act, b, 256, std[:, 0:T]), "msq")
                    b = banks.take(act, "mskv")
                    banks.give(root_of_mean(act, b, 128, std[:, T:2 * T]), "mskv")
                    for i in range(4):
                        b = banks.take(act, ("uq", i))
                        banks.give(act.activation(qMr[:, 2 * i:2 * i + 2, :], two(b[:, :]), ACT.Copy), ("uq", i))
                    for t in range(TT):
                        b = banks.take(act, ("uv", t))
                        banks.give(act.activation(Vm[:, t, :], b[:, :], ACT.Copy), ("uv", t))
                    for k, n in enumerate(("ck", "cv")):
                        for c in range(2):
                            b = banks.take(act, (n, c))
                            banks.give(act.activation(hid[:, k, c, 0:30], b[:, 0:30], ACT.Silu), (n, c))

                @block.vector
                def _(dve):
                    link = Chain(dve, L["lstep"])
                    banks.wait_drained(dve, "ms")
                    link(dve.reciprocal(rst[:, 0:T], std[:, 0:T]))
                    dve.wait_ge(L["lpar"], 16)
                    for c in range(DC):
                        dve.scalar_tensor_tensor(xnT[:, c, :], hT[:, c, :], p2("attn")[:, c:c + 1], rst[:, 0:T],
                                                 ALU.mult, ALU.mult).then_inc(L["lxn"], 1)
                    parts.subtract(dve, "dve", xnT)

                    def rope(job, source, tag, outs):
                        n = source.shape[1]
                        cos, sin = (const(f + tag).rearrange("p (o t) -> p o t", o=1).broadcast_to([P, n, T])
                                    for f in ("cos", "sin"))
                        b = banks.take(dve, job)
                        dve.tensor_tensor(ra[:, 0:n, :], source, cos, ALU.mult).then_inc(L["lcopies"], 1)
                        banks.give(dve.tensor_tensor(rb[:, 0:n, :], two(b[:, 0:n * T]), sin, ALU.mult), job)
                        banks.wait_drained(dve, job)
                        ropes.append(1)
                        dve.wait_ge(L["lcopies"], len(ropes))
                        link(outs(ra[:, 0:n, :], rb[:, 0:n, :]))

                    ropes = []

                    def add_to(dst):
                        return lambda x, y: dve.tensor_tensor(dst, x, y, ALU.add)

                    def windows(k, source):
                        for g in range(2):
                            dve.tensor_copy(Z[0:64, k, g, :], source[64 * g:64 * g + 64, :])
                            ins = dve.tensor_copy(Z[64:128, k, g, 0:T - 1], source[64 * g:64 * g + 64, 1:T])
                        link(ins)
                        z = Z[:, k].rearrange("p g (i l two) -> p l g i two", l=8, two=2)[:, :, :, :, 0]
                        pos = p2("posk" if k == 0 else "posv")
                        for half in range(2):
                            add = pos[:, 8 * half:8 * half + 8].rearrange("p (l a b) -> p l a b", a=1, b=1)\
                                .broadcast_to([P, 8, 2, NCMP])
                            dve.tensor_tensor(X[:, k, 8 * half:8 * half + 8, 0:30].rearrange("p l (g i) -> p l g i", g=2),
                                              z[:, :, :, half:half + NCMP], add, ALU.add).then_inc(L["lX"], 1)

                    rope("rc", raw[:, 4:5, :], "A", add_to(kcr.rearrange("p (o t) -> p o t", o=1)))
                    dve.memset(Z[64:128, :, :, T - 1:T], 0.0)
                    windows(0, kcr)
                    banks.wait_drained(dve, ("in", 2))
                    windows(1, raw[:, 5, :])
                    banks.wait_drained(dve, "msq")
                    banks.wait_drained(dve, "mskv")
                    link(dve.reciprocal(rst[:, :], std[:, :]))
                    for c in range(2):
                        dve.scalar_tensor_tensor(cqn[:, c, :], cq[:, c, :], p2("qn")[:, c:c + 1], rst[:, 0:T],
                                                 ALU.mult, ALU.mult).then_inc(L["lcx"], 1)
                    dve.scalar_tensor_tensor(ckvn, ckr[:, 0, :], p2("kvn"), rst[:, T:2 * T],
                                             ALU.mult, ALU.mult).then_inc(L["lcx"], 1)
                    for i in range(2):
                        rope(("rp", i), raw[:, 2 * i:2 * i + 2, :], "A", add_to(qA[:, 2 * i:2 * i + 2, :]))
                    dve.wait_ge(L["lzero"], 3)

                    def split_keys(x, y):
                        for g in range(2):
                            r = slice(64 * g, 64 * g + 64)
                            for v in range(2):
                                ins = dve.tensor_tensor(KZ2[64 * v:64 * v + 64, :, g, v, :], x[r], y[r], ALU.add)
                        return ins

                    rope(("rp", 2), raw[:, 6:8, :], "A", split_keys)
                    rope("rk", ckr[:, 1:2, :], "B", add_to(kpe.rearrange("p (o t) -> p o t", o=1)))
                    kpe2 = kpe.rearrange("p (o t) -> p o t", o=1).broadcast_to([P, 2, T])
                    for i in range(4):
                        b = banks.take(dve, ("uk", i))
                        banks.give(dve.tensor_tensor(KM[:, 2 * i:2 * i + 2, :], two(b[:, :]), kpe2, ALU.add), ("uk", i))
                    for i in range(4):
                        rope(("rq", i), qMr[:, 2 * i:2 * i + 2, :], "B", add_to(qM[:, 2 * i:2 * i + 2, :]))
                    b = banks.take(dve, "k2")
                    src = b[0:64, 0:30].rearrange("p (g i) -> p g i", g=2)
                    dve.tensor_copy(KZC[0:64, :, 0, 0:NCMP], src)
                    banks.give(dve.tensor_copy(KZC[64:128, :, 1, 0:NCMP], src), "k2")
                    b = banks.take(dve, "v2")
                    banks.give(dve.tensor_copy(vcmp[0:NCMP], two(b[0:NCMP, 0:128], 64)), "v2")

                @block.tensor
                def _(pe):
                    sum_squares(pe, "ms", sqo, DC)
                    for i in range(6):
                        linear(pe, ("in", i), i == 0)
                    bank = banks.open(pe, "G")
                    wg = p2("wg").rearrange("p (k n) -> p k n", k=DC)
                    for t in range(TT):
                        for k in range(DC):
                            ins = pe.matmul(bank[:, t * 24:(t + 1) * 24], xnT[:, k, t * P:(t + 1) * P], wg[:, k, :],
                                            start=(k == 0), stop=(k == DC - 1))
                    banks.close(ins, "G")

                    def rotate(job, matrix, source, after):
                        n = source.shape[1]
                        bank = banks.open(pe, job)
                        banks.wait_drained(pe, after)
                        banks.close(pe.matmul(bank[:, 0:n * T], const(matrix), source, start=True, stop=True), job)

                    rotate("rc", "rot64", raw[:, 4:5, :], ("in", 2))
                    sum_squares(pe, "msq", sqc, 2, (L["lsqc"], 1))
                    sum_squares(pe, "mskv", sqc[:, 2:3, :], 1, (L["lsqc"], 2))
                    for i in range(2):
                        rotate(("rp", i), "rot64", raw[:, 2 * i:2 * i + 2, :], ("in", i))
                    rotate(("rp", 2), "rot64", raw[:, 6:8, :], ("in", 3))
                    rotate("rk", "rot32", ckr[:, 1:2, :], ("in", 5))
                    pe.wait_ge(L["lcx"], 3)
                    for i in range(4):
                        if i % 2 == 0:
                            w = ring.unit(pe).rearrange("p (k n) -> p k n", k=2)
                        c = 2 * (i % 2) * P
                        linear_part(pe, ("uq", i), w, cqn, (c, c + P))
                    w = ring.unit(pe)
                    for i in range(4):
                        bank = banks.open(pe, ("uk", i))
                        for j in range(2):
                            ins = pe.matmul(bank[:, j * T:(j + 1) * T], w[:, (2 * i + j) * P:(2 * i + j + 1) * P], ckvn,
                                            start=True, stop=True)
                        banks.close(ins, ("uk", i))
                    w = ring.unit(pe)
                    for t in range(TT):
                        bank = banks.open(pe, ("uv", t))
                        banks.close(pe.matmul(bank[:, :], ckvn[:, t * P:(t + 1) * P], w[:, 0:512],
                                              start=True, stop=True), ("uv", t))
                    for k, n in enumerate(("ck", "cv")):
                        two_banks = [banks.open(pe, (n, c)) for c in range(2)]
                        pe.wait_ge(L["lX"], 2 * k + 2)
                        for part in range(4):
                            w = ring.unit(pe).rearrange("p (l n) -> p l n", n=T)
                            for lp in range(4):
                                for c in range(2):
                                    ins = pe.matmul(two_banks[c][:, 0:30], w[:, lp, c * P:(c + 1) * P],
                                                    X[:, k, 4 * part + lp, 0:30], start=(part + lp == 0),
                                                    stop=(part == 3 and lp == 3))
                                    if part == 3 and lp == 3:
                                        banks.close(ins, (n, c))
                            if part < 3:
                                ins.then_inc(ring.used, 1)
                    for i in range(4):
                        rotate(("rq", i), "rot32", qMr[:, 2 * i:2 * i + 2, :], ("uq", i))
                    banks.wait_drained(pe, ("cv", 1))
                    bank = banks.open(pe, "k2")
                    w2k = p2("w2k").rearrange("p (c n) -> p c n", c=2)
                    w2v = p2("w2v").rearrange("p (c n) -> p c n", c=2)
                    for c in range(2):
                        ins = pe.matmul(bank[0:64, 0:30], w2k[:, c, :], hid[:, 0, c, 0:30], start=(c == 0), stop=(c == 1))
                    banks.close(ins, "k2")
                    bank = banks.open(pe, "v2")
                    for g in range(2):
                        for c in range(2):
                            ins = pe.matmul(bank[0:NCMP, 64 * g:64 * g + 64], hid[:, 1, c, NCMP * g:NCMP * g + NCMP],
                                            w2v[:, c, :], start=(c == 0), stop=(c == 1))
                    banks.close(ins, "v2")

            with nc.Block() as block:
                @block.gpsimd
                def _(pool):
                    pool.memset(PTC, 0.0).then_inc(L["az"], 1)

                @block.vector
                def _(dve):
                    link = Chain(dve, L["avec"])
                    b = banks.take(dve, "sc")
                    bc = b[:, 0:TT * 8 * NCMP].rearrange("p (t h i) -> p t h i", t=TT, h=8)
                    S = Sc[:, :, :, 0:NCMP]
                    for t in range(TT):
                        add = const("cmp_add")[:, 16 * t:16 * t + NCMP].rearrange("p (o i) -> p o i", o=1)\
                            .broadcast_to([P, 8, NCMP])
                        ins = dve.scalar_tensor_tensor(S[:, t], bc[:, t], 64 ** -0.5, add, ALU.mult, ALU.add)
                    banks.give(ins, "sc")
                    banks.wait_drained(dve, "sc")
                    link(dve.tensor_reduce(stc[:, 0], S, AX.X, ALU.max))
                    for t in range(TT):
                        ins = dve.tensor_tensor(S[:, t], S[:, t], bcast(stc[:, 0, t], NCMP), ALU.subtract)
                        ins.then_inc(L["acv"], 1)

                    def compressed():
                        dve.wait_ge(L["acx"], TT)
                        for t in range(TT):
                            mul = const("cmp_mul")[:, 16 * t:16 * t + NCMP].rearrange("p (o i) -> p o i", o=1)\
                                .broadcast_to([P, 8, NCMP])
                            ins = dve.tensor_tensor(S[:, t], S[:, t], mul, ALU.mult)
                        link(ins)
                        link(dve.tensor_reduce(stc[:, 1], S, AX.X, ALU.add))
                        link(dve.tensor_scalar(stc[:, 1], stc[:, 1], 1e-30, None, ALU.max))
                        link(dve.reciprocal(stc[:, 2], stc[:, 1]))
                        link(dve.tensor_tensor(stc[:, 2], stc[:, 2], GA[:, :, :, 0], ALU.mult))
                        for t in range(TT):
                            dve.tensor_tensor(S[:, t], S[:, t], bcast(stc[:, 2, t], NCMP), ALU.mult).then_inc(L["acp"], 1)

                    def scores(number, group):
                        heads = slice(8 * group, 8 * group + 8)
                        for t in range(TT):
                            attention_vector_scores(
                                dve, SA0, SA1, range(4 * group, 4 * group + 4), lambda c: (64 if c < 8 else 96) ** -0.5,
                                lambda t, c: const("mask1")[:, P * (1 - t):T].rearrange("p (o s) -> p o s", o=1)
                                .broadcast_to([P, 2, P * (t + 1)]), "s2", t)
                            dve.tensor_reduce(NM2[:, t, heads], (SA0, SA1)[t][:, heads, :], AX.X, ALU.max, negate=True)\
                                .then_inc(L["amx"], 1)

                    def probabilities(number, group):
                        heads = slice(8 * group, 8 * group + 8)
                        for t in range(TT):
                            S2 = (SA0, SA1)[t][:, heads, :]
                            dve.wait_ge(L["aden"], 8 * (2 * number + t + 1))
                            link(dve.reciprocal(RC2[:, t, heads], DEN2[:, t, heads]))
                            if group != MLA:
                                link(dve.tensor_tensor(RC2[:, t, heads], RC2[:, t, heads], GA[:, t, :, 1 + group], ALU.mult))
                            dve.tensor_tensor(S2, S2, bcast(RC2[:, t, heads], P * (t + 1)), ALU.mult)\
                               .then_inc(L["ap"], 1)

                    scores(0, MLA)
                    scores(1, SELECTED)
                    probabilities(0, MLA)
                    scores(2, WINDOW)
                    probabilities(1, SELECTED)
                    compressed()
                    probabilities(2, WINDOW)

                @block.scalar
                def _(act):
                    act.wait_ge(L["acv"], TT)
                    for t in range(TT):
                        act.activation(Sc[:, t, :, 0:NCMP], Sc[:, t, :, 0:NCMP], ACT.Exp).then_inc(L["acx"], 1)
                    act.wait_ge(L["az"], 1)

                    def exponentials(number, group):
                        for t in range(TT):
                            S2 = (SA0, SA1)[t]
                            act.wait_ge(L["amx"], 2 * number + t + 1)
                            for hd in range(8 * group, 8 * group + 8):
                                act.activation(S2[:, hd, :], S2[:, hd, :], ACT.Exp, bias=NM2[:, t, hd:hd + 1],
                                               accum_out=DEN2[:, t, hd:hd + 1]).then_inc(L["aden"], 1)

                    def transposed(hd):
                        b = banks.take(act, ("t2", hd))
                        banks.give(act.activation(PTR[:, slot[hd], :], b[:, 0:384], ACT.Copy), ("t2", hd))

                    def output(c):
                        b = banks.take(act, ("o2", c))
                        banks.give(act.activation(aT[:, c, :], b[:, 0:T], ACT.Copy), ("o2", c))

                    exponentials(0, MLA)
                    exponentials(1, SELECTED)
                    b = banks.take(act, "V")
                    banks.give(act.activation(V2, two(b[:, :]), ACT.Copy), "V")
                    for hd in (16, 17, 18, 19):
                        transposed(hd)
                    output(4)
                    exponentials(2, WINDOW)
                    for c in range(5, 8):
                        if c < 7:
                            transposed(2 * c + 10)
                            transposed(2 * c + 11)
                        output(c)
                    for c in range(5):
                        if c < 4:
                            job = ("tc", c)
                            b = banks.take(act, job)
                            banks.give(act.activation(PTC[0:NCMP, 2 * c:2 * c + 2, :], two(b[0:NCMP, :]), ACT.Copy), job)
                            for hd in nsa_heads[c]:
                                transposed(hd)
                        if c:
                            output(c - 1)

                @block.tensor
                def _(pe):
                    bank = banks.open(pe, "sc")
                    for t in range(TT):
                        for c in range(4):
                            a = (t * 8 + 2 * c) * NCMP
                            ins = pe.matmul(bank[:, a:a + 2 * NCMP], qA[:, c, t * P:(t + 1) * P],
                                            KZC[:, c // 2, :, 0:NCMP], start=True, stop=True)
                    banks.close(ins, "sc")
                    pairs = [((qA[:, c % 4, :],), (KZ2[:, c // 4, (c % 4) // 2],)) for c in range(8)]
                    pairs += [((qM[:, 2 * c, :], qM[:, 2 * c + 1, :]), (KM[:, 2 * c, :], KM[:, 2 * c + 1, :]))
                              for c in range(4)]
                    def scores(group, t):
                        attention_tensor_scores(pe, pairs, "s2", t, range(4 * group, 4 * group + 4))

                    def transposes(hd):
                        attention_tensor_transposes(pe, SA0, SA1, hd, "t2")

                    def attend(c, heads):
                        for hd in heads:
                            banks.wait_drained(pe, ("t2", hd))
                        bank = banks.open(pe, ("o2", c))
                        for j in range(2):
                            rows = slice(64 * j, 64 * j + 64)
                            own = [hd for hd in heads if hd % 2 == j]
                            if c < 4:
                                banks.wait_drained(pe, ("tc", c))
                                pe.matmul(bank[rows, 0:T], vcmp[:, c // 2, :], PTC[:, 2 * c + j, :],
                                          start=True, stop=False)
                            for n, hd in enumerate(own):
                                if c < 4:
                                    col = P * (hd // 8) + 64 * (c // 2)
                                    v = V2[:, :, col:col + 64]
                                else:
                                    v = Vm[:, :, 64 * (hd - 16):64 * (hd - 15)]
                                pe.matmul(bank[rows, 0:T], v[:, 0, :], PTR[:, slot[hd], 0:T],
                                          start=(c >= 4), stop=False)
                                ins = pe.matmul(bank[rows, P:T], v[:, 1, :], PTR[:, slot[hd], T:384],
                                                start=False, stop=(n == len(own) - 1))
                        banks.close(ins, ("o2", c))

                    for group, t in ((MLA, 0), (MLA, 1), (SELECTED, 0), (SELECTED, 1), (WINDOW, 0)):
                        scores(group, t)
                    values(pe, "V", xnT)
                    pe.wait_ge(L["ap"], 2)
                    for hd in (16, 17, 18, 19):
                        transposes(hd)
                    attend(4, (16, 17))
                    scores(WINDOW, 1)
                    for c in range(5, 8):
                        if c < 7:
                            transposes(2 * c + 10)
                            transposes(2 * c + 11)
                        attend(c, (2 * c + 8, 2 * c + 9))
                    pe.wait_ge(L["acp"], TT)
                    pe.wait_ge(L["ap"], 6)
                    for c in range(5):
                        if c < 4:
                            bank = banks.open(pe, ("tc", c))
                            for j in range(2):
                                for t in range(TT):
                                    a = (2 * j + t) * P
                                    ins = pe.transpose(bank[0:NCMP, a:a + P], Sc[:, t, 2 * c + j, 0:NCMP], const("ident"))
                            banks.close(ins, ("tc", c))
                            for hd in nsa_heads[c]:
                                transposes(hd)
                        if c:
                            attend(c - 1, nsa_heads[c - 1])

            upper.close()
            hidden_parts = ctx.enter_context(ExitStack())
            hidden_hi, hidden_lo = (
                hidden_parts.enter_context(nc.sbuf_tensor(n, [P, FF * T // P], F32R))[:, :]
                .rearrange("p (c t) -> p c t", t=T) for n in ("hidden_hi", "hidden_lo"))
            with nc.Block() as block:
                @block.sync
                def _(sp):
                    while ring.issued < LAYER_UNITS:
                        ring.load(sp, w2[layer, ring.issued, :, :])

                @block.gpsimd
                def _(pool):
                    ring.subtract(pool, 2)
                    parts.subtract(pool, "pool", mixT)
                    ring.subtract(pool, 6)
                    parts.subtract(pool, "pool", fx)
                    ring.subtract(pool)

                @block.scalar
                def _(act):
                    act.activation(sqo, aT, ACT.Square).then_inc(L["fsq"], 1)
                    ring.round(act, 2)
                    for k in range(2):
                        b = banks.take(act, f"mo{k}")
                        banks.give(root_of_mean(act, b, 512, std[:, T * k:T * k + T]), f"mo{k}")
                    parts.round(act, mixT, L["fmix"], 0)
                    for i in range(4):
                        ring.feed(act, ("wo", i))
                        banks.wait_drained(act, ("wo", i))
                        act.activation(sqo[:, 2 * i:2 * i + 2, :], hT[:, 2 * i:2 * i + 2, :], ACT.Square)\
                           .then_inc(L["fsq2"], 1)
                    parts.round(act, fx, L["fxn2"], 0)
                    for i in range(16):
                        ring.feed(act, ("f1", i))
                        b = banks.take(act, ("f1", i))
                        if i >= 2:
                            act.wait_ge(L["fsqr"], i - 1)
                        banks.give(act.activation(relu[:, i % 2], two(b[:, :]), ACT.Relu), ("f1", i))
                    ring.round(act, FF2_UNITS)
                    for b in range(4):
                        act.wait_ge(L["fh"], b + 1)
                        act.activation(sqo[:, 2 * b:2 * b + 2, :], hT[:, 2 * b:2 * b + 2, :], ACT.Square)

                @block.vector
                def _(dve):
                    link = Chain(dve, L["fvec"])
                    for k, n in enumerate(("nsa", "mla")):
                        banks.wait_drained(dve, f"mo{k}")
                        link(dve.reciprocal(rst[:, T * k:T * k + T], std[:, T * k:T * k + T]))
                        for c in range(4):
                            dve.scalar_tensor_tensor(mixT[:, 4 * k + c, :], aT[:, 4 * k + c, :], p2(n)[:, c:c + 1],
                                                     rst[:, T * k:T * k + T], ALU.mult, ALU.mult).then_inc(L["fmix"], 1)
                    parts.subtract(dve, "dve", mixT)
                    for i in range(4):
                        b = banks.take(dve, ("wo", i))
                        banks.give(dve.tensor_tensor(hT[:, 2 * i:2 * i + 2, :], hT[:, 2 * i:2 * i + 2, :], two(b[:, :]),
                                                     ALU.add), ("wo", i))
                        banks.wait_drained(dve, ("wo", i))
                    for c in range(DC):
                        dve.tensor_scalar(fx[:, c, :], hT[:, c, :], p2("mlp")[:, c:c + 1], None, ALU.mult)\
                           .then_inc(L["fxn2"], 1)
                    parts.subtract(dve, "dve", fx)
                    for i in range(16):
                        if i == 2:
                            b = banks.take(dve, "mf")
                            banks.give(dve.tensor_scalar(std[:, 0:T], b[:, 0:T], 1.0 / D, EPS, ALU.mult, ALU.add), "mf")
                            banks.wait_drained(dve, "mf")
                            link(dve.reciprocal(rst[:, 0:T], std[:, 0:T]))
                        banks.wait_drained(dve, ("f1", i))
                        if i:
                            dve.wait_ge(L["fhid"], i)
                        dve.tensor_tensor(squared, relu[:, i % 2], relu[:, i % 2], ALU.mult).then_inc(L["fsqr"], 1)
                        dve.wait_ge(L["fsqr"], i + 1)
                        pair = slice(2 * i, 2 * i + 2)
                        dve.tensor_copy(hidden_hi[:, pair, :], squared).then_inc(L["fhigh"], 1)
                        dve.wait_ge(L["fhigh"], i + 1)
                        dve.tensor_tensor(hidden_lo[:, pair, :], squared, hidden_hi[:, pair, :].bitcast(F32),
                                          ALU.subtract).then_inc(L["fhid"], 1)
                    for b in range(4):
                        bank = banks.take(dve, ("f2", b))
                        dve.wait_ge(L["fhid"], 16)
                        if b:
                            dve.wait_ge(L["fh"], b)
                        r2 = rst[:, 0:T].rearrange("p (o t) -> p o t", o=1).broadcast_to([P, 2, T])
                        banks.give(dve.tensor_tensor(squared, two(bank[:, :]), r2, ALU.mult), ("f2", b))
                        banks.wait_drained(dve, ("f2", b))
                        dve.tensor_tensor(hT[:, 2 * b:2 * b + 2, :], hT[:, 2 * b:2 * b + 2, :], squared,
                                          ALU.add).then_inc(L["fh"], 1)

                @block.tensor
                def _(pe):
                    for k in range(2):
                        sum_squares(pe, f"mo{k}", sqo[:, 4 * k:4 * k + 4, :], 4, (L["fsq"], 1))
                    for i in range(4):
                        linear(pe, ("wo", i), i == 0)
                    for i in range(16):
                        if i == 2:
                            sum_squares(pe, "mf", sqo, DC, (L["fsq2"], 4))
                        linear(pe, ("f1", i), i == 0)
                    out_banks = [banks.open(pe, ("f2", b)) for b in range(4)]
                    for u in range(FF2_UNITS):
                        high = ring.high(pe)
                        pe.wait_ge(L["fhid"], u // 2 + 1)

                        def products(w, x, c, start=False):
                            return pe.matmul(out_banks[c // 2][:, (c % 2) * T:(c % 2 + 1) * T], w[:, c * P:(c + 1) * P],
                                             x[:, u, :], start=start, stop=False, skip_group_check=True)

                        if u < FF2_UNITS - 1:
                            for c in range(DC):
                                products(high, hidden_hi, c, u == 0 and c % 2 == 0)
                                products(high, hidden_lo, c)
                            low = ring.low(pe)
                            for c in range(DC):
                                ins = products(low, hidden_hi, c)
                        else:
                            low = ring.low(pe)
                            for c in range(DC):
                                products(high, hidden_hi, c)
                                products(high, hidden_lo, c)
                                ins = products(low, hidden_hi, c)
                                if c % 2:
                                    banks.close(ins, ("f2", c // 2))
                        if u < FF2_UNITS - 1:
                            ins.then_inc(ring.used, 1)

        e_ms, e_std, e_rst, e_y, e_out = (sem(n) for n in ("end_ms", "end_std", "end_rst", "end_y", "end_out"))
        with nc.Block() as block:
            @block.scalar
            def _(act):
                act.wait_ge(e_ms, 1)
                root_of_mean(act, psum[0], D, std[:, 0:T]).then_inc(e_std, 1)

            @block.tensor
            def _(pe):
                for c in range(DC):
                    ins = pe.matmul(psum[0][:, 0:T], const("ones"), sqo[:, c, :], start=(c == 0), stop=(c == DC - 1))
                ins.then_inc(e_ms, 1)

            @block.vector
            def _(dve):
                dve.wait_ge(e_std, 1)
                dve.reciprocal(rst[:, 0:T], std[:, 0:T]).then_inc(e_rst, 1)
                dve.wait_ge(e_rst, 1)
                for c in range(DC):
                    dve.scalar_tensor_tensor(fx[:, c, :], hT[:, c, :], par("final")[:, c:c + 1], rst[:, 0:T],
                                             ALU.mult, ALU.mult).then_inc(e_y, 1)

            @block.sync
            def _(sp):
                for half in range(2):
                    sp.wait_ge(e_y, DC // 2 * (half + 1))
                    cols = slice(half * D, (half + 1) * D)
                    sp.dma_start(out[:, cols], fx[:, half * DC // 2:(half + 1) * DC // 2, :]).then_inc(e_out, 16)
                sp.wait_ge(e_out, 32)


def _blocks(w, k, n):
    rows, cols = w.shape
    return w.reshape(k, P, cols // n, n).transpose(2, 1, 0, 3).reshape(cols // n, P, k * n)


def _tall(v):
    return v.reshape(-1, P).T


def _constants():
    c = np.zeros((P, NCONST), np.float32)

    def put(name, a):
        lo, hi = CONST[name]
        c[:a.shape[0], lo:lo + a.shape[1]] = a

    i = np.arange(P)
    put("ones", np.ones((P, P)))
    put("blk64", (i[:, None] // 64 == i[None, :] // 64).astype(np.float32))
    put("ident", np.eye(P))
    for name, dim, starts in (("rot64", 64, (0, 64)), ("rot32", 32, (64,))):
        r = np.zeros((P, P), np.float32)
        for s in starts:
            for d in range(dim // 2):
                r[s + d + dim // 2, s + d] = -1.0
                r[s + d, s + d + dim // 2] = 1.0
        put(name, r)
    for tag, dim, starts in (("A", 64, (0, 64)), ("B", 32, (64,))):
        inv = (np.float32(1.0) / (np.float32(10000.0) ** (np.arange(0, dim, 2, dtype=np.float32) / np.float32(dim))))
        ang = np.arange(T, dtype=np.float32)[:, None] * inv.astype(np.float32)[None, :]
        ang = np.concatenate([ang, ang], axis=-1).T
        cos, sin = np.ones((P, T), np.float32), np.zeros((P, T), np.float32)
        for s in starts:
            cos[s:s + dim], sin[s:s + dim] = np.cos(ang), np.sin(ang)
        put("cos" + tag, cos)
        put("sin" + tag, sin)
    put("mask1", np.concatenate([np.zeros((P, P)), np.where(i[None, :] <= i[:, None], 0.0, NEG)], axis=1))
    end = np.arange(NCMP) * 16 + 31
    ok = np.stack([end[None, :] <= (i[:, None] + P * t) for t in range(TT)], axis=1)
    wide = np.zeros((P, TT, 16), np.float32)
    wide[:, :, :NCMP] = np.where(ok, 0.0, NEG)
    put("cmp_add", wide.reshape(P, 32).copy())
    wide[:, :, :NCMP] = ok
    put("cmp_mul", wide.reshape(P, 32))
    put("time", np.tile(np.arange(T, dtype=np.float32), (P, 1)))
    put("lane", np.tile(i.astype(np.float32), (P, 1)))
    return c


def _lay(inputs):
    a = {k: np.asarray(v) for k, v in inputs.items()}
    f = np.float32
    out = {}
    out["xT"] = a["x"][0].T.reshape(DC, P, T).transpose(1, 0, 2).reshape(P, DC * T)
    out["consts"] = _constants()

    par = np.zeros((P, NPAR1), f)

    def put(name, v, table=PAR1, dst=None):
        lo, hi = table[name]
        (par if dst is None else dst)[:, lo:lo + v.shape[1]] = v

    put("ln1", _tall(a["ln1_g"][0]))
    put("ln2", _tall(a["ln2_g"][0]))
    put("bgate", _tall(a["b_gate"][0]))
    for name, key in (("lre", "s5_lambda_re"), ("lim", "s5_lambda_im")):
        put(name, a[key][0].reshape(SC, P).T)
    put("lstep", np.repeat(a["s5_log_step"][0].reshape(SC, 2), 64, axis=1).T)
    put("dskip", _tall(a["s5_d"][0].reshape(-1)))
    put("gq", np.tile(a["q_norm_g"][0], 2)[:, None])
    put("gk", np.tile(a["k_norm_g"][0], 2)[:, None])
    put("sinks", np.tile(a["attn_sinks"][0], (P, 1)))
    put("final", _tall(a["final_norm_2"]))
    cs = np.stack([a["s5_c_re"][0], a["s5_c_im"][0]], axis=1)
    cs = cs.reshape(SC, 2, 2, 16, 64).transpose(1, 4, 0, 2, 3).reshape(P, SC * 32)
    put("cs5", cs)
    out["par1"] = par

    dist = np.arange(P)[:, None] + P - np.arange(2 * P)[None, :]
    d = np.maximum(dist, 0)
    d_f = np.maximum(d, 1).astype(f)
    large = 16 + (np.log(d_f / f(16)) / f(np.log(8.0)) * f(16)).astype(np.int32)
    bucket = np.where(d < 16, d, np.minimum(large, 31))
    table = a["rel_bias_table"][bucket].transpose(0, 2, 1)
    ok = (dist >= 0) & (dist < 128)
    out["bias1"] = np.where(ok[:, None, :], table, f(NEG)).reshape(P, NH * T)

    bs = np.zeros((UC, 4, 2, P, P), f)
    for k, key in enumerate(("s5_b_re", "s5_b_im")):
        b = a[key][0]
        for g in range(G1):
            sc, half = g // 2, g % 2
            uc, q = sc // 4, sc % 4
            r0 = 32 * q + 16 * half
            bs[uc, q, k, r0:r0 + 16, 64 * half:64 * half + 64] = b[g].T
    bs = bs.transpose(0, 3, 1, 2, 4).reshape(UC, P, SLOT)
    glu = _blocks(a["s5_w_glu"][0], 4, 256)
    w_in = _blocks(a["w_in"][0], DC, P)
    out["w1"] = np.concatenate([
        w_in[:22], bs[:1], w_in[22:28], bs[1:2], w_in[28:], bs[2:],
        _blocks(a["w_attn_branch"][0], DC, P), glu[2:], glu[:2],
        _blocks(a["w_s5_branch"][0], 4, 256), _blocks(a["w_out"][0], DC, P),
        _blocks(a["peer_w_query"][0], DC, P)])
    sk = a["peer_sub_keys"][0]
    keys = np.zeros((2, 64, PH, 2, NSUB), f)
    for k in range(2):
        keys[k, :, :, k, :] = sk[:, k].transpose(2, 0, 1)
    out["keys"] = keys.reshape(P, PH * T)
    u = a["peer_u"][0].reshape(NSUB, NE2, DC, P)
    out["wu"] = np.ascontiguousarray(u.transpose(1, 3, 2, 0)).reshape(NE2, P, SLOT)
    v = a["peer_v"][0].reshape(NSUB, NE2, SLOT)
    out["wv"] = np.ascontiguousarray(v.transpose(1, 0, 2))
    _lay_layers(a, out)
    return {k: np.ascontiguousarray(v, dtype=v.dtype) for k, v in out.items()}


def _lay_layers(a, out):
    f = np.float32
    pars, units = [], []
    for l in range(LAYERS):
        par = np.zeros((P, NPAR2), f)

        def put(name, v):
            lo, hi = PAR2[name]
            par[:, lo:lo + v.shape[1]] = v

        for name, key in (("attn", "attn_norm_2"), ("mlp", "mlp_norm_2"), ("qn", "mla_q_norm_2"),
                          ("kvn", "mla_kv_norm_2"), ("nsa", "nsa_out_norm_2"), ("mla", "mla_out_norm_2")):
            put(name, _tall(a[key][l]))
        for name, key in (("posk", "cmp_pos_k_2"), ("posv", "cmp_pos_v_2")):
            put(name, a[key][l].reshape(16, P).T)
        for name, key in (("w2k", "cmp_w2_k_2"), ("w2v", "cmp_w2_v_2")):
            put(name, a[key][l].reshape(2, P, 64).transpose(1, 0, 2).reshape(P, 128))
        w = a["w_in_2"][l]
        q, kc, vc, ks, vs, kw, vw, g, cq, ckv, kr = np.split(w, np.cumsum([512] + [128] * 6 + [24, 256, 128]), axis=1)
        put("wg", g.reshape(DC, P, 24).transpose(1, 0, 2).reshape(P, DC * 24))
        krp = np.zeros((D, P), f)
        krp[:, 64:96] = kr
        w_in = np.concatenate([q, kc, vc, ks, kw, cq, ckv, krp, vs, vw], axis=1)
        wq = np.zeros((256, 8, P), f)
        wq[:, :, :96] = a["w_q_up_2"][l].reshape(256, 8, 96)
        wkv = a["w_kv_up_2"][l].reshape(P, 8, P)
        up = np.zeros((2, P, SLOT), f)
        up[0].reshape(P, 8, P)[:, :, :64] = wkv[:, :, :64]
        up[1, :, 0:512] = wkv[:, :, 64:].reshape(P, 512)
        tall = [a[k][l].reshape(-1, SLOT // a[k].shape[2], P, a[k].shape[2]).transpose(0, 2, 1, 3).reshape(-1, P, SLOT)
                for k in ("cmp_w1_k_2", "cmp_w1_v_2", "w_ff2_2")]
        units.append(np.concatenate([
            _blocks(w_in, DC, P)[:12], _blocks(wq.reshape(256, 1024), 2, 512), up, tall[0], tall[1],
            _blocks(w_in, DC, P)[12:],
            _blocks(a["w_out_2"][l], DC, P), _blocks(a["w_ff1_2"][l], DC, P), tall[2]]))
        pars.append(par)
    out["par2"] = np.stack(pars)
    out["w2"] = np.stack(units)


_INS = ["xT", "consts", "par1", "bias1", "w1", "keys", "wu", "wv", "par2", "w2"]


def kernel(**inputs):
    import concourse.bacc as _bacc
    from concourse.bass_utils import run_bass_kernel_spmd as _run

    arrays = _lay(inputs)
    nc = _bacc.Bacc("TRN2", target_bir_lowering=False, num_devices=1)
    args = [nc.dram_tensor(n, arrays[n].shape, mybir.dt.from_np(arrays[n].dtype), kind="ExternalInput").ap() for n in _INS]
    out = nc.dram_tensor("yT", (P, DC * T), F32, kind="ExternalOutput").ap()
    build(nc, None, *args, out)
    r = _run(nc, [{n: arrays[n] for n in _INS}], core_ids=[0])
    y = np.asarray(r.results[0]["yT"]).reshape(P, DC, T).transpose(2, 1, 0).reshape(1, T, D)
    return y
```
